# Optimizing a Trainium2 kernel written in Bass

```python
import jax, jax.numpy as jnp
from jax import lax
import numpy as np

D_MODEL = 1024
BATCH = 1
SEQ = 1024
DEPTH = 1
DEC_BATCH = 8
DEC_SEQ = 16
PAST_LEN = 1024

CHUNK = 64
D_MIX = D_MODEL
GLA_HEADS = 4
GLA_DV = (D_MIX // 2) // GLA_HEADS
GLA_DK = GLA_DV // 2
GLA_RANK = 16
GLA_TAU = 16.0
M_HEADS = 4
M_DH = (D_MIX // 2) // M_HEADS
D_FF = 2816
FFN_CONV = 3
EPS = 1e-6
GLA_QK = GLA_HEADS * GLA_DK
GLA_V = GLA_HEADS * GLA_DV
M_W = M_HEADS * M_DH
D_IN = 2 * GLA_QK + 2 * GLA_V + GLA_RANK + 4 * M_W + 2 * M_HEADS

kernel_name = "gla_mlstm_parallel_convffn_stream_step"

def _rmsnorm(x, g):
    xf = x.astype(jnp.float32)
    y = xf * lax.rsqrt(jnp.mean(xf * xf, axis=-1, keepdims=True) + EPS) * g.astype(jnp.float32)
    return y.astype(x.dtype)

def _head_rmsnorm(t, g):
    return t * lax.rsqrt(jnp.mean(t * t, axis=-1, keepdims=True) + EPS) * g.astype(jnp.float32)

def _split_proj(p):
    sizes = (GLA_QK, GLA_QK, GLA_V, GLA_V, GLA_RANK, M_W, M_W, M_W, M_W, M_HEADS, M_HEADS)
    idx = []
    s = 0
    for z in sizes[:-1]:
        s += z
        idx.append(s)
    return jnp.split(p, idx, axis=-1)

def _to_chunks(t, c):
    B, L = t.shape[0], t.shape[1]
    t = t.reshape((B, L // c, c) + t.shape[2:])
    return jnp.moveaxis(t, 1, 0)

def _from_chunks(t):
    t = jnp.moveaxis(t, 0, 1)
    return t.reshape((t.shape[0], t.shape[1] * t.shape[2]) + t.shape[3:])

def _gla(q, k, v, log_a, S0):
    L = q.shape[1]
    c = min(CHUNK, L)
    causal = jnp.tril(jnp.ones((c, c), dtype=bool))

    def step(S, inp):
        qc, kc, vc, ac = inp
        b = jnp.cumsum(ac, axis=1)
        inter = jnp.einsum('bthk,bhkv->bthv', qc * jnp.exp(b), S)
        diff = b[:, :, None] - b[:, None, :]
        diff = jnp.where(causal[None, :, :, None, None], diff, -jnp.inf)
        scores = jnp.einsum('bthk,bshk,btshk->bhts', qc, kc, jnp.exp(diff))
        intra = jnp.einsum('bhts,bshv->bthv', scores, vc)
        b_last = b[:, -1]
        k_dec = kc * jnp.exp(b_last[:, None] - b)
        S_new = jnp.exp(b_last)[..., None] * S + jnp.einsum('bshk,bshv->bhkv', k_dec, vc)
        return S_new, inter + intra

    xs = (_to_chunks(q, c), _to_chunks(k, c), _to_chunks(v, c), _to_chunks(log_a, c))
    S_fin, o = lax.scan(step, S0, xs)
    return _from_chunks(o), S_fin

def _mlstm(q, k, v, i_pre, log_f, C0, n0, m0):
    L = q.shape[1]
    c = min(CHUNK, L)
    causal = jnp.tril(jnp.ones((c, c), dtype=bool))

    def step(carry, inp):
        C, n, m = carry
        qc, kc, vc, ic, fc = inp
        F = jnp.moveaxis(jnp.cumsum(fc, axis=1), 1, 2)
        ih = jnp.moveaxis(ic, 1, 2)
        D = F[..., :, None] - F[..., None, :] + ih[..., None, :]
        D = jnp.where(causal, D, -jnp.inf)
        g_inter = F + m[..., None]
        m_t = jnp.maximum(g_inter, jnp.max(D, axis=-1))
        w_inter = jnp.exp(g_inter - m_t)
        W = jnp.exp(D - m_t[..., None])
        qk = jnp.einsum('bthd,bshd->bhts', qc, kc) * W
        w_bt = jnp.moveaxis(w_inter, 1, 2)
        num = (jnp.einsum('bhts,bshv->bthv', qk, vc)
               + w_bt[..., None] * jnp.einsum('bthd,bhdv->bthv', qc, C))
        den = jnp.sum(qk, axis=-1) + w_inter * jnp.einsum('bthd,bhd->bht', qc, n)
        den = jnp.maximum(jnp.abs(den), jnp.exp(-m_t))
        h = num / jnp.moveaxis(den, 1, 2)[..., None]
        m_c = m_t[..., -1]
        decay = jnp.exp(F[..., -1] + m - m_c)
        ws = jnp.exp(F[..., -1:] - F + ih - m_c[..., None])
        C_new = decay[..., None, None] * C + jnp.einsum('bhs,bshd,bshv->bhdv', ws, kc, vc)
        n_new = decay[..., None] * n + jnp.einsum('bhs,bshd->bhd', ws, kc)
        return (C_new, n_new, m_c), h

    xs = (_to_chunks(q, c), _to_chunks(k, c), _to_chunks(v, c),
          _to_chunks(i_pre, c), _to_chunks(log_f, c))
    (C_f, n_f, m_f), h = lax.scan(step, (C0, n0, m0), xs)
    return _from_chunks(h), C_f, n_f, m_f

def _conv_ffn(h, conv_st, w_g, w_u, conv_w, conv_b, w_d):
    L = h.shape[1]
    g = h @ w_g
    u = h @ w_u
    gp = jnp.concatenate([conv_st.astype(g.dtype), g], axis=1)
    gc = conv_b + sum(conv_w[j] * gp[:, j:j + L] for j in range(FFN_CONV))
    y = (jax.nn.gelu(gc) * u) @ w_d
    return y, gp[:, -(FFN_CONV - 1):]

def _layer(x, S_g, C_m, n_m, m_m, conv_st, norm1, w_in, w_gla_a, b_gla_a, gla_norm,
           b_m_i, b_m_f, m_norm, w_out, norm2, w_g, w_u, conv_w, conv_b, w_d):
    B, L, _ = x.shape
    f32 = jnp.float32
    h = _rmsnorm(x, norm1)
    gq, gk, gv, gr, glr, mq, mk, mv, mo, mi, mf = _split_proj(h @ w_in)

    def heads(t, H, d):
        return t.astype(f32).reshape(B, L, H, d)

    log_a = jax.nn.log_sigmoid((glr @ w_gla_a + b_gla_a).astype(f32)) / GLA_TAU
    o_g, S_new = _gla(heads(gq, GLA_HEADS, GLA_DK) * (GLA_DK ** -0.5),
                      heads(gk, GLA_HEADS, GLA_DK), heads(gv, GLA_HEADS, GLA_DV),
                      heads(log_a, GLA_HEADS, GLA_DK), S_g.astype(f32))
    o_g = _head_rmsnorm(o_g, gla_norm) * jax.nn.silu(heads(gr, GLA_HEADS, GLA_DV))

    i_pre = mi.astype(f32) + b_m_i.astype(f32)
    log_f = jax.nn.log_sigmoid(mf.astype(f32) + b_m_f.astype(f32))
    h_m, C_new, n_new, m_new = _mlstm(heads(mq, M_HEADS, M_DH),
                                      heads(mk, M_HEADS, M_DH) * (M_DH ** -0.5),
                                      heads(mv, M_HEADS, M_DH), i_pre, log_f,
                                      C_m.astype(f32), n_m.astype(f32), m_m.astype(f32))
    h_m = _head_rmsnorm(jax.nn.sigmoid(heads(mo, M_HEADS, M_DH)) * h_m, m_norm)

    mix = jnp.concatenate([o_g.reshape(B, L, GLA_V), h_m.reshape(B, L, M_W)], axis=-1)
    x = x + mix.astype(x.dtype) @ w_out
    y, conv_new = _conv_ffn(_rmsnorm(x, norm2), conv_st, w_g, w_u, conv_w, conv_b, w_d)
    x = x + y
    dt = x.dtype
    return x, (S_new.astype(dt), C_new.astype(dt), n_new.astype(dt), m_new.astype(dt),
               conv_new.astype(dt))

def setup_inputs(seed: int = 0) -> dict:
    key = jax.random.key(seed)
    ks = jax.random.split(key, 32)
    nrm = jax.random.normal
    f32 = jnp.float32
    Dp = DEPTH
    return {
        "x_prompt": nrm(ks[0], (BATCH, SEQ, D_MODEL), f32),
        "x_sample": nrm(ks[1], (DEC_BATCH, DEC_SEQ, D_MODEL), f32),
        "state_gla": 0.5 * nrm(ks[2], (Dp, DEC_BATCH, GLA_HEADS, GLA_DK, GLA_DV), f32),
        "state_mlstm_C": 0.5 * nrm(ks[3], (Dp, DEC_BATCH, M_HEADS, M_DH, M_DH), f32),
        "state_mlstm_n": 0.5 * nrm(ks[4], (Dp, DEC_BATCH, M_HEADS, M_DH), f32),
        "state_mlstm_m": nrm(ks[5], (Dp, DEC_BATCH, M_HEADS), f32),
        "cache_ffn_conv": nrm(ks[6], (Dp, DEC_BATCH, FFN_CONV - 1, D_FF), f32),
        "norm1": 1.0 + 0.02 * nrm(ks[7], (Dp, D_MODEL), f32),
        "w_in": nrm(ks[8], (Dp, D_MODEL, D_IN), f32) * D_MODEL ** -0.5,
        "w_gla_a": nrm(ks[9], (Dp, GLA_RANK, GLA_QK), f32) * GLA_RANK ** -0.5,
        "b_gla_a": 0.01 * nrm(ks[10], (Dp, GLA_QK), f32),
        "gla_norm": 1.0 + 0.02 * nrm(ks[11], (Dp, GLA_DV), f32),
        "b_m_i": 0.1 * nrm(ks[12], (Dp, M_HEADS), f32),
        "b_m_f": jnp.linspace(3.0, 6.0, M_HEADS, dtype=f32)[None] + 0.1 * nrm(ks[13], (Dp, M_HEADS), f32),
        "m_norm": 1.0 + 0.02 * nrm(ks[14], (Dp, M_DH), f32),
        "w_out": nrm(ks[15], (Dp, D_MIX, D_MODEL), f32) * D_MIX ** -0.5,
        "norm2": 1.0 + 0.02 * nrm(ks[16], (Dp, D_MODEL), f32),
        "w_g": nrm(ks[17], (Dp, D_MODEL, D_FF), f32) * D_MODEL ** -0.5,
        "w_u": nrm(ks[18], (Dp, D_MODEL, D_FF), f32) * D_MODEL ** -0.5,
        "conv_w": nrm(ks[19], (Dp, FFN_CONV, D_FF), f32) * FFN_CONV ** -0.5,
        "conv_b": 0.01 * nrm(ks[20], (Dp, D_FF), f32),
        "w_d": nrm(ks[21], (Dp, D_FF, D_MODEL), f32) * D_FF ** -0.5,
        "norm_f": 1.0 + 0.02 * nrm(ks[22], (D_MODEL,), f32),
    }

def reference(x_prompt, x_sample, state_gla, state_mlstm_C, state_mlstm_n, state_mlstm_m,
              cache_ffn_conv, norm1, w_in, w_gla_a, b_gla_a, gla_norm, b_m_i, b_m_f, m_norm,
              w_out, norm2, w_g, w_u, conv_w, conv_b, w_d, norm_f):
    xp = x_prompt
    xs = x_sample
    Bp = x_prompt.shape[0]
    dt = x_prompt.dtype
    p_st = []
    s_st = []
    for l in range(DEPTH):
        w = (norm1[l], w_in[l], w_gla_a[l], b_gla_a[l], gla_norm[l], b_m_i[l], b_m_f[l],
             m_norm[l], w_out[l], norm2[l], w_g[l], w_u[l], conv_w[l], conv_b[l], w_d[l])
        xp, st_p = _layer(xp,
                          jnp.zeros((Bp, GLA_HEADS, GLA_DK, GLA_DV), dt),
                          jnp.zeros((Bp, M_HEADS, M_DH, M_DH), dt),
                          jnp.zeros((Bp, M_HEADS, M_DH), dt),
                          jnp.zeros((Bp, M_HEADS), dt),
                          jnp.zeros((Bp, FFN_CONV - 1, D_FF), dt), *w)
        xs, st_s = _layer(xs, state_gla[l], state_mlstm_C[l], state_mlstm_n[l],
                          state_mlstm_m[l], cache_ffn_conv[l], *w)
        p_st.append(st_p)
        s_st.append(st_s)
    y_prompt = _rmsnorm(xp, norm_f)
    y_sample = _rmsnorm(xs, norm_f)
    p_gla = jnp.stack([s[0] for s in p_st])
    p_mC = jnp.stack([s[1] for s in p_st])
    p_mn = jnp.stack([s[2] for s in p_st])
    p_mm = jnp.stack([s[3] for s in p_st])
    p_conv = jnp.stack([s[4] for s in p_st])
    s_gla = jnp.stack([s[0] for s in s_st])
    s_mC = jnp.stack([s[1] for s in s_st])
    s_mn = jnp.stack([s[2] for s in s_st])
    s_mm = jnp.stack([s[3] for s in s_st])
    s_conv = jnp.stack([s[4] for s in s_st])
    return (y_prompt, y_sample, p_gla, p_mC, p_mn, p_mm, p_conv, s_gla, s_mC, s_mn, s_mm, s_conv)


_drawn_inputs = setup_inputs


def setup_inputs(seed=0):
    import zlib

    import numpy as np

    out = dict(_drawn_inputs(seed))
    spreads = {}
    factors = {'b_gla_a': 8.0,
     'gla_norm': 7.319,
     'm_norm': 4.722,
     'norm2': 2.862,
     'conv_b': 8.0,
     'norm_f': 2.815}
    for name, (base, spread) in spreads.items():
        noise = np.random.default_rng([zlib.crc32(name.encode()), seed]).standard_normal(out[name].shape)
        drawn = base * np.exp(spread * noise) if base else spread * noise
        out[name] = __import__('jax').numpy.asarray(drawn.astype(out[name].dtype))
    for name, factor in factors.items():
        out[name] = (out[name] * factor).astype(out[name].dtype)
    return out
```

```python
from contextlib import ExitStack

import concourse.bass as bass
from concourse import mybir

F32 = mybir.dt.float32
F32R = mybir.dt.float32r
I32 = mybir.dt.int32
ALU = mybir.AluOpType
ACT = mybir.ActivationFunctionType
AX = mybir.AxisListType

P = 128
D = 1024
KD = D // P
PROMPT = 1024
NB, LB = 8, 16
ROWS = PROMPT + NB * LB
RT = ROWS // P
NC = PROMPT // P
RBW = 384
RB = ROWS // RBW
JR = RBW // P
EPS = 1e-6
H = 4
DK, DV, DH = 64, 128, 128
VX = DH + 1
RANK = 16
TAU = 16.0
F = 2816
NF = F // P
QSCALE = DK ** -0.5
KSCALE = DH ** -0.5
NT = 12
NN = 4
LEVELS = 7
PIECE = D
PC_GATE, PC_T, PC_N = 0, 1, 1 + NT
PC_OUT = PC_N + 4 * NN
PC_FFN = PC_OUT + KD
N_PIECES = PC_FFN + 3 * NF
EXT = 1 + PROMPT + NB * (LB + 1)
NEG = -1.0e30
C_CAUS = 0
C_KEEP = C_CAUS + P
C_LV = C_KEEP + 2 * P
C_SHARED = C_LV + 3 * P
C_ONE = C_LV + (LEVELS + 1) * P
C_BLK = C_ONE + P
C_SAMPLE = C_BLK + H * P
C_CAUSB = C_SAMPLE
C_KEEPB = C_CAUSB + P
C_BM = C_KEEPB + 2 * P
N_CONST = C_BM + NB
K_N1, K_N2, K_GN, K_MN, K_BA, K_BG = 0, 8, 16, 17, 18, 20
K_M0 = 21
N_COL = K_M0 + NB


class Count:

    def __init__(self, eng, sem, base=0):
        self.eng, self.sem, self.base, self.n = eng, sem, base, 0

    def link(self, ins):
        ins.then_inc(self.sem, 1)
        self.n += 1
        self.eng.wait_ge(self.sem, self.base + self.n)


class Sems:

    def __init__(self, nc, ctx, prefix):
        self.nc, self.prefix, self.taken = nc, prefix, []
        ctx.callback(self.clear)

    def __call__(self, name):
        self.taken.append(self.nc.alloc_semaphore(name=self.prefix + name))
        return self.taken[-1]

    def clear(self):
        self.nc.clear_and_free_semaphores(self.taken)
        self.nc.all_engine_barrier()


def mm3(pe, out, stat, mov, start, stop):
    pe.matmul(out, stat[0], mov[0], start=start, stop=False)
    pe.matmul(out, stat[0], mov[1], start=False, stop=False)
    return pe.matmul(out, stat[1], mov[0], start=False, stop=stop)


class Norm:

    def __init__(self, nc, ctx, name, x9, hT, ident, gain, banks):
        sem = lambda n: ctx.enter_context(nc.semaphore(f"{name}_{n}"))
        sb = lambda n, s: ctx.enter_context(nc.sbuf_tensor(f"{name}_{n}", s, F32))
        self.x9, self.hT, self.ident, self.gain, self.banks = x9, hT, ident, gain, banks
        self.xs = sb("scaled", [P, JR, D])
        self.sq = sb("squares", [P, D])
        self.ss = sb("sumsq", [P, RT])
        self.inv = sb("inv", [P, RT])
        self.rstd = sb("rstd", [P, RT])
        self.summed, self.inverted, self.rooted = sem("summed"), sem("inverted"), sem("rooted")
        self.scaled, self.turned, self.hi_done, self.lo_done = sem("scaled"), sem("turned"), sem("hi"), sem("lo")

    def act_sums(self, act, rb, ready):
        for r in range(rb * JR, rb * JR + JR):
            ready(act, r)
            if r:
                act.wait_ge(self.summed, r)
            act.activation(self.sq[:, :], self.x9[:, r, :], ACT.Square,
                           accum_out=self.ss[:, r:r + 1]).then_inc(self.summed, 1)

    def act_root(self, act, rb):
        act.wait_ge(self.inverted, rb + 1)
        s = slice(rb * JR, rb * JR + JR)
        act.activation(self.rstd[:, s], self.inv[:, s], ACT.Sqrt).then_inc(self.rooted, 1)

    def act_hi(self, act, rb):
        for k in range(KD):
            n = rb * KD + k
            act.wait_ge(self.turned, n + 1)
            act.activation(self.hT[0][:, k, rb * RBW:(rb + 1) * RBW], self.banks[n % 2][:, 0:RBW], ACT.Copy,
                           scale=self.gain[:, k:k + 1]).then_inc(self.hi_done, 1)

    def dve_invert(self, dve, rb, chain):
        s = slice(rb * JR, rb * JR + JR)
        dve.wait_ge(self.summed, rb * JR + JR)
        chain.link(dve.tensor_scalar(self.ss[:, s], self.ss[:, s], 1.0 / D, EPS, ALU.mult, ALU.add))
        dve.reciprocal(self.inv[:, s], self.ss[:, s]).then_inc(self.inverted, 1)

    def dve_scale(self, dve, rb):
        dve.wait_ge(self.rooted, rb + 1)
        if rb:
            dve.wait_ge(self.turned, rb * KD)
        for j in range(JR):
            r = rb * JR + j
            dve.tensor_scalar(self.xs[:, j, :], self.x9[:, r, :], self.rstd[:, r:r + 1], None,
                              ALU.mult).then_inc(self.scaled, 1)

    def dve_lo(self, dve, rb):
        for k in range(KD):
            n = rb * KD + k
            s = slice(rb * RBW, (rb + 1) * RBW)
            dve.wait_ge(self.hi_done, n + 1)
            dve.scalar_tensor_tensor(out=self.hT[1][:, k, s], in0=self.banks[n % 2][:, 0:RBW],
                                     scalar=self.gain[:, k:k + 1], in1=self.hT[0][:, k, s].bitcast(F32),
                                     op0=ALU.mult, op1=ALU.subtract).then_inc(self.lo_done, 1)

    def pe_turn(self, pe, rb):
        pe.wait_ge(self.scaled, rb * JR + JR)
        for k in range(KD):
            n = rb * KD + k
            if n >= 2:
                pe.wait_ge(self.lo_done, n - 1)
            for j in range(JR):
                t = pe.transpose(self.banks[n % 2][:, j * P:(j + 1) * P], self.xs[:, j, k * P:(k + 1) * P],
                                 self.ident)
            t.then_inc(self.turned, 1)


def build(nc, a, o):
    with ExitStack() as top:
        sb = lambda n, s, d=F32: top.enter_context(nc.sbuf_tensor(n, s, d))
        pb = [top.enter_context(nc.psum_tensor(f"bank{2 * i}", [P, 2, 512], F32)) for i in range(4)]
        bank = [pb[i // 2][:, i % 2, :] for i in range(8)]
        const = sb("ident", [P, P])
        cols = sb("cols", [P, N_COL])
        hT = [sb("hT_hi", [P, KD, ROWS], F32R), sb("hT_lo", [P, KD, ROWS], F32R)]
        ident = const[:, :]
        gain1 = cols[:, K_N1:K_N1 + KD]
        gain2 = cols[:, K_N2:K_N2 + KD]
        normalise(nc, a, const, cols, hT, ident, gain1, bank)
        project(nc, a, o, cols, hT, bank)
        mix(nc, a, o, ident, cols, hT, pb, bank, sample=False)
        mix(nc, a, o, ident, cols, hT, pb, bank, sample=True)
        with nc.sbuf_tensor("x9", [P, RT, D], F32) as x9:
            output(nc, a, x9, hT, ident, gain2, bank)
            ffn(nc, a, o, x9, hT, bank)


def normalise(nc, a, const, cols, hT, ident, gain1, bank):
    with ExitStack() as ctx:
        sem = lambda n: ctx.enter_context(nc.semaphore(n))
        x9 = ctx.enter_context(nc.sbuf_tensor("x_in", [P, RT, D], F32))
        x_loaded = [sem(f"x_loaded{r}") for r in range(RT)]
        const_loaded = sem("const_loaded")
        step = sem("norm_step")
        norm = Norm(nc, ctx, "norm1", x9, hT, ident, gain1, bank[0:2])
        block = ctx.enter_context(nc.Block())

        @block.sync
        def _(sp):
            for r in range(RT):
                sp.dma_start(x9[:, r, :], a["x"][r]).then_inc(x_loaded[r], 16)
                if r == 0:
                    sp.dma_start(const[:, :], a["ident"]).then_inc(const_loaded, 16)
                    sp.dma_start(cols[:, :], a["cols"]).then_inc(const_loaded, 16)

        @block.scalar
        def _(act):
            ready = lambda eng, r: eng.wait_ge(x_loaded[r], 16)
            norm.act_sums(act, 0, ready)
            norm.act_root(act, 0)
            act.wait_ge(const_loaded, 32)
            for rb in range(1, RB):
                norm.act_sums(act, rb, ready)
                norm.act_root(act, rb)
                norm.act_hi(act, rb - 1)
            norm.act_hi(act, RB - 1)

        @block.vector
        def _(dve):
            chain = Count(dve, step)
            norm.dve_invert(dve, 0, chain)
            norm.dve_scale(dve, 0)
            dve.wait_ge(const_loaded, 32)
            for rb in range(1, RB):
                norm.dve_invert(dve, rb, chain)
                norm.dve_lo(dve, rb - 1)
                norm.dve_scale(dve, rb)
            norm.dve_lo(dve, RB - 1)

        @block.tensor
        def _(pe):
            pe.wait_ge(const_loaded, 32)
            for rb in range(RB):
                norm.pe_turn(pe, rb)


def split_spans(rb):
    a = rb * RBW
    n = min(PROMPT - a, RBW)
    return (0, n), (n, RBW - n)


def project(nc, a, o, cols, hT, bank):
    with ExitStack() as ctx:
        sb = lambda n, s, d=F32: ctx.enter_context(nc.sbuf_tensor(n, s, d))
        sem = lambda n: ctx.enter_context(nc.semaphore(n))
        raw = sb("w_raw", [P, 4, PIECE])
        w_hi = sb("w_hi", [P, 8, PIECE], F32R)
        w_lo = sb("w_lo", [P, 8, PIECE], F32R)
        tout = sb("t_out", [P, 2, ROWS])
        nout = sb("n_out", [P, 2, 512])
        sig = sb("sig", [P, 512])
        wa = sb("w_decay", [RANK, 2 * P])
        glr = sb("glr", [RANK, ROWS])
        m_ext = sb("m_ext", [H, EXT])
        lf_ext = sb("lf_ext", [H, EXT])
        g_f = sb("g_f", [H, ROWS])
        g_u = sb("g_u", [P, ROWS])
        keep = sb("keep", [H, ROWS])
        raw_loaded = [sem(f"raw_loaded{s}") for s in range(4)]
        t_stored = [sem(f"t_stored{s}") for s in range(2)]
        n_stored = [sem(f"n_stored{s}") for s in range(2)]
        small_loaded, rows_stored = sem("small_loaded"), sem("rows_stored")
        piece_hi = sem("piece_hi")
        piece_split = sem("piece_split")
        sums_ready = sem("sums_ready")
        sums_taken = sem("sums_taken")
        n_filled, mo_filled = sem("n_filled"), sem("mo_filled")
        sig_ready = sem("sig_ready")
        step, act_step = sem("gate_step"), sem("gate_act_step")
        z_ready, z_taken = sem("z_ready"), sem("z_taken")
        abs_ready, ln_ready, decay_ready = sem("abs_ready"), sem("ln_ready"), sem("decay_ready")
        expo_ready, rows_ready = sem("expo_ready"), sem("rows_ready")
        RAW_CREDIT, BANK_CREDIT = 4, 6
        T_USES = 3 * (1 + NT)
        NUNIT = ((0, 3, 4, 5), (6, 7, 1, 2))
        block = ctx.enter_context(nc.Block())

        def n_unit(n):
            t, q = divmod(n - PC_N, 4)
            return NUNIT[t % 2][q]

        def n_before(n):
            t, q = divmod(n - PC_N, 4)
            return ((3 * NT, 0, 0, 0), (0, 3, T_USES, 0))[t][q] if t < 2 else T_USES + (t - 1) * RT

        @block.sync
        def _(sp):
            for n in range(4):
                sp.wait_ge(piece_split, n + 1)
                sp.dma_start(raw[:, n, :], a["w"][n]).then_inc(raw_loaded[n], 16)
            sp.dma_start(wa[:, :], a["w_decay"]).then_inc(small_loaded, 16)
            sp.dma_start(keep[:, :], a["keep"]).then_inc(small_loaded, 16)
            with sp.Fori(0, NT // 4) as four:
                i = 4 * four
                for q in range(4):
                    sp.wait_ge(piece_split, i + (5 + q))
                    sp.dma_start(raw[:, q, :], a["w"][i + (4 + q)]).then_inc(raw_loaded[q], 16)
                    sp.wait_ge(sums_taken, 3 * i + (BANK_CREDIT + 3 * (q + 2)))
                    sp.dma_start(a["pT"][i + q], tout[:, q % 2, :]).then_inc(t_stored[q % 2], 16)

            def load(n):
                sp.wait_ge(piece_split, n + 1)
                sp.dma_start(raw[:, n % 4, :], a["w"][n]).then_inc(raw_loaded[n % 4], 16)

            load(NT + 4)
            for t in range(NN):
                if t < NN - 1:
                    for q in range(4):
                        load(PC_N + 4 * (t + 1) + q)
                if t == 1:
                    for j in range(2):
                        sp.wait_ge(decay_ready, j + 1)
                        sp.dma_start(a["pT"][NT + j], tout[:, j, :]).then_inc(t_stored[j], 16)
                if t == 2:
                    sp.wait_ge(rows_ready, 4)
                    for q, row in enumerate((g_f, g_u, lf_ext, keep, glr)):
                        sp.dma_start(a["rows"][:, q, :], row[0:H, 0:ROWS]).then_inc(rows_stored, 16)
                    sp.dma_start(o["mm"], m_ext[:, :]).then_inc(rows_stored, 16)
                for r in range(RT):
                    u = t * RT + r
                    if t < NN - 1:
                        sp.wait_ge(n_filled, u + 1)
                    else:
                        sp.wait_ge(mo_filled, r + 1)
                    sp.dma_start(a["pN"][t, r], nout[:, u % 2, :]).then_inc(n_stored[u % 2], 16)
            sp.wait_ge(rows_stored, 6 * 16)
            for s in range(2):
                sp.wait_ge(t_stored[s], 16 * (NT // 2 + 2))
                sp.wait_ge(n_stored[s], 16 * (NN * RT // 2))

        @block.gpsimd
        def _(pool):
            pool.sem_inc(piece_split, RAW_CREDIT)
            pool.sem_inc(sums_taken, BANK_CREDIT)
            pool.sem_inc(t_stored[0], 16)
            pool.sem_inc(t_stored[1], 16)

            def lo(n, unit, slot):
                pool.wait_ge(piece_hi, n + 1)
                pool.tensor_tensor(w_lo[:, unit, :], raw[:, slot, :], w_hi[:, unit, :].bitcast(F32),
                                   ALU.subtract).then_inc(piece_split, 1)

            lo(0, 7, 0)
            lo(1, 0, 1)
            with pool.Fori(0, NT // 4) as four:
                i = 4 * four
                for q in range(4):
                    lo(i + (q + 2), (q + 1) % 2, (q + 2) % 4)
            for n in range(PC_N + 1, PC_OUT):
                lo(n, n_unit(n), n % 4)

        @block.scalar
        def _(act):
            def hi(n, unit, slot, loads):
                act.wait_ge(raw_loaded[slot], loads)
                act.activation(w_hi[:, unit, :], raw[:, slot, :], ACT.Copy).then_inc(piece_hi, 1)

            hi(0, 7, 0, 16)
            hi(1, 0, 1, 16)
            with act.Fori(0, NT // 4) as four:
                i = 4 * four
                for q in range(4):
                    act.wait_ge(sums_ready, 3 * i + 3 * (q + 1))
                    hi(i + (q + 2), (q + 1) % 2, (q + 2) % 4, 4 * i + 16 * ((q + 2) // 4 + 1))

            def hi_n(n):
                if n_before(n):
                    act.wait_ge(sums_ready, n_before(n))
                hi(n, n_unit(n), n % 4, 16 * (n // 4 + 1))

            for n in range(PC_N + 1, PC_N + 4):
                hi_n(n)
            for j in range(2):
                act.wait_ge(abs_ready, j + 1)
                act.activation(g_u[:, :], g_u[:, :], ACT.Exp).then_inc(act_step, 1)
                act.wait_ge(act_step, 2 * j + 1)
                act.activation(g_u[:, :], g_u[:, :], ACT.Ln, bias=1.0).then_inc(ln_ready, 1)
                act.sem_inc(act_step, 1)
            for n in range(PC_N + 4, PC_N + 8):
                hi_n(n)
            act.wait_ge(abs_ready, 3)
            act.activation(g_u[0:H, :], g_u[0:H, :], ACT.Exp).then_inc(act_step, 1)
            act.wait_ge(act_step, 5)
            act.activation(g_u[0:H, :], g_u[0:H, :], ACT.Ln, bias=1.0).then_inc(ln_ready, 1)
            act.wait_ge(expo_ready, 1)
            act.activation(lf_ext[:, 0:ROWS], lf_ext[:, 0:ROWS], ACT.Exp).then_inc(rows_ready, 1)
            act.activation(keep[:, :], keep[:, :], ACT.Exp).then_inc(rows_ready, 1)
            m_p, m_s = ext_views(m_ext)
            act.activation(glr[0:H, 0:PROMPT], m_p, ACT.Exp, scale=-1.0).then_inc(rows_ready, 1)
            act.activation(streams(glr[0:H, PROMPT:ROWS]), m_s, ACT.Exp, scale=-1.0).then_inc(rows_ready, 1)
            for n in range(PC_N + 8, PC_N + 12):
                hi_n(n)
            for n in range(PC_N + 12, PC_OUT):
                hi_n(n)
            for t in (2, 3):
                for r in range(RT):
                    u = t * RT + r
                    act.wait_ge(sums_ready, T_USES + u + 1)
                    psum = bank[(T_USES + u) % 6][:, :]
                    if t == 2:
                        act.wait_ge(n_filled, u)
                        act.activation(sig[:, :], psum, ACT.Sigmoid).then_inc(sig_ready, 1)
                    else:
                        act.wait_ge(n_stored[u % 2], 16 * (u // 2))
                        act.activation(nout[:, u % 2, :], psum, ACT.Sigmoid).then_inc(mo_filled, 1)

        @block.tensor
        def _(pe):
            def tile_t(n, unit, use, use_bank, width=P):
                pe.wait_ge(piece_split, n + (RAW_CREDIT + 1))
                for rb in range(RB):
                    pe.wait_ge(sums_taken, use + (rb + 1))
                    for k in range(KD):
                        w = [x[:, unit, k * P:(k + 1) * P] for x in (w_hi, w_lo)]
                        x = [h[:, k, rb * RBW:(rb + 1) * RBW] for h in hT]
                        mm = mm3(pe, bank[use_bank + rb][:, 0:RBW], w, x, k == 0, k == KD - 1)
                    if rb < RB - 1:
                        mm.then_inc(sums_ready, 1)
                mm.then_inc(sums_ready, 1)

            tile_t(0, 7, 0, 0)
            with pe.Fori(0, NT // 4) as four:
                i = 4 * four
                for q in range(4):
                    tile_t(i + (q + 1), q % 2, 3 * i + 3 * (q + 1), 3 * ((q + 1) % 2))
            pe.wait_ge(small_loaded, 32)
            pe.wait_ge(sums_taken, BANK_CREDIT + RB)
            for j in range(2):
                for rb in range(RB):
                    n = j * RB + rb
                    if n >= 2:
                        pe.wait_ge(z_taken, n - 1)
                    pe.matmul(bank[6 + n % 2][:, 0:RBW], wa[:, j * P:(j + 1) * P],
                              glr[:, rb * RBW:(rb + 1) * RBW], start=True, stop=True).then_inc(z_ready, 1)
            for t in range(NN):
                units = NUNIT[t % 2]
                for r in range(RT):
                    u = t * RT + r
                    if u < 6:
                        pe.wait_ge(sums_taken, T_USES + u + 1)
                    elif u - 6 < (NN - 1) * RT:
                        pe.wait_ge(n_filled, u - 5)
                    else:
                        pe.wait_ge(mo_filled, u - 5 - (NN - 1) * RT)
                    for k in range(KD):
                        if r == 0 and k % 2 == 0:
                            pe.wait_ge(piece_split, PC_N + 4 * t + k // 2 + 1 + RAW_CREDIT)
                        x = [h[:, k, r * P:(r + 1) * P] for h in hT]
                        w = [y[:, units[k // 2], (k % 2) * 512:(k % 2 + 1) * 512] for y in (w_hi, w_lo)]
                        mm = mm3(pe, bank[(T_USES + u) % 6], x, w, k == 0, k == KD - 1)
                    mm.then_inc(sums_ready, 1)

        @block.vector
        def _(dve):
            chain = Count(dve, step)
            bf = cols[0:H, K_BG:K_BG + 1]
            bi = cols[32:32 + H, K_BG:K_BG + 1]
            i_p, i_s = ext_views(m_ext)
            lf_p, lf_s = ext_views(lf_ext)
            dve.memset(m_ext[:, :], 0.0).then_inc(step, 1)
            dve.memset(lf_ext[:, :], NEG).then_inc(step, 1)
            chain.n = 2
            dve.wait_ge(step, 2)
            for rb in range(RB):
                dve.wait_ge(sums_ready, rb + 1)
                s = slice(rb * RBW, (rb + 1) * RBW)
                (p0, pn), (s0, sn) = split_spans(rb)
                dve.tensor_scalar(g_f[:, s], bank[rb][0:H, 0:RBW], bf, None, ALU.add)
                dve.tensor_scalar(i_p[:, rb * RBW:rb * RBW + pn], bank[rb][32:32 + H, 0:pn], bi, None, ALU.add)
                if sn:
                    dve.tensor_scalar(i_s, streams(bank[rb][32:32 + H, s0:s0 + sn]), bi, None, ALU.add)
                dve.tensor_copy(glr[:, s], bank[rb][64:64 + RANK, 0:RBW]).then_inc(sums_taken, 1)
            with dve.Fori(0, NT // 4) as four:
                i = 4 * four
                for q in range(4):
                    dve.wait_ge(t_stored[q % 2], 8 * i + 16 * (q // 2 + 1))
                    for rb in range(RB):
                        dve.wait_ge(sums_ready, 3 * i + (3 * (q + 1) + rb + 1))
                        dve.tensor_copy(tout[:, q % 2, rb * RBW:(rb + 1) * RBW],
                                        bank[3 * ((q + 1) % 2) + rb][:, 0:RBW]).then_inc(sums_taken, 1)
            for j in range(2):
                dve.wait_ge(t_stored[j], 16 * (NT // 2 + 1))
                for rb in range(RB):
                    n = j * RB + rb
                    dve.wait_ge(z_ready, n + 1)
                    dve.tensor_scalar(tout[:, j, rb * RBW:(rb + 1) * RBW], bank[6 + n % 2][:, 0:RBW],
                                      cols[:, K_BA + j:K_BA + j + 1], None, ALU.add).then_inc(z_taken, 1)
                dve.wait_ge(z_taken, RB * (j + 1))
                z = tout[:, j, :]
                if j:
                    dve.wait_ge(decay_ready, j)
                dve.scalar_tensor_tensor(out=g_u[:, :], in0=z, scalar=-1.0, in1=z, op0=ALU.mult,
                                         op1=ALU.min).then_inc(abs_ready, 1)
                dve.wait_ge(ln_ready, j + 1)
                dve.scalar_tensor_tensor(out=z, in0=z, scalar=0.0, in1=g_u[:, :], op0=ALU.min,
                                         op1=ALU.subtract).then_inc(decay_ready, 1)

            def take(t):
                for r in range(RT):
                    u = t * RT + r
                    dve.wait_ge(sums_ready, T_USES + u + 1)
                    if u >= 2:
                        dve.wait_ge(n_stored[u % 2], 16 * (u // 2))
                    psum = bank[(T_USES + u) % 6][:, :]
                    if t < 2:
                        dve.tensor_copy(nout[:, u % 2, :], psum).then_inc(n_filled, 1)
                    else:
                        dve.wait_ge(sig_ready, r + 1)
                        dve.tensor_tensor(nout[:, u % 2, :], psum, sig[:, :], ALU.mult).then_inc(n_filled, 1)

            take(0)
            dve.wait_ge(small_loaded, 32)
            dve.wait_ge(decay_ready, 2)
            u4 = g_u[0:H, :]
            dve.scalar_tensor_tensor(out=u4, in0=g_f[:, :], scalar=-1.0, in1=g_f[:, :], op0=ALU.mult,
                                     op1=ALU.min).then_inc(abs_ready, 1)
            dve.wait_ge(ln_ready, 3)
            chain.link(dve.scalar_tensor_tensor(out=u4, in0=g_f[:, :], scalar=0.0, in1=u4, op0=ALU.min,
                                                op1=ALU.subtract))
            dve.tensor_copy(lf_p, u4[:, 0:PROMPT])
            dve.tensor_copy(lf_s, streams(u4[:, PROMPT:ROWS]))
            chain.link(dve.tensor_copy(first_slots(m_ext), cols[0:H, K_M0:K_M0 + NB]))
            chain.link(dve.tensor_tensor_scan(g_f[:, :], keep[:, :], u4, 0.0, ALU.mult, ALU.add))
            dve.tensor_tensor(u4[:, 0:PROMPT], i_p, g_f[:, 0:PROMPT], ALU.subtract)
            chain.link(dve.tensor_tensor(streams(u4[:, PROMPT:ROWS]), i_s, streams(g_f[:, PROMPT:ROWS]),
                                         ALU.subtract))
            chain.link(dve.tensor_tensor_scan(m_ext[:, :], lf_ext[:, :], m_ext[:, :], 0.0, ALU.add, ALU.max))
            dve.tensor_tensor(g_f[:, 0:PROMPT], g_f[:, 0:PROMPT], i_p, ALU.subtract)
            chain.link(dve.tensor_tensor(streams(g_f[:, PROMPT:ROWS]), streams(g_f[:, PROMPT:ROWS]), i_s,
                                         ALU.subtract))
            rp, rs = chunks(g_f[:, 0:PROMPT]), streams(g_f[:, PROMPT:ROWS])
            dve.tensor_tensor(chunks(lf_ext[:, 0:PROMPT]), rp,
                              chunks(m_ext[:, 0:PROMPT])[:, :, 0:1].to_broadcast([H, NC, P]), ALU.add)
            dve.tensor_tensor(streams(lf_ext[:, PROMPT:ROWS]), rs,
                              first_slots(m_ext).unsqueeze(2).to_broadcast([H, NB, LB]), ALU.add)
            dve.tensor_tensor(chunks(keep[:, 0:PROMPT]), chunks(u4[:, 0:PROMPT]),
                              rp[:, :, P - 1:P].to_broadcast([H, NC, P]), ALU.add)
            dve.tensor_tensor(streams(keep[:, PROMPT:ROWS]), streams(u4[:, PROMPT:ROWS]),
                              rs[:, :, LB - 1:LB].to_broadcast([H, NB, LB]), ALU.add).then_inc(expo_ready, 1)
            take(1)
            take(2)


def streams(ap):
    return ap.rearrange("h (b e) -> h b e", e=LB)


def chunks(ap):
    return ap.rearrange("h (c e) -> h c e", e=P)


def ext_views(ext):
    return (ext[0:H, 1:1 + PROMPT],
            ext[0:H, 1 + PROMPT:EXT].rearrange("h (b e) -> h b e", e=LB + 1)[:, :, 1:LB + 1])


def first_slots(ext):
    return ext[0:H, 1 + PROMPT:EXT].rearrange("h (b e) -> h b e", e=LB + 1)[:, :, 0]


def mix(nc, a, o, ident, cols, hT, pb, bank, sample):
    NS = NB if sample else 1
    LS = LB if sample else P
    LV0 = 3 if sample else 0
    NL = LEVELS - LV0
    SLOTS = 1 if sample else 2
    c0, c1 = (C_SHARED, N_CONST) if sample else (0, C_SAMPLE)
    nm = "s" if sample else "p"
    with ExitStack() as ctx:
        sb = lambda n, s, d=F32: ctx.enter_context(nc.sbuf_tensor(f"{nm}_{n}", s, d))
        sem = Sems(nc, ctx, f"{nm}_")
        const = sb("const", [P, c1 - c0])
        tin = sb("t_in", [P, SLOTS, NT + 2, P])
        nin = sb("n_in", [P, SLOTS, 3, 512])
        vin = sb("v_in", [P, SLOTS, H, VX])
        rin = sb("r_in", [H, SLOTS, 5, P])
        ex = sb("ex", [P, NL + 2, 2 * P])
        qx, kx = sb("qx", [P, NL + 1, 2 * P]), sb("kx", [P, NL + 1, 2 * P])
        q8 = sb("q8", [P, 2 * P])
        gsc = sb("gla_scores", [P, H, P])
        kdn = sb("k_decayed", [P, 2 * P])
        S = sb("S", [P, NS, 2, 2 * DV])
        C = sb("C", [P, NS, H, VX])
        rblk, dg = sb("rblk", [H, H * P]), sb("dg", [H, NS, H])
        NCOL = 3 * H + NS * H
        col = sb("col", [P, NCOL])
        wt, am = sb("wt", [P, H * P]), sb("am", [P, H, P])
        ksn = sb("ks", [P, H, DH])
        it, num = sb("inter", [P, H, VX]), sb("num", [P, H, VX])
        den = [sb(f"den{i}", [P, H, 1]) for i in range(3)]
        mixn, sq = sb("mixn", [P, 2 * H, P]), sb("sq", [P, 2 * H, P])
        ss, var, rstd = sb("ss", [P, 2 * H]), sb("var", [P, 2 * H]), sb("rstd", [P, 2 * H])
        if sample:
            qm = sb("q_masked", [P, H, NB * (P + LB)])
            vm = sb("v_masked", [P, NB, H * VX])
        chunk_in = [sem(f"chunk_in{s}") for s in range(SLOTS)]
        const_in, state_in, state_out = sem("const_in"), sem("state_in"), sem("state_out")
        step = sem("dve_step")
        names = ("zeroed expo_in lv_exp q8_ready kx_ready dg_ready cols_ready pd_ready qk_ready kt_ready "
                 "minter_ready cols_taken dm_ready qx_ready wt_ready it_ready am_ready ksn_ready lvl_ready "
                 "lvl_taken kdt_ready kdn_ready mintra_ready um_ready o_ready ug_ready v_ready ln_ready "
                 "rstd_ready mixn_ready mt_ready mhi_ready mix_done lvl_seen qm_ready vm_ready um_taken ug_taken")
        g = {n: sem(n) for n in names.split()}
        cs = lambda k, n: const[:, k - c0:k - c0 + n]
        ones4, blk4 = cs(C_ONE, P)[0:H, :], cs(C_BLK, H * P)[0:H, :]
        id4 = ident[0:H, 0:H]
        CREDIT, LVL_CREDIT = 2, 1
        NSTEP = 8
        bankm = pb[3]
        pair = lambda h: bankm[:, h // 2, (h % 2) * VX:(h % 2 + 1) * VX]
        half = lambda ap, h: ap[(h % 2) * DK:(h % 2 + 1) * DK]
        um_bank = lambda b: pb[1 + b % 2]
        L = NL + 1
        NPAIR = (L + 1) // 2
        lvl_banks = lambda m: pb[2 * (m % 2)]
        block = ctx.enter_context(nc.Block())

        def each_chunk(eng, body):
            if sample:
                body(0, 0)
            else:
                with eng.Fori(0, NC // 2) as two:
                    body(2 * two, 0)
                    body(2 * two + 1, 1)

        def row0(c):
            return bass.ts(c + (NC if sample else 0), P)

        @block.sync
        def _(sp):
            sp.dma_start(const[:, :], a["const"][:, c0:c1]).then_inc(const_in, 16)
            sp.wait_ge(g["zeroed"], 3)
            if sample:
                for h2 in range(2):
                    sp.dma_start(S[h2 * DK:(h2 + 1) * DK, :, :, h2 * DV:(h2 + 1) * DV],
                                 a["s_gla"][h2 * DK:(h2 + 1) * DK]).then_inc(state_in, 16)
                sp.dma_start(C[:, :, :, :], a["s_mc"]).then_inc(state_in, 16)

            def loads(c, s):
                sp.wait_ge(g["mix_done"], c + 1)
                r = row0(c)
                t = c + (NC if sample else 0)
                sp.dma_start(tin[:, s, :, :], a["pT"][:, :, r].rearrange("t p f -> p t f")).then_inc(chunk_in[s], 16)
                sp.dma_start(rin[:, s, :, :], a["rows"][:, :, r]).then_inc(chunk_in[s], 16)
                sp.dma_start(vin[:, s, :, 0:DH], a["pN"][1, t].rearrange("p (h v) -> p h v", h=H)).then_inc(chunk_in[s], 16)
                sp.dma_start(nin[:, s, 0, :], a["pN"][0, t]).then_inc(chunk_in[s], 16)
                for q in (1, 2):
                    sp.dma_start(nin[:, s, q, :], a["pN"][q + 1, t]).then_inc(chunk_in[s], 16)

            each_chunk(sp, loads)
            n = 1 if sample else NC
            sp.wait_ge(g["mix_done"], n + CREDIT)
            for h2 in range(2):
                dst = o["q_gla"] if sample else o["p_gla"].unsqueeze(1)
                sp.dma_start(dst[h2 * DK:(h2 + 1) * DK], S[h2 * DK:(h2 + 1) * DK, :, :, h2 * DV:(h2 + 1) * DV])\
                  .then_inc(state_out, 16)
            sp.dma_start(o["q_mc"] if sample else o["p_mc"].unsqueeze(1), C[:, :, :, :]).then_inc(state_out, 16)
            sp.wait_ge(state_out, 48)

        @block.gpsimd
        def _(pool):
            pool.memset(S[:, :, :, :], 0.0).then_inc(g["zeroed"], 1)
            pool.memset(C[:, :, :, :], 0.0).then_inc(g["zeroed"], 1)
            pool.memset(vin[:, :, :, DH:VX], 1.0).then_inc(g["zeroed"], 1)
            pool.memset(gsc[:, :, :], 0.0).then_inc(g["zeroed"], 1)
            if sample:
                pool.memset(qm[:, :, :], 0.0).then_inc(g["zeroed"], 1)
            pool.sem_inc(g["mix_done"], CREDIT)
            pool.sem_inc(g["lvl_taken"], LVL_CREDIT)

            def body(c, s):
                pool.wait_ge(g["lv_exp"], c + 1)
                k = tin[:, s, 2:4, :].rearrange("p j f -> p (j f)").unsqueeze(1).to_broadcast([P, NL + 1, 2 * P])
                pool.tensor_tensor(kx[:, :, :], ex[:, 1:NL + 2, :], k, ALU.mult).then_inc(g["kx_ready"], 1)

            each_chunk(pool, body)

        @block.scalar
        def _(act):
            def body(c, s):
                act.wait_ge(g["expo_in"], c + 1)
                act.activation(q8[:, :], tin[:, s, 0:2, :].rearrange("p j f -> p (j f)"), ACT.Copy,
                               scale=QSCALE).then_inc(g["q8_ready"], 1)
                act.activation(ex[:, :, :], ex[:, :, :], ACT.Exp, scale=1.0 / TAU).then_inc(g["lv_exp"], 1)
                act.wait_ge(g["dm_ready"], c + 1)
                act.activation(wt[:, :], wt[:, :], ACT.Exp).then_inc(g["wt_ready"], 1)
                act.wait_ge(g["minter_ready"], c + 1)
                act.wait_ge(g["cols_taken"], c + 1)
                for h in range(H):
                    act.activation(it[:, h, :], pair(h), ACT.Copy, scale=col[:, h:h + 1])\
                       .then_inc(g["it_ready"], 1)
                act.wait_ge(g["kdt_ready"], c + 1)
                act.activation(kdn[:, :], bank[4][:, 0:2 * P], ACT.Copy).then_inc(g["kdn_ready"], 1)
                act.wait_ge(g["v_ready"], c + 1)
                act.activation(var[:, :], var[:, :], ACT.Ln).then_inc(g["ln_ready"], 1)
                act.wait_ge(g["ln_ready"], c + 1)
                act.activation(rstd[:, :], var[:, :], ACT.Exp, scale=-0.5).then_inc(g["rstd_ready"], 1)
                for m in range(2):
                    act.wait_ge(g["mt_ready"], 2 * c + (m + 1))
                    act.activation(hT[0][:, m * H:(m + 1) * H, row0(c)],
                                   bank[m].rearrange("p (h f) -> p h f", h=H), ACT.Copy,
                                   scale=cols[:, K_GN + m:K_GN + m + 1]).then_inc(g["mhi_ready"], 1)

            each_chunk(act, body)

        @block.tensor
        def _(pe):
            def body(c, s):
                pe.wait_ge(g["dg_ready"], c + 1)
                for q in range(3):
                    pe.matmul(bank[6][:, H * q:H * (q + 1)], rin[:, s, 2 + q, :], id4, start=True, stop=True)
                pe.matmul(bank[6][:, 3 * H:NCOL], ones4, dg[:, :, :].rearrange("p b h -> p (b h)"),
                          start=True, stop=True).then_inc(g["cols_ready"], 1)
                pe.matmul(bank[5], ones4, rblk[:, :], start=True, stop=False)
                pe.matmul(bank[5], rin[:, s, 1, :], blk4, start=False, stop=True).then_inc(g["pd_ready"], 1)
                for h in range(H):
                    mm = pe.matmul(bank[2][:, h * P:(h + 1) * P], tin[:, s, 8 + h, :], tin[:, s, 4 + h, :],
                                   start=True, stop=True)
                mm.then_inc(g["qk_ready"], 1)
                for h in range(H):
                    mm = pe.transpose(bank[3][:, h * P:(h + 1) * P], tin[:, s, 8 + h, :], ident)
                mm.then_inc(g["kt_ready"], 1)
                pe.wait_ge(g["cols_taken"], c + 1)
                if sample:
                    pe.wait_ge(g["qm_ready"], 1)
                for h in range(H):
                    for b in range(NS):
                        q = qm[:, h, b * P:(b + 1) * P] if sample else tin[:, s, 4 + h, :]
                        mm = pe.matmul(pair(h), q, C[:, b, h, :], start=(b == 0), stop=(b == NS - 1))
                mm.then_inc(g["minter_ready"], 1)

                def levels(m):
                    if m >= 2:
                        pe.wait_ge(g["lvl_taken"], L * c + (2 * (m - 1) + LVL_CREDIT))
                    for n in range(2 * m, min(2 * m + 2, NL + 1)):
                        for h in range(H):
                            f = slice((h // 2) * P, (h // 2 + 1) * P)
                            if n < NL:
                                k, q = half(kx, h)[:, n, f], half(qx, h)[:, n + 1, f]
                            else:
                                k, q = half(tin, h)[:, s, 2 + h // 2, :], half(q8, h)[:, f]
                            at = (n % 2) * 2 * P + (h // 2) * P
                            mm = pe.matmul(lvl_banks(m)[:, h % 2, at:at + P], k, q, start=True, stop=True)
                    mm.then_inc(g["lvl_ready"], 1)

                pe.wait_ge(g["kx_ready"], c + 1)
                pe.wait_ge(g["qx_ready"], c + 1)
                levels(0)
                pe.wait_ge(g["dm_ready"], c + 1)
                for m in range(1, NPAIR):
                    levels(m)
                pe.wait_ge(g["it_ready"], 4 * c + 4)
                pe.wait_ge(g["am_ready"], c + 1)
                for h in range(H):
                    mm = pe.matmul(pair(h), am[:, h, :], vin[:, s, h, :], start=True, stop=True)
                mm.then_inc(g["mintra_ready"], 1)
                pe.wait_ge(g["ksn_ready"], c + 1)
                if not sample:
                    for h in range(H):
                        mm = pe.matmul(um_bank(0)[:, h // 2, (h % 2) * VX:(h % 2 + 1) * VX], ksn[:, h, :],
                                       vin[:, s, h, :], start=True, stop=True)
                    mm.then_inc(g["um_ready"], 1)
                else:
                    pe.wait_ge(g["lvl_taken"], L + LVL_CREDIT)
                    pe.wait_ge(g["vm_ready"], 1)
                    for b in range(NB):
                        if b >= 2:
                            pe.wait_ge(g["um_taken"], H * (b - 1))
                        for h in range(H):
                            mm = pe.matmul(um_bank(b)[:, h // 2, (h % 2) * VX:(h % 2 + 1) * VX], ksn[:, h, :],
                                           vm[:, b, h * VX:(h + 1) * VX], start=True, stop=True)
                        mm.then_inc(g["um_ready"], 1)
                    pe.wait_ge(g["um_taken"], H * NB)
                    pe.wait_ge(g["qm_ready"], 2)
                pe.wait_ge(g["lvl_taken"], L * c + (L + LVL_CREDIT))
                for j in range(2):
                    mm = pe.transpose(bank[4][:, j * P:(j + 1) * P], kx[:, NL, j * P:(j + 1) * P], ident)
                mm.then_inc(g["kdt_ready"], 1)
                for j in range(2):
                    out = bank[5][:, j * 256:(j + 1) * 256]
                    for b in range(NS):
                        q = qm[:, j, b * P:(b + 1) * P] if sample else qx[:, 0, j * P:(j + 1) * P]
                        pe.matmul(out, q, S[:, b, j, :], start=(b == 0), stop=False, skip_group_check=True)
                    for h in (2 * j, 2 * j + 1):
                        mm = pe.matmul(bank[5][:, h * P:(h + 1) * P], gsc[:, (h % 2) * 2 + h // 2, :], nin[:, s, 0, h * P:(h + 1) * P],
                                       start=False, stop=(h % 2 == 1), skip_group_check=True)
                mm.then_inc(g["o_ready"], 1)
                pe.wait_ge(g["kdn_ready"], c + 1)
                if sample:
                    pe.wait_ge(g["vm_ready"], 2)
                for b in range(NS):
                    if b >= 2:
                        pe.wait_ge(g["ug_taken"], H * (b - 1))
                    for j in range(2):
                        v = vm[:, b, j * 256:(j + 1) * 256] if sample else nin[:, s, 0, j * 256:(j + 1) * 256]
                        mm = pe.matmul(ug_bank(b)[:, j * 256:(j + 1) * 256], kdn[:, j * P:(j + 1) * P], v,
                                       start=True, stop=True)
                    mm.then_inc(g["ug_ready"], 1)
                pe.wait_ge(g["mixn_ready"], 8 * c + 8)
                for m in range(2):
                    for h in range(H):
                        mm = pe.transpose(bank[m][:, h * P:(h + 1) * P], mixn[:, m * H + h, :], ident)
                    mm.then_inc(g["mt_ready"], 1)

            ug_bank = lambda b: bank[2 + b % 2] if sample else bank[4]
            pe.wait_ge(const_in, 16)
            pe.wait_ge(g["zeroed"], 5 if sample else 4)
            if sample:
                pe.wait_ge(state_in, 48)
            each_chunk(pe, body)

        @block.vector
        def _(dve):
            ug_bank = lambda b: bank[2 + b % 2] if sample else bank[4]

            def body(c, s):
                chain = Count(dve, step, NSTEP * c)
                dve.wait_ge(chunk_in[s], (3 * c + (6 if s == 0 else 3)) * 16)
                keep = cs(C_KEEPB if sample else C_KEEP, 2 * P)
                la = tin[:, s, NT:NT + 2, :].rearrange("p j f -> p (j f)")
                chain.link(dve.tensor_tensor_scan(ex[:, 0, :], keep, la, 0.0, ALU.mult, ALU.add))
                for n in range(NL):
                    w = P >> (n + LV0 + 1)
                    b = ex[:, 0, :].rearrange("p (n w) -> p n w", w=2 * w)
                    e = ex[:, 1 + n, :].rearrange("p (n w) -> p n w", w=2 * w)
                    ref = b[:, :, w - 1:w].to_broadcast([P, P // w, w])
                    dve.tensor_tensor(e[:, :, 0:w], ref, b[:, :, 0:w], ALU.subtract)
                    dve.tensor_tensor(e[:, :, w:2 * w], b[:, :, w:2 * w], ref, ALU.subtract)
                b = ex[:, 0, :].rearrange("p (n w) -> p n w", w=LS)
                e = ex[:, NL + 1, :].rearrange("p (n w) -> p n w", w=LS)
                dve.tensor_tensor(e, b[:, :, LS - 1:LS].to_broadcast([P, 2 * P // LS, LS]), b, ALU.subtract)\
                   .then_inc(g["expo_in"], 1)
                dve.tensor_tensor(rblk[:, :].rearrange("p (h f) -> p h f", h=H),
                                  rin[:, s, 0, :].unsqueeze(1).to_broadcast([H, H, P]),
                                  blk4.rearrange("p (h f) -> p h f", h=H), ALU.mult)
                dec = rin[:, s, 2, :].rearrange("p (b f) -> p b f", f=LS)[:, :, LS - 1:LS]
                dve.tensor_tensor(dg[:, :, :], dec.to_broadcast([H, NS, H]),
                                  id4.unsqueeze(1).to_broadcast([H, NS, H]), ALU.mult).then_inc(g["dg_ready"], 1)
                dve.wait_ge(g["cols_ready"], c + 1)
                dve.tensor_copy(col[:, :], bank[6][:, 0:NCOL]).then_inc(g["cols_taken"], 1)
                dve.wait_ge(g["pd_ready"], c + 1)
                caus = cs(C_CAUSB if sample else C_CAUS, P)
                dve.tensor_tensor(wt[:, :].rearrange("p (h f) -> p h f", h=H),
                                  bank[5].rearrange("p (h f) -> p h f", h=H),
                                  caus.unsqueeze(1).to_broadcast([P, H, P]), ALU.add).then_inc(g["dm_ready"], 1)
                dve.wait_ge(g["q8_ready"], c + 1)
                if sample:
                    mq = tin[:, s, 4:8, :].rearrange("p h (b e) -> p h b e", e=LB)
                    dve.tensor_copy(stream_blocks(qm, H), mq).then_inc(g["qm_ready"], 1)
                dve.wait_ge(g["lv_exp"], c + 1)
                dve.tensor_tensor(qx[:, :, :], ex[:, 0:NL + 1, :],
                                  q8[:, :].unsqueeze(1).to_broadcast([P, NL + 1, 2 * P]), ALU.mult)\
                   .then_inc(g["qx_ready"], 1)
                dve.wait_ge(g["kt_ready"], c + 1)
                dve.wait_ge(g["cols_taken"], c + 1)
                for h in range(H):
                    k = dve.tensor_scalar(ksn[:, h, :], bank[3][:, h * P:(h + 1) * P], col[:, H + h:H + h + 1],
                                          KSCALE, ALU.mult, ALU.mult)
                k.then_inc(g["ksn_ready"], 1)
                dve.wait_ge(g["wt_ready"], c + 1)
                dve.scalar_tensor_tensor(out=am[:, :, :].rearrange("p h f -> p (h f)"), in0=bank[2], scalar=KSCALE,
                                         in1=wt[:, :], op0=ALU.mult, op1=ALU.mult).then_inc(g["am_ready"], 1)
                for n in range(NL + 1):
                    if n % 2 == 0:
                        dve.wait_ge(g["lvl_ready"], NPAIR * c + (n // 2 + 1))
                    dve.wait_ge(g["lvl_taken"], L * c + (n + LVL_CREDIT))
                    dve.sem_inc(g["lvl_seen"], 1)
                    k = C_LV + (n + LV0) * P
                    mask = cs(k, P).bitcast(I32).unsqueeze(1).unsqueeze(1).to_broadcast([P, 2, 2, P])
                    src = lvl_banks(n // 2)[:, :, (n % 2) * 2 * P:(n % 2 + 1) * 2 * P]
                    cp = dve.copy_predicated(gsc[:, :, :].rearrange("p (e j) f -> p e j f", e=2), mask,
                                             src.rearrange("p e (j f) -> p e j f", j=2))
                    cp.then_inc(g["lvl_taken"], 1)
                bm = cs(C_BM, NB) if sample else None
                if sample:
                    dve.tensor_tensor(vm[:, :, :], vin[:, s, :, :].rearrange("p h v -> p (h v)").unsqueeze(1)
                                      .to_broadcast([P, NB, H * VX]),
                                      bm.unsqueeze(2).to_broadcast([P, NB, H * VX]), ALU.mult)\
                       .then_inc(g["vm_ready"], 1)
                    dve.wait_ge(g["minter_ready"], 1)
                    dve.wait_ge(g["qx_ready"], 1)
                    dve.tensor_copy(stream_blocks(qm, 2),
                                    qx[:, 0, :].rearrange("p (j b e) -> p j b e", j=2, e=LB))\
                       .then_inc(g["qm_ready"], 1)
                dve.wait_ge(g["mintra_ready"], c + 1)
                dve.wait_ge(g["it_ready"], 4 * c + 4)
                chain.link(dve.tensor_tensor(num[:, :, :].rearrange("p (a b) v -> p a (b v)", a=2),
                                             it[:, :, :].rearrange("p (a b) v -> p a (b v)", a=2),
                                             bankm[:, :, 0:2 * VX], ALU.add))
                d = num[:, :, DH:VX]
                chain.link(dve.scalar_tensor_tensor(out=den[0][:, :, :], in0=d, scalar=-1.0, in1=d, op0=ALU.mult,
                                                    op1=ALU.max))
                chain.link(dve.tensor_tensor(den[1][:, :, :], den[0][:, :, :], col[:, 2 * H:3 * H].unsqueeze(2),
                                             ALU.max))
                chain.link(dve.reciprocal(den[2][:, :, :], den[1][:, :, :]))
                for h in range(H):
                    dve.scalar_tensor_tensor(out=mixn[:, H + h, :], in0=num[:, h, 0:DH], scalar=den[2][:, h, :],
                                             in1=nin[:, s, 2, h * P:(h + 1) * P], op0=ALU.mult, op1=ALU.mult)
                for b in range(NS):
                    dve.wait_ge(g["um_ready"], NS * c + (b + 1))
                    for h in range(H):
                        dve.scalar_tensor_tensor(
                            out=C[:, b, h, :], in0=C[:, b, h, :],
                            scalar=col[:, 3 * H + b * H + h:3 * H + b * H + h + 1],
                            in1=um_bank(b)[:, h // 2, (h % 2) * VX:(h % 2 + 1) * VX], op0=ALU.mult, op1=ALU.add)\
                           .then_inc(g["um_taken"], 1)
                if sample:
                    dve.tensor_tensor(vm[:, :, 0:512], nin[:, s, 0, :].unsqueeze(1).to_broadcast([P, NB, 512]),
                                      bm.unsqueeze(2).to_broadcast([P, NB, 512]), ALU.mult)\
                       .then_inc(g["vm_ready"], 1)
                dve.wait_ge(g["o_ready"], c + 1)
                chain.link(dve.tensor_copy(mixn[:, 0:H, :], bank[5].rearrange("p (h f) -> p h f", h=H)))
                for b in range(NS):
                    dve.wait_ge(g["ug_ready"], NS * c + (b + 1))
                    for h in range(H):
                        j, hs, vs = h // 2, slice((h % 2) * DK, (h % 2 + 1) * DK), slice((h % 2) * DV, (h % 2 + 1) * DV)
                        last = j * P + (b + 1) * LS - 1
                        dve.scalar_tensor_tensor(
                            out=S[hs, b, j, vs], in0=S[hs, b, j, vs], scalar=ex[hs, 0, last:last + 1],
                            in1=ug_bank(b)[hs, j * 256 + vs.start:j * 256 + vs.stop], op0=ALU.mult, op1=ALU.add)\
                           .then_inc(g["ug_taken"], 1)
                chain.link(dve.tensor_tensor(sq[:, :, :], mixn[:, :, :], mixn[:, :, :], ALU.mult))
                chain.link(dve.tensor_reduce(ss[:, :], sq[:, :, :], AX.X, ALU.add))
                dve.tensor_scalar(var[:, :], ss[:, :], 1.0 / P, EPS, ALU.mult, ALU.add).then_inc(g["v_ready"], 1)
                dve.wait_ge(g["rstd_ready"], c + 1)
                for h in range(H):
                    dve.scalar_tensor_tensor(out=mixn[:, h, :], in0=mixn[:, h, :], scalar=rstd[:, h:h + 1],
                                             in1=nin[:, s, 1, h * P:(h + 1) * P], op0=ALU.mult, op1=ALU.mult)\
                       .then_inc(g["mixn_ready"], 1)
                for h in range(H):
                    dve.tensor_scalar(mixn[:, H + h, :], mixn[:, H + h, :], rstd[:, H + h:H + h + 1], None,
                                      ALU.mult).then_inc(g["mixn_ready"], 1)
                for m in range(2):
                    dve.wait_ge(g["mhi_ready"], 2 * c + (m + 1))
                    rows = (slice(None), slice(m * H, (m + 1) * H), row0(c))
                    lo = dve.scalar_tensor_tensor(
                        out=hT[1][rows], in0=bank[m].rearrange("p (h f) -> p h f", h=H),
                        scalar=cols[:, K_GN + m:K_GN + m + 1], in1=hT[0][rows].bitcast(F32), op0=ALU.mult,
                        op1=ALU.subtract)
                lo.then_inc(g["mix_done"], 1)
                assert chain.n == NSTEP, chain.n

            dve.wait_ge(const_in, 16)
            dve.wait_ge(g["zeroed"], 5 if sample else 4)
            if sample:
                dve.wait_ge(state_in, 48)
            each_chunk(dve, body)


def stream_blocks(qm, n):
    return qm[:, 0:n, :].rearrange("p h (b e) -> p h b e", e=P + LB)[:, :, :, 0:LB]


def output(nc, a, x9, hT, ident, gain2, bank):
    with ExitStack() as ctx:
        sb = lambda n, s, d=F32: ctx.enter_context(nc.sbuf_tensor(f"o_{n}", s, d))
        sem = lambda n: ctx.enter_context(nc.semaphore(f"o_{n}"))
        raw = sb("w_raw", [P, 2, PIECE])
        w_hi, w_lo = sb("w_hi", [P, KD, PIECE], F32R), sb("w_lo", [P, KD, PIECE], F32R)
        x_loaded = [sem(f"x_loaded{r}") for r in range(RT)]
        raw_loaded = [sem(f"raw_loaded{s}") for s in range(2)]
        piece_hi, piece_split = sem("piece_hi"), sem("piece_split")
        sums_ready, added, step = sem("sums_ready"), sem("added"), sem("step")
        norm = Norm(nc, ctx, "norm2", x9, hT, ident, gain2, bank[6:8])
        block = ctx.enter_context(nc.Block())

        @block.sync
        def _(sp):
            for n in range(KD):
                if n >= 2:
                    sp.wait_ge(piece_split, n - 1)
                sp.dma_start(raw[:, n % 2, :], a["w"][PC_OUT + n]).then_inc(raw_loaded[n % 2], 16)
            for r in range(RT):
                sp.dma_start(x9[:, r, :], a["x"][r]).then_inc(x_loaded[r], 16)

        @block.gpsimd
        def _(pool):
            for n in range(KD):
                pool.wait_ge(piece_hi, n + 1)
                pool.tensor_tensor(w_lo[:, n, :], raw[:, n % 2, :], w_hi[:, n, :].bitcast(F32),
                                   ALU.subtract).then_inc(piece_split, 1)

        @block.scalar
        def _(act):
            for n in range(KD):
                act.wait_ge(raw_loaded[n % 2], 16 * (n // 2 + 1))
                act.activation(w_hi[:, n, :], raw[:, n % 2, :], ACT.Copy).then_inc(piece_hi, 1)
            ready = lambda eng, r: eng.wait_ge(added, 2 * r + 2)
            norm.act_sums(act, 0, ready)
            norm.act_root(act, 0)
            for rb in range(1, RB):
                norm.act_sums(act, rb, ready)
                norm.act_hi(act, rb - 1)
                norm.act_root(act, rb)
            norm.act_hi(act, RB - 1)

        @block.tensor
        def _(pe):
            def rows(rb):
                for u in range(2 * JR * rb, 2 * JR * (rb + 1)):
                    r, n = divmod(u, 2)
                    if u >= 6:
                        pe.wait_ge(added, u - 5)
                    for k in range(KD):
                        if u == 0:
                            pe.wait_ge(piece_split, k + 1)
                        x = [h[:, k, r * P:(r + 1) * P] for h in hT]
                        w = [y[:, k, n * 512:(n + 1) * 512] for y in (w_hi, w_lo)]
                        mm = mm3(pe, bank[u % 6], x, w, k == 0, k == KD - 1)
                    mm.then_inc(sums_ready, 1)

            rows(0)
            for rb in range(1, RB):
                rows(rb)
                norm.pe_turn(pe, rb - 1)
            norm.pe_turn(pe, RB - 1)

        @block.vector
        def _(dve):
            chain = Count(dve, step)

            def add(rb):
                for u in range(2 * JR * rb, 2 * JR * (rb + 1)):
                    r, n = divmod(u, 2)
                    if n == 0:
                        dve.wait_ge(x_loaded[r], 16)
                    dve.wait_ge(sums_ready, u + 1)
                    x = x9[:, r, n * 512:(n + 1) * 512]
                    dve.tensor_tensor(x, bank[u % 6], x, ALU.add).then_inc(added, 1)

            for rb in range(RB):
                add(rb)
                if rb:
                    norm.dve_lo(dve, rb - 1)
                norm.dve_invert(dve, rb, chain)
                norm.dve_scale(dve, rb)
            norm.dve_lo(dve, RB - 1)


def ffn(nc, a, o, x9, hT, bank):
    NP = NF // 2
    SX = LB + 2
    with ExitStack() as ctx:
        sb = lambda n, s, d=F32: ctx.enter_context(nc.sbuf_tensor(f"f_{n}", s, d))
        sem = lambda n: ctx.enter_context(nc.semaphore(f"f_{n}"))
        raw = sb("w_raw", [P, 3, PIECE])
        w_hi, w_lo = sb("w_hi", [P, 6, PIECE], F32R), sb("w_lo", [P, 6, PIECE], F32R)
        a_hi, a_lo = sb("a_hi", [P, 2, ROWS], F32R), sb("a_lo", [P, 2, ROWS], F32R)
        gp = sb("gate_prompt", [P, 2 + PROMPT])
        gs = sb("gate_sample", [P, NB, SX])
        gc = sb("gate_conv", [P, 2, RBW])
        cache, taps = sb("cache", [P, NF, 2 * NB]), sb("taps", [P, NF, 4])
        tails = sb("tails", [P, NF, 2 + 2 * NB])
        raw_loaded = [sem(f"raw_loaded{s}") for s in range(3)]
        small_in, tails_out = sem("small_in"), sem("tails_out")
        piece_hi, piece_split = sem("piece_hi"), sem("piece_split")
        up_ready = sem("up_ready")
        g_out = sem("g_out")
        conv_step, conv_done = sem("conv_step"), sem("conv_done")
        gelu_done, u_taken = sem("gelu_done"), sem("u_taken")
        ahi_done, a_split = sem("ahi_done"), sem("a_split")
        down_ready, down_added = sem("down_ready"), sem("down_added")
        tails_done, zeroed = sem("tails_done"), sem("zeroed")
        RAW, UP, CONV, GC, DOWN = 3, 3, 3, 2, 2
        NG = 5
        def splits_after(n, last):
            return () if last and n > 1 else ((0,), (1,), (), (2,), (3,), (4, 5))[n]

        block = ctx.enter_context(nc.Block())

        def pairs(eng, body):
            with eng.Fori(0, NP - 1) as i:
                body(i, False)
            body(NP - 1, True)

        @block.sync
        def _(sp):
            def load(m, slot):
                sp.wait_ge(piece_split, m + 1)
                sp.dma_start(raw[:, slot, :], a["w"][m + PC_FFN]).then_inc(raw_loaded[slot], 16)

            sp.dma_start(cache[:, :, :], a["cache"]).then_inc(small_in, 16)
            sp.dma_start(taps[:, :, :], a["taps"]).then_inc(small_in, 16)
            for m in range(4):
                load(m, m % 3)

            def body(i, last):
                for k in range(2 if last else 6):
                    load(6 * i + (4 + k), (4 + k) % 3)

            pairs(sp, body)
            sp.wait_ge(tails_done, 2 * NF)
            sp.dma_start(o["conv"], tails[:, :, :]).then_inc(tails_out, 16)
            sp.wait_ge(tails_out, 16)

        @block.gpsimd
        def _(pool):
            for s, n in ((piece_split, RAW), (u_taken, UP), (conv_done, CONV), (a_split, GC), (down_added, DOWN)):
                pool.sem_inc(s, n)
            pool.memset(gp[:, 0:2], 0.0).then_inc(zeroed, 1)

            def lo(m, unit, slot):
                pool.wait_ge(piece_hi, m + 1)
                pool.tensor_tensor(w_lo[:, unit, :], raw[:, slot, :], w_hi[:, unit, :].bitcast(F32),
                                   ALU.subtract).then_inc(piece_split, 1)

            for m in range(4):
                lo(m, m, m % 3)

            def body(i, last):
                for n in range(2 * RB):
                    q, rb = divmod(n, RB)
                    s = slice(rb * RBW, (rb + 1) * RBW)
                    pool.wait_ge(ahi_done, 6 * i + (n + 1))
                    pool.tensor_tensor(a_lo[:, q, s], gc[:, n % 2, :], a_hi[:, q, s].bitcast(F32),
                                       ALU.subtract).then_inc(a_split, 1)
                    for k in splits_after(n, last):
                        lo(6 * i + (4 + k), (4 + k) % 6, (4 + k) % 3)

            pairs(pool, body)

        @block.scalar
        def _(act):
            def hi(m, unit, slot, loads):
                act.wait_ge(raw_loaded[slot], loads)
                act.activation(w_hi[:, unit, :], raw[:, slot, :], ACT.Copy).then_inc(piece_hi, 1)

            for m in range(4):
                hi(m, m, m % 3, 16 * (m // 3 + 1))
            act.wait_ge(small_in, 32)

            def body(i, last):
                for n in range(2 * RB):
                    q, rb = divmod(n, RB)
                    f = 2 * i + q
                    act.wait_ge(up_ready, 12 * i + (2 * n + 1))
                    act.wait_ge(conv_done, 6 * i + (3 * q + (2 if rb == 0 else 3)))
                    g = bank[2 * rb]
                    if rb < 2:
                        act.activation(gp[:, 2 + rb * RBW:2 + (rb + 1) * RBW], g[:, 0:RBW], ACT.Copy).then_inc(g_out, 1)
                    else:
                        np_ = PROMPT - 2 * RBW
                        act.activation(gp[:, 2 + 2 * RBW:2 + PROMPT], g[:, 0:np_], ACT.Copy).then_inc(g_out, 1)
                        act.activation(gs[:, :, 2:SX], streams(g[:, np_:RBW]), ACT.Copy).then_inc(g_out, 1)
                        act.activation(gs[:, :, 0:2], cache[:, f, :].rearrange("p (b e) -> p b e", e=2),
                                       ACT.Copy).then_inc(g_out, 1)
                        act.wait_ge(g_out, 2 * NG * i + NG * (q + 1))
                        act.activation(tails[:, f, 0:2], gp[:, PROMPT:PROMPT + 2], ACT.Copy).then_inc(tails_done, 1)
                        act.activation(tails[:, f, 2:2 + 2 * NB].rearrange("p (b e) -> p b e", e=2),
                                       gs[:, :, LB:SX], ACT.Copy).then_inc(tails_done, 1)
                    act.wait_ge(conv_done, 6 * i + (n + 1 + CONV))
                    act.activation(gc[:, n % 2, :], gc[:, n % 2, :], ACT.Gelu_apprx_tanh).then_inc(gelu_done, 1)
                    act.wait_ge(u_taken, 6 * i + (n + 1 + UP))
                    act.activation(a_hi[:, q, rb * RBW:(rb + 1) * RBW], gc[:, n % 2, :], ACT.Copy).then_inc(ahi_done, 1)
                    for k in splits_after(n, last):
                        if k < 2:
                            act.wait_ge(up_ready, 12 * i + 1)
                        else:
                            act.wait_ge(up_ready, 12 * i + (5, 6, 11, 12)[k - 2])
                        hi(6 * i + (4 + k), (4 + k) % 6, (4 + k) % 3, 32 * i + 16 * ((4 + k) // 3 + 1))

            pairs(act, body)

        @block.tensor
        def _(pe):
            with pe.Fori(0, NP) as i:
                for q in range(2):
                    for rb in range(RB):
                        n = 3 * q + rb
                        pe.wait_ge(u_taken, 6 * i + (n + 1))
                        for m in range(2):
                            if rb == 0:
                                pe.wait_ge(piece_split, 6 * i + (2 * q + m + 1 + RAW))
                            for k in range(KD):
                                w = [y[:, 2 * q + m, k * P:(k + 1) * P] for y in (w_hi, w_lo)]
                                x = [h[:, k, rb * RBW:(rb + 1) * RBW] for h in hT]
                                mm = mm3(pe, bank[2 * rb + m][:, 0:RBW], w, x, k == 0, k == KD - 1)
                            mm.then_inc(up_ready, 1)
                pe.wait_ge(piece_split, 6 * i + (6 + RAW))
                for r in range(RT):
                    if r % JR == 0:
                        pe.wait_ge(a_split, 6 * i + (RB + r // JR + 1 + GC))
                    for half in range(2):
                        pe.wait_ge(down_added, 2 * RT * i + (2 * r + half + 1))
                        for q in range(2):
                            x = [y[:, q, r * P:(r + 1) * P] for y in (a_hi, a_lo)]
                            w = [y[:, 4 + q, half * 512:(half + 1) * 512] for y in (w_hi, w_lo)]
                            mm = mm3(pe, bank[6 + half], x, w, q == 0, q == 1)
                        mm.then_inc(down_ready, 1)

        @block.vector
        def _(dve):
            dve.wait_ge(small_in, 32)
            dve.wait_ge(zeroed, 1)
            with dve.Fori(0, NP) as i:
                chain = Count(dve, conv_step, 12 * i)
                for n in range(2 * RB):
                    q, rb = divmod(n, RB)
                    tap = [taps[:, 2 * i + q, j:j + 1] for j in range(4)]
                    np_ = min(RBW, PROMPT - rb * RBW)
                    out = gc[:, n % 2, :]
                    parts = [(lambda j: gp[:, rb * RBW + j:rb * RBW + j + np_], out[:, 0:np_])]
                    if np_ < RBW:
                        parts.append((lambda j: gs[:, :, j:j + LB], streams(out[:, np_:RBW])))
                    dve.wait_ge(g_out, 2 * NG * i + (NG * q + (rb + 1 if rb < 2 else NG)))
                    dve.wait_ge(a_split, 6 * i + (n + 1))
                    for src, dst in parts:
                        ins = dve.tensor_scalar(dst, src(2), tap[2], tap[3], ALU.mult, ALU.add)
                    chain.link(ins)
                    for src, dst in parts:
                        ins = dve.scalar_tensor_tensor(out=dst, in0=src(1), scalar=tap[1], in1=dst, op0=ALU.mult,
                                                       op1=ALU.add)
                    chain.link(ins)
                    for src, dst in parts:
                        ins = dve.scalar_tensor_tensor(out=dst, in0=src(0), scalar=tap[0], in1=dst, op0=ALU.mult,
                                                       op1=ALU.add)
                    ins.then_inc(conv_done, 1)
                    dve.wait_ge(gelu_done, 6 * i + (n + 1))
                    dve.wait_ge(up_ready, 12 * i + (2 * n + 2))
                    dve.tensor_tensor(out, bank[2 * rb + 1][:, 0:RBW], out, ALU.mult).then_inc(u_taken, 1)
                assert chain.n == 12
                for u in range(2 * RT):
                    r, half = divmod(u, 2)
                    x = x9[:, r, half * 512:(half + 1) * 512]
                    dve.wait_ge(down_ready, 2 * RT * i + (u + 1))
                    dve.tensor_tensor(x, bank[6 + half], x, ALU.add).then_inc(down_added, 1)

    with ExitStack() as ctx:
        sb = lambda n, s, d=F32: ctx.enter_context(nc.sbuf_tensor(f"e_{n}", s, d))
        sem = lambda n: ctx.enter_context(nc.semaphore(f"e_{n}"))
        SLOTS = 3
        gain = sb("gain", [P, D])
        yt, sq = sb("y", [P, SLOTS, D]), sb("sq", [P, D])
        ss, inv, rstd = sb("ss", [P, RT]), sb("inv", [P, RT]), sb("rstd", [P, RT])
        gain_in = sem("gain_in")
        stored = [sem(f"stored{s}") for s in range(SLOTS)]
        summed, shifted, inverted, rooted, y_ready = (sem(n) for n in "summed shifted inverted rooted y_ready".split())
        block = ctx.enter_context(nc.Block())

        @block.sync
        def _(sp):
            sp.dma_start(gain[:, :], a["norm_f"].to_broadcast([P, D])).then_inc(gain_in, 16)
            for r in range(RT):
                sp.wait_ge(y_ready, r + 1)
                sp.dma_start(o["y"][r], yt[:, r % SLOTS, :]).then_inc(stored[r % SLOTS], 16)
            for s in range(SLOTS):
                sp.wait_ge(stored[s], 16 * (RT // SLOTS))

        @block.scalar
        def _(act):
            for r in range(RT):
                if r:
                    act.wait_ge(summed, r)
                act.activation(sq[:, :], x9[:, r, :], ACT.Square, accum_out=ss[:, r:r + 1]).then_inc(summed, 1)
                if r % JR == JR - 1:
                    act.wait_ge(inverted, r // JR + 1)
                    s = slice(r - JR + 1, r + 1)
                    act.activation(rstd[:, s], inv[:, s], ACT.Sqrt).then_inc(rooted, 1)

        @block.vector
        def _(dve):
            dve.wait_ge(gain_in, 16)
            for r in range(RT):
                if r % JR == 0:
                    s = slice(r, r + JR)
                    dve.wait_ge(summed, r + JR)
                    dve.tensor_scalar(ss[:, s], ss[:, s], 1.0 / D, EPS, ALU.mult, ALU.add).then_inc(shifted, 1)
                    dve.wait_ge(shifted, r // JR + 1)
                    dve.reciprocal(inv[:, s], ss[:, s]).then_inc(inverted, 1)
                    dve.wait_ge(rooted, r // JR + 1)
                if r >= SLOTS:
                    dve.wait_ge(stored[r % SLOTS], 16 * (r // SLOTS))
                dve.scalar_tensor_tensor(out=yt[:, r % SLOTS, :], in0=x9[:, r, :], scalar=rstd[:, r:r + 1],
                                         in1=gain[:, :], op0=ALU.mult, op1=ALU.mult).then_inc(y_ready, 1)


def kernel(**inputs):
    import numpy as np
    import concourse.bacc as _bacc
    from concourse.bass_utils import run_bass_kernel_spmd as _run

    g = {n: np.asarray(v) for n, v in inputs.items()}
    f32 = np.float32
    w_in, w_out = g["w_in"][0], g["w_out"][0]
    QK, V, W = H * DK, H * DV, H * DH
    ofs = np.cumsum([0, QK, QK, V, V, RANK, W, W, W, W, H, H])
    gq, gk, gv, gr, gl, mq, mk, mv, mo, mi, mf = [w_in[:, ofs[i]:ofs[i + 1]] for i in range(11)]

    def piece(w):
        n = w.shape[1]
        per = PIECE // n
        return w.reshape(KD // per, per, P, n).transpose(0, 2, 1, 3).reshape(KD // per, P, PIECE)

    gate = np.zeros((D, P), f32)
    gate[:, 0:H], gate[:, 32:32 + H], gate[:, 64:64 + RANK] = mf, mi, gl
    trans = np.concatenate([gq, gk, mq, mk], axis=1)
    pieces = [piece(gate)]
    pieces += [piece(trans[:, t * P:(t + 1) * P]) for t in range(NT)]
    pieces += [piece(w) for w in (gv, mv, gr, mo)]
    pieces += [w_out.reshape(KD, P, D)]
    wg, wu, wd = g["w_g"][0], g["w_u"][0], g["w_d"][0].reshape(NF, P, D)
    up = [(piece(wg[:, f * P:(f + 1) * P]), piece(wu[:, f * P:(f + 1) * P])) for f in range(NF)]
    pieces += [*up[0], *up[1]]
    for i in range(0, NF, 2):
        pieces += [wd[i:i + 2]]
        if i + 2 < NF:
            pieces += [*up[i + 2], *up[i + 3]]
    ins = {"w": np.concatenate(pieces)}
    assert ins["w"].shape == (N_PIECES, P, PIECE)
    ins["x"] = np.concatenate([g["x_prompt"][0], g["x_sample"].reshape(-1, D)]).reshape(RT, P, D)
    cols = np.zeros((P, N_COL), f32)
    cols[:, K_N1:K_N1 + KD] = g["norm1"][0].reshape(KD, P).T
    cols[:, K_N2:K_N2 + KD] = g["norm2"][0].reshape(KD, P).T
    cols[:, K_GN] = g["gla_norm"][0]
    cols[:, K_MN] = g["m_norm"][0]
    cols[:, K_BA:K_BA + 2] = g["b_gla_a"][0].reshape(2, P).T
    cols[0:H, K_BG], cols[32:32 + H, K_BG] = g["b_m_f"][0], g["b_m_i"][0]
    cols[0:H, K_M0:K_M0 + NB] = g["state_mlstm_m"][0].T
    ins["cols"] = cols
    ins["w_decay"] = g["w_gla_a"][0]
    keep = np.ones((H, ROWS), f32)
    keep[:, 0:PROMPT:P] = 0
    keep[:, PROMPT::LB] = 0
    ins["keep"] = keep
    ins["ident"] = np.eye(P, dtype=f32)
    s, t = np.arange(P)[:, None], np.arange(P)[None, :]
    const = np.zeros((P, N_CONST), f32)
    for lv in range(LEVELS):
        w = P >> (lv + 1)
        const[:, C_LV + lv * P:C_LV + (lv + 1) * P] = (s // (2 * w) == t // (2 * w)) & (s % (2 * w) < w) & (t % (2 * w) >= w)
    const[:, C_LV + LEVELS * P:C_LV + (LEVELS + 1) * P] = s == t
    const[:, C_CAUS:C_CAUS + P] = np.where(s <= t, 0.0, NEG)
    const[:, C_CAUSB:C_CAUSB + P] = np.where((s <= t) & (s // LB == t // LB), 0.0, NEG)
    const[:, C_KEEP:C_KEEP + 2 * P] = np.arange(2 * P) % P != 0
    const[:, C_KEEPB:C_KEEPB + 2 * P] = np.arange(2 * P) % LB != 0
    const[:, C_BM:C_BM + NB] = s // LB == np.arange(NB)[None, :]
    const[:, C_ONE:C_ONE + P] = 1.0
    const[0:H, C_BLK:C_BLK + H * P] = np.repeat(np.eye(H), P, axis=1)
    ins["const"] = const
    ins["cache"] = g["cache_ffn_conv"][0].reshape(NB * 2, NF, P).transpose(2, 1, 0)
    taps = np.concatenate([g["conv_w"][0], g["conv_b"]])
    ins["taps"] = taps.reshape(4, NF, P).transpose(2, 1, 0)
    ins["norm_f"] = g["norm_f"].reshape(1, D)
    ins["s_gla"] = g["state_gla"][0].reshape(NB, 2, 2, DK, DV).transpose(2, 3, 0, 1, 4).reshape(P, NB, 2, DV)
    ins["s_mc"] = np.concatenate([g["state_mlstm_C"][0].transpose(2, 0, 1, 3),
                                  g["state_mlstm_n"][0].transpose(2, 0, 1)[..., None]], axis=3)
    outs = {"y": (RT, P, D), "p_gla": (P, 2, DV), "p_mc": (P, H, VX), "mm": (H, EXT), "conv": (P, NF, 2 + 2 * NB),
            "q_gla": (P, NB, 2, DV), "q_mc": (P, NB, H, VX)}
    scratch = {"pT": (NT + 2, P, ROWS), "pN": (NN, RT, P, 512), "rows": (H, 5, ROWS)}
    nc = _bacc.Bacc("TRN2", target_bir_lowering=False, num_devices=1)
    ins = {n: np.ascontiguousarray(v) for n, v in ins.items()}
    a = {n: nc.dram_tensor(f"in_{n}", v.shape, F32, kind="ExternalInput").ap() for n, v in ins.items()}
    a.update({n: nc.dram_tensor(f"scratch_{n}", s, F32, kind="Internal").ap() for n, s in scratch.items()})
    o = {n: nc.dram_tensor(f"out_{n}", s, F32, kind="ExternalOutput").ap() for n, s in outs.items()}
    build(nc, a, o)
    r = _run(nc, [{f"in_{n}": v for n, v in ins.items()}], core_ids=[0]).results[0]
    y = r["out_y"].reshape(ROWS, D)
    mm = r["out_mm"]
    conv = r["out_conv"].transpose(2, 1, 0).reshape(2 + 2 * NB, F)

    def gla(s):
        return s.reshape(2, DK, -1, 2, DV).transpose(2, 3, 0, 1, 4).reshape(1, -1, H, DK, DV)

    def mc(s):
        s = s.reshape(P, -1, H, VX)
        return s[..., 0:DH].transpose(1, 2, 0, 3)[None], s[..., DH].transpose(1, 2, 0)[None]

    p_c, p_n = mc(r["out_p_mc"])
    q_c, q_n = mc(r["out_q_mc"])
    q_m = mm[:, 1 + PROMPT:].reshape(H, NB, LB + 1)[:, :, LB].T
    res = (y[0:PROMPT][None], y[PROMPT:].reshape(NB, LB, D),
           gla(r["out_p_gla"]), p_c, p_n, mm[:, PROMPT].reshape(1, 1, H), conv[0:2].reshape(1, 1, 2, F),
           gla(r["out_q_gla"]), q_c, q_n, q_m.reshape(1, NB, H), conv[2:].reshape(1, NB, 2, F))
    return tuple(np.ascontiguousarray(v) for v in res)
```

```python
from contextlib import ExitStack

import concourse.bass as bass
from concourse import mybir

F32 = mybir.dt.float32
F32R = mybir.dt.float32r
I32 = mybir.dt.int32
ALU = mybir.AluOpType
ACT = mybir.ActivationFunctionType
AX = mybir.AxisListType

P = 128
D = 1024
KD = D // P
PROMPT = 1024
NB, LB = 8, 16
ROWS = PROMPT + NB * LB
RT = ROWS // P
NC = PROMPT // P
RBW = 384
RB = ROWS // RBW
JR = RBW // P
EPS = 1e-6
H = 4
DK, DV, DH = 64, 128, 128
VX = DH + 1
RANK = 16
TAU = 16.0
F = 2816
NF = F // P
QSCALE = DK ** -0.5
KSCALE = DH ** -0.5
NT = 12
NN = 4
LEVELS = 7
PIECE = D
PC_GATE, PC_T, PC_N = 0, 1, 1 + NT
PC_OUT = PC_N + 4 * NN
PC_FFN = PC_OUT + KD
N_PIECES = PC_FFN + 3 * NF
EXT = 1 + PROMPT + NB * (LB + 1)
NEG = -1.0e30
C_CAUS = 0
C_KEEP = C_CAUS + P
C_LV = C_KEEP + 2 * P
C_SHARED = C_LV + 3 * P // 2
C_DIAG = C_LV + LEVELS * P // 2
C_ONE = C_DIAG + P
C_SAMPLE = C_ONE + P
C_CAUSB = C_SAMPLE
C_KEEPB = C_CAUSB + P
C_BM = C_KEEPB + 2 * P
N_CONST = C_BM + NB
K_N1, K_N2, K_MIX, K_BA, K_BG = 0, 8, 16, 24, 26
K_M0 = 27
N_COL = K_M0 + NB


class Count:

    def __init__(self, eng, sem, base=0):
        self.eng, self.sem, self.base, self.n = eng, sem, base, 0

    def link(self, ins):
        ins.then_inc(self.sem, 1)
        self.n += 1
        self.eng.wait_ge(self.sem, self.base + self.n)


class Sems:

    def __init__(self, nc, ctx, prefix):
        self.nc, self.prefix, self.taken = nc, prefix, []
        ctx.callback(self.clear)

    def __call__(self, name):
        self.taken.append(self.nc.alloc_semaphore(name=self.prefix + name))
        return self.taken[-1]

    def clear(self):
        self.nc.clear_and_free_semaphores(self.taken)
        self.nc.all_engine_barrier()


def mm3(pe, out, stat, mov, start, stop):
    pe.matmul(out, stat[0], mov[0], start=start, stop=False)
    pe.matmul(out, stat[0], mov[1], start=False, stop=False)
    return pe.matmul(out, stat[1], mov[0], start=False, stop=stop)


class Turn:

    def __init__(self, nc, sem, name, hT, ident, gain, banks, source):
        self.hT, self.ident, self.gain, self.banks, self.source = hT, ident, gain, banks, source
        self.turned, self.hi_done, self.lo_done = (sem(f"{name}_{n}") for n in ("turned", "hi", "lo"))

    def pe_turn(self, pe, rb):
        for k in range(KD):
            n = rb * KD + k
            if n >= 2:
                pe.wait_ge(self.lo_done, n - 1)
            for j in range(JR):
                t = pe.transpose(self.banks[n % 2][:, j * P:(j + 1) * P], self.source(rb, j, k), self.ident)
            t.then_inc(self.turned, 1)

    def act_hi(self, act, rb, ks=range(KD)):
        for k in ks:
            n = rb * KD + k
            act.wait_ge(self.turned, n + 1)
            act.activation(self.hT[0][:, k, rb * RBW:(rb + 1) * RBW], self.banks[n % 2][:, 0:RBW], ACT.Copy,
                           scale=self.gain[:, k:k + 1]).then_inc(self.hi_done, 1)

    def dve_lo(self, dve, rb):
        for k in range(KD):
            n = rb * KD + k
            s = slice(rb * RBW, (rb + 1) * RBW)
            dve.wait_ge(self.hi_done, n + 1)
            dve.scalar_tensor_tensor(out=self.hT[1][:, k, s], in0=self.banks[n % 2][:, 0:RBW],
                                     scalar=self.gain[:, k:k + 1], in1=self.hT[0][:, k, s].bitcast(F32),
                                     op0=ALU.mult, op1=ALU.subtract).then_inc(self.lo_done, 1)


class Norm(Turn):

    def __init__(self, nc, ctx, sem, name, x9, hT, ident, gain, banks):
        sb = lambda n, s: ctx.enter_context(nc.sbuf_tensor(f"{name}_{n}", s, F32))
        self.x9 = x9
        self.xs = sb("scaled", [P, JR, D])
        self.sq = sb("squares", [P, D])
        self.ss = sb("sumsq", [P, RT])
        self.inv = sb("inv", [P, RT])
        self.rstd = sb("rstd", [P, RT])
        self.summed, self.inverted, self.rooted, self.scaled = (
            sem(f"{name}_{n}") for n in ("summed", "inverted", "rooted", "scaled"))
        super().__init__(nc, sem, name, hT, ident, gain, banks, lambda rb, j, k: self.xs[:, j, k * P:(k + 1) * P])

    def pe_turn(self, pe, rb):
        pe.wait_ge(self.scaled, rb * JR + JR)
        super().pe_turn(pe, rb)

    def act_sums(self, act, rb, ready):
        for r in range(rb * JR, rb * JR + JR):
            ready(act, r)
            if r:
                act.wait_ge(self.summed, r)
            act.activation(self.sq[:, :], self.x9[:, r, :], ACT.Square,
                           accum_out=self.ss[:, r:r + 1]).then_inc(self.summed, 1)

    def act_root(self, act, rb):
        act.wait_ge(self.inverted, rb + 1)
        s = slice(rb * JR, rb * JR + JR)
        act.activation(self.rstd[:, s], self.inv[:, s], ACT.Sqrt).then_inc(self.rooted, 1)

    def dve_invert(self, dve, rb, chain):
        s = slice(rb * JR, rb * JR + JR)
        dve.wait_ge(self.summed, rb * JR + JR)
        chain.link(dve.tensor_scalar(self.ss[:, s], self.ss[:, s], 1.0 / D, EPS, ALU.mult, ALU.add))
        dve.reciprocal(self.inv[:, s], self.ss[:, s]).then_inc(self.inverted, 1)

    def dve_scale(self, dve, rb):
        dve.wait_ge(self.rooted, rb + 1)
        if rb:
            dve.wait_ge(self.turned, rb * KD)
        for j in range(JR):
            r = rb * JR + j
            dve.tensor_scalar(self.xs[:, j, :], self.x9[:, r, :], self.rstd[:, r:r + 1], None,
                              ALU.mult).then_inc(self.scaled, 1)


def build(nc, a, o):
    with ExitStack() as top:
        sb = lambda n, s, d=F32: top.enter_context(nc.sbuf_tensor(n, s, d))
        pb = [top.enter_context(nc.psum_tensor(f"bank{2 * i}", [P, 2, 512], F32)) for i in range(4)]
        bank = [pb[i // 2][:, i % 2, :] for i in range(8)]
        const = sb("ident", [P, P])
        cols = sb("cols", [P, N_COL])
        ident = const[:, :]

        def halves(ctx, name):
            return [ctx.enter_context(nc.sbuf_tensor(f"{name}_{n}", [P, KD, ROWS], F32R)) for n in ("hi", "lo")]

        with ExitStack() as ctx:
            hT = halves(ctx, "h1T")
            normalise(nc, a, const, cols, hT, ident, bank)
            project(nc, a, o, cols, hT, bank)
        x9, ssq = sb("x9", [P, RT, D]), sb("ssq", [P, RT, 2 * H])
        mix(nc, a, o, ident, x9, ssq, pb, bank, sample=False)
        mix(nc, a, o, ident, x9, ssq, pb, bank, sample=True)
        hT = halves(top, "h2T")
        output(nc, a, x9, ssq, cols, hT, ident, bank)
        ffn(nc, a, o, x9, hT, bank)


def normalise(nc, a, const, cols, hT, ident, bank):
    with ExitStack() as ctx:
        sem = Sems(nc, ctx, "")
        x9 = ctx.enter_context(nc.sbuf_tensor("x_in", [P, RT, D], F32))
        x_loaded = [sem(f"x_loaded{r}") for r in range(RT)]
        const_loaded = sem("const_loaded")
        step = sem("norm_step")
        norm = Norm(nc, ctx, sem, "norm1", x9, hT, ident, cols[:, K_N1:K_N1 + KD], bank[0:2])
        block = ctx.enter_context(nc.Block())

        @block.sync
        def _(sp):
            for r in range(RT):
                sp.dma_start(x9[:, r, :], a["x"][r]).then_inc(x_loaded[r], 16)
                if r == 0:
                    sp.dma_start(const[:, :], a["ident"]).then_inc(const_loaded, 16)
                    sp.dma_start(cols[:, :], a["cols"]).then_inc(const_loaded, 16)

        @block.scalar
        def _(act):
            ready = lambda eng, r: eng.wait_ge(x_loaded[r], 16)
            norm.act_sums(act, 0, ready)
            norm.act_root(act, 0)
            act.wait_ge(const_loaded, 32)
            for rb in range(1, RB):
                norm.act_sums(act, rb, ready)
                norm.act_root(act, rb)
                norm.act_hi(act, rb - 1)
            norm.act_hi(act, RB - 1)

        @block.vector
        def _(dve):
            chain = Count(dve, step)
            norm.dve_invert(dve, 0, chain)
            norm.dve_scale(dve, 0)
            dve.wait_ge(const_loaded, 32)
            for rb in range(1, RB):
                norm.dve_invert(dve, rb, chain)
                norm.dve_lo(dve, rb - 1)
                norm.dve_scale(dve, rb)
            norm.dve_lo(dve, RB - 1)

        @block.tensor
        def _(pe):
            pe.wait_ge(const_loaded, 32)
            for rb in range(RB):
                norm.pe_turn(pe, rb)


def split_spans(rb):
    a = rb * RBW
    n = min(PROMPT - a, RBW)
    return (0, n), (n, RBW - n)


def project(nc, a, o, cols, hT, bank):
    with ExitStack() as ctx:
        sb = lambda n, s, d=F32: ctx.enter_context(nc.sbuf_tensor(n, s, d))
        sem = Sems(nc, ctx, "")
        raw = sb("w_raw", [P, 4, PIECE])
        w_hi = sb("w_hi", [P, 8, PIECE], F32R)
        w_lo = sb("w_lo", [P, 8, PIECE], F32R)
        tout = sb("t_out", [P, 2, ROWS])
        nout = sb("n_out", [P, 2, 512])
        sig = sb("sig", [P, 512])
        wa = sb("w_decay", [RANK, 2 * P])
        glr = sb("glr", [RANK, ROWS])
        m_ext = sb("m_ext", [H, EXT])
        lf_ext = sb("lf_ext", [H, EXT])
        g_f = sb("g_f", [H, ROWS])
        g_u = sb("g_u", [P, ROWS])
        keep = sb("keep", [H, ROWS])
        raw_loaded = [sem(f"raw_loaded{s}") for s in range(4)]
        t_stored = [sem(f"t_stored{s}") for s in range(2)]
        n_stored = [sem(f"n_stored{s}") for s in range(2)]
        small_loaded, rows_stored = sem("small_loaded"), sem("rows_stored")
        piece_hi = sem("piece_hi")
        piece_split = sem("piece_split")
        sums_ready = sem("sums_ready")
        sums_taken = sem("sums_taken")
        n_filled, mo_filled = sem("n_filled"), sem("mo_filled")
        sig_ready = sem("sig_ready")
        step, act_step = sem("gate_step"), sem("gate_act_step")
        z_ready, z_taken = sem("z_ready"), sem("z_taken")
        abs_ready, ln_ready, decay_ready = sem("abs_ready"), sem("ln_ready"), sem("decay_ready")
        expo_ready, rows_ready = sem("expo_ready"), sem("rows_ready")
        RAW_CREDIT, BANK_CREDIT = 4, 6
        T_USES = 3 * (1 + NT)
        NUNIT = ((0, 3, 4, 5), (6, 7, 1, 2))
        block = ctx.enter_context(nc.Block())

        def n_unit(n):
            t, q = divmod(n - PC_N, 4)
            return NUNIT[t % 2][q]

        def n_before(n):
            t, q = divmod(n - PC_N, 4)
            return ((3 * NT, 0, 0, 0), (0, 3, T_USES, 0))[t][q] if t < 2 else T_USES + (t - 1) * RT

        @block.sync
        def _(sp):
            for n in range(4):
                sp.wait_ge(piece_split, n + 1)
                sp.dma_start(raw[:, n, :], a["w"][n]).then_inc(raw_loaded[n], 16)
            sp.dma_start(wa[:, :], a["w_decay"]).then_inc(small_loaded, 16)
            sp.dma_start(keep[:, :], a["keep"]).then_inc(small_loaded, 16)
            with sp.Fori(0, NT // 4) as four:
                i = 4 * four
                for q in range(4):
                    sp.wait_ge(piece_split, i + (5 + q))
                    sp.dma_start(raw[:, q, :], a["w"][i + (4 + q)]).then_inc(raw_loaded[q], 16)
                    sp.wait_ge(sums_taken, 3 * i + (BANK_CREDIT + 3 * (q + 2)))
                    sp.dma_start(a["pT"][i + q], tout[:, q % 2, :]).then_inc(t_stored[q % 2], 16)

            def load(n):
                sp.wait_ge(piece_split, n + 1)
                sp.dma_start(raw[:, n % 4, :], a["w"][n]).then_inc(raw_loaded[n % 4], 16)

            load(NT + 4)
            for t in range(NN):
                if t < NN - 1:
                    for q in range(4):
                        load(PC_N + 4 * (t + 1) + q)
                if t == 1:
                    for j in range(2):
                        sp.wait_ge(decay_ready, j + 1)
                        sp.dma_start(a["pT"][NT + j], tout[:, j, :]).then_inc(t_stored[j], 16)
                if t == 2:
                    sp.wait_ge(rows_ready, 4)
                    for q, row in enumerate((g_f, g_u, lf_ext, keep, glr)):
                        sp.dma_start(a["rows"][:, q, :], row[0:H, 0:ROWS]).then_inc(rows_stored, 16)
                    sp.dma_start(o["mm"], m_ext[:, :]).then_inc(rows_stored, 16)
                for r in range(RT):
                    u = t * RT + r
                    if t < NN - 1:
                        sp.wait_ge(n_filled, u + 1)
                    else:
                        sp.wait_ge(mo_filled, r + 1)
                    sp.dma_start(a["pN"][t, r], nout[:, u % 2, :]).then_inc(n_stored[u % 2], 16)
            sp.wait_ge(rows_stored, 6 * 16)
            for s in range(2):
                sp.wait_ge(t_stored[s], 16 * (NT // 2 + 2))
                sp.wait_ge(n_stored[s], 16 * (NN * RT // 2))

        @block.gpsimd
        def _(pool):
            pool.sem_inc(piece_split, RAW_CREDIT)
            pool.sem_inc(sums_taken, BANK_CREDIT)
            pool.sem_inc(t_stored[0], 16)
            pool.sem_inc(t_stored[1], 16)

            def lo(n, unit, slot):
                pool.wait_ge(piece_hi, n + 1)
                pool.tensor_tensor(w_lo[:, unit, :], raw[:, slot, :], w_hi[:, unit, :].bitcast(F32),
                                   ALU.subtract).then_inc(piece_split, 1)

            lo(0, 7, 0)
            lo(1, 0, 1)
            with pool.Fori(0, NT // 4) as four:
                i = 4 * four
                for q in range(4):
                    lo(i + (q + 2), (q + 1) % 2, (q + 2) % 4)
            for n in range(PC_N + 1, PC_OUT):
                lo(n, n_unit(n), n % 4)

        @block.scalar
        def _(act):
            def hi(n, unit, slot, loads):
                act.wait_ge(raw_loaded[slot], loads)
                act.activation(w_hi[:, unit, :], raw[:, slot, :], ACT.Copy).then_inc(piece_hi, 1)

            hi(0, 7, 0, 16)
            hi(1, 0, 1, 16)
            with act.Fori(0, NT // 4) as four:
                i = 4 * four
                for q in range(4):
                    act.wait_ge(sums_ready, 3 * i + 3 * (q + 1))
                    hi(i + (q + 2), (q + 1) % 2, (q + 2) % 4, 4 * i + 16 * ((q + 2) // 4 + 1))

            def hi_n(n):
                if n_before(n):
                    act.wait_ge(sums_ready, n_before(n))
                hi(n, n_unit(n), n % 4, 16 * (n // 4 + 1))

            for n in range(PC_N + 1, PC_N + 4):
                hi_n(n)
            for j in range(2):
                act.wait_ge(abs_ready, j + 1)
                act.activation(g_u[:, :], g_u[:, :], ACT.Exp).then_inc(act_step, 1)
                act.wait_ge(act_step, 2 * j + 1)
                act.activation(g_u[:, :], g_u[:, :], ACT.Ln, bias=1.0).then_inc(ln_ready, 1)
                act.sem_inc(act_step, 1)
            for n in range(PC_N + 4, PC_N + 8):
                hi_n(n)
            act.wait_ge(abs_ready, 3)
            act.activation(g_u[0:H, :], g_u[0:H, :], ACT.Exp).then_inc(act_step, 1)
            act.wait_ge(act_step, 5)
            act.activation(g_u[0:H, :], g_u[0:H, :], ACT.Ln, bias=1.0).then_inc(ln_ready, 1)
            act.wait_ge(expo_ready, 1)
            act.activation(lf_ext[:, 0:ROWS], lf_ext[:, 0:ROWS], ACT.Exp).then_inc(rows_ready, 1)
            act.activation(keep[:, :], keep[:, :], ACT.Exp).then_inc(rows_ready, 1)
            m_p, m_s = ext_views(m_ext)
            act.activation(glr[0:H, 0:PROMPT], m_p, ACT.Exp, scale=-1.0).then_inc(rows_ready, 1)
            act.activation(streams(glr[0:H, PROMPT:ROWS]), m_s, ACT.Exp, scale=-1.0).then_inc(rows_ready, 1)
            for n in range(PC_N + 8, PC_N + 12):
                hi_n(n)
            for n in range(PC_N + 12, PC_OUT):
                hi_n(n)
            for t in (2, 3):
                for r in range(RT):
                    u = t * RT + r
                    act.wait_ge(sums_ready, T_USES + u + 1)
                    psum = bank[(T_USES + u) % 6][:, :]
                    if t == 2:
                        act.wait_ge(n_filled, u)
                        act.activation(sig[:, :], psum, ACT.Sigmoid).then_inc(sig_ready, 1)
                    else:
                        act.wait_ge(n_stored[u % 2], 16 * (u // 2))
                        act.activation(nout[:, u % 2, :], psum, ACT.Sigmoid).then_inc(mo_filled, 1)

        @block.tensor
        def _(pe):
            def tile_t(n, unit, use, use_bank, width=P):
                pe.wait_ge(piece_split, n + (RAW_CREDIT + 1))
                for rb in range(RB):
                    pe.wait_ge(sums_taken, use + (rb + 1))
                    for k in range(KD):
                        w = [x[:, unit, k * P:(k + 1) * P] for x in (w_hi, w_lo)]
                        x = [h[:, k, rb * RBW:(rb + 1) * RBW] for h in hT]
                        mm = mm3(pe, bank[use_bank + rb][:, 0:RBW], w, x, k == 0, k == KD - 1)
                    if rb < RB - 1:
                        mm.then_inc(sums_ready, 1)
                mm.then_inc(sums_ready, 1)

            tile_t(0, 7, 0, 0)
            with pe.Fori(0, NT // 4) as four:
                i = 4 * four
                for q in range(4):
                    tile_t(i + (q + 1), q % 2, 3 * i + 3 * (q + 1), 3 * ((q + 1) % 2))
            pe.wait_ge(small_loaded, 32)
            pe.wait_ge(sums_taken, BANK_CREDIT + RB)
            for j in range(2):
                for rb in range(RB):
                    n = j * RB + rb
                    if n >= 2:
                        pe.wait_ge(z_taken, n - 1)
                    pe.matmul(bank[6 + n % 2][:, 0:RBW], wa[:, j * P:(j + 1) * P],
                              glr[:, rb * RBW:(rb + 1) * RBW], start=True, stop=True).then_inc(z_ready, 1)
            for t in range(NN):
                units = NUNIT[t % 2]
                for r in range(RT):
                    u = t * RT + r
                    if u < 6:
                        pe.wait_ge(sums_taken, T_USES + u + 1)
                    elif u - 6 < (NN - 1) * RT:
                        pe.wait_ge(n_filled, u - 5)
                    else:
                        pe.wait_ge(mo_filled, u - 5 - (NN - 1) * RT)
                    for k in range(KD):
                        if r == 0 and k % 2 == 0:
                            pe.wait_ge(piece_split, PC_N + 4 * t + k // 2 + 1 + RAW_CREDIT)
                        x = [h[:, k, r * P:(r + 1) * P] for h in hT]
                        w = [y[:, units[k // 2], (k % 2) * 512:(k % 2 + 1) * 512] for y in (w_hi, w_lo)]
                        mm = mm3(pe, bank[(T_USES + u) % 6], x, w, k == 0, k == KD - 1)
                    mm.then_inc(sums_ready, 1)

        @block.vector
        def _(dve):
            chain = Count(dve, step)
            bf = cols[0:H, K_BG:K_BG + 1]
            bi = cols[32:32 + H, K_BG:K_BG + 1]
            i_p, i_s = ext_views(m_ext)
            lf_p, lf_s = ext_views(lf_ext)
            dve.memset(m_ext[:, :], 0.0).then_inc(step, 1)
            dve.memset(lf_ext[:, :], NEG).then_inc(step, 1)
            chain.n = 2
            dve.wait_ge(step, 2)
            for rb in range(RB):
                dve.wait_ge(sums_ready, rb + 1)
                s = slice(rb * RBW, (rb + 1) * RBW)
                (p0, pn), (s0, sn) = split_spans(rb)
                dve.tensor_scalar(g_f[:, s], bank[rb][0:H, 0:RBW], bf, None, ALU.add)
                dve.tensor_scalar(i_p[:, rb * RBW:rb * RBW + pn], bank[rb][32:32 + H, 0:pn], bi, None, ALU.add)
                if sn:
                    dve.tensor_scalar(i_s, streams(bank[rb][32:32 + H, s0:s0 + sn]), bi, None, ALU.add)
                dve.tensor_copy(glr[:, s], bank[rb][64:64 + RANK, 0:RBW]).then_inc(sums_taken, 1)
            with dve.Fori(0, NT // 4) as four:
                i = 4 * four
                for q in range(4):
                    dve.wait_ge(t_stored[q % 2], 8 * i + 16 * (q // 2 + 1))
                    for rb in range(RB):
                        dve.wait_ge(sums_ready, 3 * i + (3 * (q + 1) + rb + 1))
                        dve.tensor_copy(tout[:, q % 2, rb * RBW:(rb + 1) * RBW],
                                        bank[3 * ((q + 1) % 2) + rb][:, 0:RBW]).then_inc(sums_taken, 1)
            for j in range(2):
                dve.wait_ge(t_stored[j], 16 * (NT // 2 + 1))
                for rb in range(RB):
                    n = j * RB + rb
                    dve.wait_ge(z_ready, n + 1)
                    dve.tensor_scalar(tout[:, j, rb * RBW:(rb + 1) * RBW], bank[6 + n % 2][:, 0:RBW],
                                      cols[:, K_BA + j:K_BA + j + 1], None, ALU.add).then_inc(z_taken, 1)
                dve.wait_ge(z_taken, RB * (j + 1))
                z = tout[:, j, :]
                if j:
                    dve.wait_ge(decay_ready, j)
                dve.scalar_tensor_tensor(out=g_u[:, :], in0=z, scalar=-1.0, in1=z, op0=ALU.mult,
                                         op1=ALU.min).then_inc(abs_ready, 1)
                dve.wait_ge(ln_ready, j + 1)
                dve.scalar_tensor_tensor(out=z, in0=z, scalar=0.0, in1=g_u[:, :], op0=ALU.min,
                                         op1=ALU.subtract).then_inc(decay_ready, 1)

            def take(t):
                for r in range(RT):
                    u = t * RT + r
                    dve.wait_ge(sums_ready, T_USES + u + 1)
                    if u >= 2:
                        dve.wait_ge(n_stored[u % 2], 16 * (u // 2))
                    psum = bank[(T_USES + u) % 6][:, :]
                    if t < 2:
                        dve.tensor_copy(nout[:, u % 2, :], psum).then_inc(n_filled, 1)
                    else:
                        dve.wait_ge(sig_ready, r + 1)
                        dve.tensor_tensor(nout[:, u % 2, :], psum, sig[:, :], ALU.mult).then_inc(n_filled, 1)

            take(0)
            dve.wait_ge(small_loaded, 32)
            dve.wait_ge(decay_ready, 2)
            u4 = g_u[0:H, :]
            dve.scalar_tensor_tensor(out=u4, in0=g_f[:, :], scalar=-1.0, in1=g_f[:, :], op0=ALU.mult,
                                     op1=ALU.min).then_inc(abs_ready, 1)
            dve.wait_ge(ln_ready, 3)
            chain.link(dve.scalar_tensor_tensor(out=u4, in0=g_f[:, :], scalar=0.0, in1=u4, op0=ALU.min,
                                                op1=ALU.subtract))
            dve.tensor_copy(lf_p, u4[:, 0:PROMPT])
            dve.tensor_copy(lf_s, streams(u4[:, PROMPT:ROWS]))
            chain.link(dve.tensor_copy(first_slots(m_ext), cols[0:H, K_M0:K_M0 + NB]))
            chain.link(dve.tensor_tensor_scan(g_f[:, :], keep[:, :], u4, 0.0, ALU.mult, ALU.add))
            dve.tensor_tensor(u4[:, 0:PROMPT], i_p, g_f[:, 0:PROMPT], ALU.subtract)
            chain.link(dve.tensor_tensor(streams(u4[:, PROMPT:ROWS]), i_s, streams(g_f[:, PROMPT:ROWS]),
                                         ALU.subtract))
            chain.link(dve.tensor_tensor_scan(m_ext[:, :], lf_ext[:, :], m_ext[:, :], 0.0, ALU.add, ALU.max))
            dve.tensor_tensor(g_f[:, 0:PROMPT], g_f[:, 0:PROMPT], i_p, ALU.subtract)
            chain.link(dve.tensor_tensor(streams(g_f[:, PROMPT:ROWS]), streams(g_f[:, PROMPT:ROWS]), i_s,
                                         ALU.subtract))
            rp, rs = chunks(g_f[:, 0:PROMPT]), streams(g_f[:, PROMPT:ROWS])
            dve.tensor_tensor(chunks(lf_ext[:, 0:PROMPT]), rp,
                              chunks(m_ext[:, 0:PROMPT])[:, :, 0:1].to_broadcast([H, NC, P]), ALU.add)
            dve.tensor_tensor(streams(lf_ext[:, PROMPT:ROWS]), rs,
                              first_slots(m_ext).unsqueeze(2).to_broadcast([H, NB, LB]), ALU.add)
            dve.tensor_tensor(chunks(keep[:, 0:PROMPT]), chunks(u4[:, 0:PROMPT]),
                              rp[:, :, P - 1:P].to_broadcast([H, NC, P]), ALU.add)
            dve.tensor_tensor(streams(keep[:, PROMPT:ROWS]), streams(u4[:, PROMPT:ROWS]),
                              rs[:, :, LB - 1:LB].to_broadcast([H, NB, LB]), ALU.add).then_inc(expo_ready, 1)
            take(1)
            take(2)


def streams(ap):
    return ap.rearrange("h (b e) -> h b e", e=LB)


def chunks(ap):
    return ap.rearrange("h (c e) -> h c e", e=P)


def ext_views(ext):
    return (ext[0:H, 1:1 + PROMPT],
            ext[0:H, 1 + PROMPT:EXT].rearrange("h (b e) -> h b e", e=LB + 1)[:, :, 1:LB + 1])


def first_slots(ext):
    return ext[0:H, 1 + PROMPT:EXT].rearrange("h (b e) -> h b e", e=LB + 1)[:, :, 0]


def mix(nc, a, o, ident, x9, ssq, pb, bank, sample):
    NS = NB if sample else 1
    LS = LB if sample else P
    LV0 = 3 if sample else 0
    NL = LEVELS - LV0
    N = 1 if sample else NC
    SLOTS = min(N, 2)
    c0, c1 = (C_SHARED, N_CONST) if sample else (0, C_SAMPLE)
    nm = "s" if sample else "p"
    HP = P // 2
    E_B, E_LAST, E_LV = 0, 2 * P, 4 * P
    with ExitStack() as ctx:
        sb = lambda n, s, d=F32: ctx.enter_context(nc.sbuf_tensor(f"{nm}_{n}", s, d))
        sem = Sems(nc, ctx, f"{nm}_")
        const = sb("const", [P, c1 - c0])
        tin = sb("t_in", [P, SLOTS, NT + 2, P])
        rin = sb("r_in", [H, SLOTS, 5, P])
        wt = sb("wt", [P, SLOTS, H, P])
        wq = sb("wq", [P, SLOTS, H, P])
        nin = sb("n_in", [P, SLOTS, 3, 512])
        vin = sb("v_in", [P, SLOTS, H, VX])
        ex = sb("ex", [P, SLOTS, E_LV + NL * 2 * P])
        q8 = sb("q8", [P, SLOTS, 2, 2, P])
        qb = sb("qb", [P, SLOTS, 2 * P])
        qx = sb("qx", [P, SLOTS, NL, 2, 2, HP])
        kx = sb("kx", [P, SLOTS, NL + 2, 2 * P])
        qs = sb("qs", [P, SLOTS, H, P])
        dg = sb("dg", [H, NS, H])
        NCOL = 3 * H + NS * H
        col = sb("col", [P, SLOTS, NCOL])
        am = sb("am", [P, SLOTS, H, P])
        ksn = sb("ks", [P, SLOTS, H, DH])
        gsc = sb("gla_scores", [P, H, P])
        kdn = sb("k_decayed", [P, 2, P])
        S = sb("S", [P, NS, 2, DV])
        C = sb("C", [P, NS, H, VX])
        den = [sb(f"den{i}", [P, 2, 2, 1]) for i in range(3)]
        sq = sb("sq", [P, 2 * H, P])
        if sample:
            qm = {n: sb(f"{n}_masked", [P, k, NB * (P + LB)]) for n, k in (("qs", H), ("qb", 2))}
            vm = {"m": sb("mv_masked", [P, NB, H * VX]), "g": sb("gv_masked", [P, NB, 512])}
        front_in = [sem(f"front_in{s}") for s in range(SLOTS)]
        back_in = [sem(f"back_in{s}") for s in range(SLOTS)]
        const_in, state_in, state_out = sem("const_in"), sem("state_in"), sem("state_out")
        names = ("zeroed b_ready upper_ready lower_ready lv_exp q8_ready rmask_ready kx_ready qs_ready "
                 "dg_ready cols_ready cols_taken qk_ready kt_ready wt_ready am_ready ksn_ready qx_ready "
                 "kdt_ready kdn_ready lvl_ready lvl_taken lvl_seen num_ready den_step mlstm_done um_ready "
                 "um_taken o_ready o_squared sq_done o_taken ug_ready ug_taken qm_ready vm_ready")
        g = {n: sem(n) for n in names.split()}
        cs = lambda k, n: const[:, k - c0:k - c0 + n]
        ones4 = cs(C_ONE, P)[0:H, :]
        id4 = ident[0:H, 0:H]
        ZEROED = 6 + 2 * SLOTS + (2 if sample else 0)
        o_bank = lambda h: lvl_b[:, h % 2, (h // 2) * P:(h // 2 + 1) * P]
        half = lambda ap, h: ap[(h % 2) * DK:(h % 2 + 1) * DK]
        lvl_b, lvl_a, bankm = pb[0], pb[2], pb[3]
        num = lambda h: bankm[:, h // 2, (h % 2) * VX:(h % 2 + 1) * VX]
        COLS = 2 * VX
        UG = 3 * P
        groups = [(range(0, 4), lvl_a)] + ([(range(4, NL), lvl_b)] if NL > 4 else [])
        groups += [(range(NL, NL + 1), groups[len(groups) - 2][1] if len(groups) > 1 else lvl_b)]
        L = NL + 1
        um_bank = lambda b: pb[2 - b % 2]
        ug_out = lambda b, j: bank[6 + b % 2][:, j * P:(j + 1) * P] if sample else bankm[:, j, UG:UG + P]
        lowers = lambda ap, w: ap.rearrange("p (n w) -> p n w", w=2 * w)[:, :, 0:w]
        packed = lambda ap, w: ap.rearrange("p (n w) -> p n w", w=w)
        width = lambda n: P >> (n + LV0 + 1)
        block = ctx.enter_context(nc.Block())

        def pipeline(eng, front, step, back):
            front(0, 0)
            if N > 1:
                with eng.Fori(0, (N - 2) // 2) as two:
                    step(2 * two, 0)
                    step(2 * two + 1, 1)
                step(N - 2, 0)
                back(N - 1, 1)
            else:
                back(0, 0)

        def loads(sem_in, c, s, n):
            return 8 * n * (c + (2 if s == 0 else 1))

        def row0(c):
            return bass.ts(c + (NC if sample else 0), P)

        def tile_of(c):
            return c + (NC if sample else 0)

        @block.sync
        def _(sp):
            def front(c, s):
                r = row0(c)
                sp.dma_start(tin[:, s, :, :], a["pT"][:, :, r].rearrange("t p f -> p t f")).then_inc(front_in[s], 16)
                sp.dma_start(rin[:, s, :, :], a["rows"][:, :, r]).then_inc(front_in[s], 16)
                for dst, q in ((wt, 0), (wq, 2)):
                    sp.dma_start(dst[:, s, :, :], a["rows"][:, q, r].unsqueeze(0).to_broadcast([P, H, P]))\
                      .then_inc(front_in[s], 16)

            def back(c, s):
                t = tile_of(c)
                sp.dma_start(vin[:, s, :, 0:DH], a["pN"][1, t].rearrange("p (h v) -> p h v", h=H)).then_inc(back_in[s], 16)
                sp.dma_start(nin[:, s, 0, :], a["pN"][0, t]).then_inc(back_in[s], 16)
                sp.dma_start(nin[:, s, 1:3, :], a["pN"][2:4, t].rearrange("q p v -> p q v")).then_inc(back_in[s], 16)

            front(0, 0)
            sp.dma_start(const[:, :], a["const"][:, c0:c1]).then_inc(const_in, 16)
            sp.wait_ge(g["zeroed"], ZEROED)
            if sample:
                sp.dma_start(S[:, :, :, :], a["s_gla"]).then_inc(state_in, 16)
                sp.dma_start(C[:, :, :, :], a["s_mc"]).then_inc(state_in, 16)
            back(0, 0)
            if not sample:
                front(1, 1)
                back(1, 1)
                with sp.Fori(0, (N - 2) // 2) as two:
                    for s in range(2):
                        c = 2 * two + s
                        for n in ("am_ready", "qs_ready", "q8_ready", "kt_ready"):
                            sp.wait_ge(g[n], c + 1)
                        front(c + 2, s)
                        sp.wait_ge(g["ug_taken"], 2 * c + 2 + 2)
                        back(c + 2, s)
            sp.wait_ge(g["ug_taken"], 2 * NS * N + 2)
            sp.dma_start(o["q_gla"] if sample else o["p_gla"].unsqueeze(1), S[:, :, :, :]).then_inc(state_out, 16)
            sp.dma_start(o["q_mc"] if sample else o["p_mc"].unsqueeze(1), C[:, :, :, :]).then_inc(state_out, 16)
            sp.wait_ge(state_out, 32)

        @block.gpsimd
        def _(pool):
            pool.sem_inc(g["lvl_taken"], 1)
            pool.sem_inc(g["ug_taken"], 2)
            pool.sem_inc(g["o_taken"], 1)
            for s in range(SLOTS):
                pool.memset(kx[:, s, :, :], 0.0).then_inc(g["zeroed"], 1)
                pool.memset(q8[:, s, :, :, :], 0.0).then_inc(g["zeroed"], 1)
            for x in (S[:, :, :, :], C[:, :, :, :], gsc[:, :, :]):
                pool.memset(x, 0.0).then_inc(g["zeroed"], 1)
            pool.memset(vin[:, :, :, DH:VX], 1.0).then_inc(g["zeroed"], 1)
            for x in qm.values() if sample else ():
                pool.memset(x[:, :, :], 0.0).then_inc(g["zeroed"], 1)
            pool.memset(sq[:, :, :], 0.0).then_inc(g["zeroed"], 1)
            pool.memset(den[0][:, :, :, :], 0.0).then_inc(g["zeroed"], 1)
            pool.wait_ge(const_in, 16)
            pool.wait_ge(g["zeroed"], ZEROED)

            def front(c, s):
                e = ex[:, s, :]
                pool.wait_ge(g["b_ready"], c + 1)
                for n in range(NL):
                    w = width(n)
                    b = e[:, E_B:E_B + 2 * P].rearrange("p (n w) -> p n w", w=2 * w)
                    at = E_LV + n * 2 * P + P
                    pool.tensor_tensor(packed(e[:, at:at + P], w), b[:, :, w - 1:w].to_broadcast([P, P // w, w]),
                                       b[:, :, 0:w], ALU.subtract)
                b = e[:, E_B:E_B + 2 * P].rearrange("p (n w) -> p n w", w=LS)
                pool.tensor_tensor(packed(e[:, E_LAST:E_LAST + 2 * P], LS),
                                   b[:, :, LS - 1:LS].to_broadcast([P, 2 * P // LS, LS]), b,
                                   ALU.subtract).then_inc(g["lower_ready"], 1)
                caus = cs(C_CAUSB if sample else C_CAUS, P)
                pool.tensor_tensor(wt[:, s, :, :], wt[:, s, :, :], caus.unsqueeze(1).to_broadcast([P, H, P]),
                                   ALU.add).then_inc(g["rmask_ready"], 1)
                pool.wait_ge(g["lv_exp"], c + 1)
                k = tin[:, s, 2:4, :].rearrange("p j f -> p (j f)")
                for n in range(NL):
                    w = width(n)
                    at = E_LV + n * 2 * P + P
                    pool.tensor_tensor(lowers(kx[:, s, n, :], w), packed(e[:, at:at + P], w), lowers(k, w), ALU.mult)
                pool.tensor_tensor(kx[:, s, NL, :], e[:, E_LAST:E_LAST + 2 * P], k, ALU.mult)\
                    .then_inc(g["kx_ready"], 1)
                pool.tensor_tensor(qs[:, s, :, :], tin[:, s, 4:8, :], wq[:, s, :, :], ALU.mult)\
                    .then_inc(g["qs_ready"], 1)

            pipeline(pool, front, lambda c, s: front(c + 1, 1 - s), lambda c, s: None)

        @block.scalar
        def _(act):
            def front_queries(c, s):
                act.wait_ge(g["b_ready"], c + 1)
                act.activation(kx[:, s, NL + 1, :], tin[:, s, 2:4, :].rearrange("p j f -> p (j f)"), ACT.Copy)
                for e in range(2):
                    q = act.activation(q8[e * DK:(e + 1) * DK, s, :, e, :], tin[e * DK:(e + 1) * DK, s, 0:2, :],
                                       ACT.Copy, scale=QSCALE)
                q.then_inc(g["q8_ready"], 1)

            def front_powers(c, s):
                act.wait_ge(g["upper_ready"], c + 1)
                act.wait_ge(g["lower_ready"], c + 1)
                act.activation(ex[:, s, :], ex[:, s, :], ACT.Exp, scale=1.0 / TAU).then_inc(g["lv_exp"], 1)

            def front_weights(c, s):
                act.wait_ge(g["rmask_ready"], c + 1)
                act.wait_ge(g["cols_taken"], c + 1)
                for h in range(H):
                    w = act.activation(wt[:, s, h, :], wt[:, s, h, :], ACT.Exp, bias=col[:, s, h:h + 1])
                w.then_inc(g["wt_ready"], 1)

            def front_keys(c, s):
                act.wait_ge(g["kt_ready"], c + 1)
                for h in range(H):
                    k = act.activation(ksn[:, s, h, :], bank[3][:, h * P:(h + 1) * P], ACT.Copy,
                                       scale=col[:, s, H + h:H + h + 1])
                k.then_inc(g["ksn_ready"], 1)

            def back_decayed(c, s):
                act.wait_ge(g["kdt_ready"], c + 1)
                act.activation(kdn[:, :, :], bank[3][:, 0:2 * P].rearrange("p (j f) -> p j f", j=2), ACT.Copy).then_inc(g["kdn_ready"], 1)

            def back_squares(c, s):
                act.wait_ge(g["mlstm_done"], c + 1)
                for h in range(H):
                    act.activation(sq[:, H + h, :], x9[:, tile_of(c), 512 + h * P:512 + (h + 1) * P], ACT.Square,
                                   accum_out=ssq[:, tile_of(c), H + h:H + h + 1])
                act.wait_ge(g["o_ready"], c + 1)
                for h in range(H):
                    q = act.activation(sq[:, h, :], o_bank(h), ACT.Square,
                                       accum_out=ssq[:, tile_of(c), h:h + 1])
                q.then_inc(g["o_squared"], 1)

            def front(c, s):
                front_queries(c, s)
                front_powers(c, s)
                front_weights(c, s)
                front_keys(c, s)

            def step(c, s):
                front_queries(c + 1, 1 - s)
                back_decayed(c, s)
                front_powers(c + 1, 1 - s)
                front_weights(c + 1, 1 - s)
                back_squares(c, s)
                front_keys(c + 1, 1 - s)

            def back(c, s):
                back_decayed(c, s)
                back_squares(c, s)

            act.wait_ge(g["zeroed"], ZEROED)
            pipeline(act, front, step, back)

        @block.tensor
        def _(pe):
            def front_scores(c, s):
                pe.wait_ge(front_in[s], loads(front_in, c, s, 4))
                for h in range(H):
                    mm = pe.matmul(bank[2][:, h * P:(h + 1) * P], tin[:, s, 8 + h, :], tin[:, s, 4 + h, :],
                                   start=True, stop=True)
                mm.then_inc(g["qk_ready"], 1)

            def front_rows(c, s):
                pe.wait_ge(g["dg_ready"], c + 1)
                for n, q in enumerate((1, 3, 4)):
                    pe.matmul(bank[6][:, COLS + H * n:COLS + H * (n + 1)], rin[:, s, q, :], id4, start=True, stop=True)
                pe.matmul(bank[6][:, COLS + 3 * H:COLS + NCOL], ones4, dg[:, :, :].rearrange("p b h -> p (b h)"),
                          start=True, stop=True).then_inc(g["cols_ready"], 1)

            def front_turn(c, s):
                for h in range(H):
                    mm = pe.transpose(bank[3][:, h * P:(h + 1) * P], tin[:, s, 8 + h, :], ident)
                mm.then_inc(g["kt_ready"], 1)

            def front(c, s):
                front_scores(c, s)
                front_rows(c, s)
                front_turn(c, s)

            def scores(c, s, n):
                levels, out = groups[n]
                for v in levels:
                    for j in range(2):
                        at = (v - levels[0]) * HP
                        dst = out[:, j, :].rearrange("p (e x) -> p e x", e=2)
                        if v < NL:
                            mm = pe.matmul(dst[:, :, at:at + HP], kx[:, s, v, j * P:(j + 1) * P], qx[:, s, v, j, :, :],
                                           start=True, stop=True)
                        else:
                            mm = pe.matmul(dst[:, :, 0:P], kx[:, s, NL + 1, j * P:(j + 1) * P], q8[:, s, j, :, :],
                                           start=True, stop=True)
                mm.then_inc(g["lvl_ready"], 1)

            def back_first(c, s):
                pe.wait_ge(g["kx_ready"], c + 1)
                pe.wait_ge(g["qx_ready"], c + 1)
                scores(c, s, 0)

            def back_rest(c, s, front_rows_done, following=None):
                pe.wait_ge(g["ksn_ready"], c + 1)
                for j in range(2):
                    mm = pe.transpose(bank[3][:, j * P:(j + 1) * P], kx[:, s, NL, j * P:(j + 1) * P], ident)
                mm.then_inc(g["kdt_ready"], 1)
                pe.wait_ge(g["o_taken"], c + 1)
                scores(c, s, 1)
                if len(groups) > 2:
                    pe.wait_ge(g["lvl_taken"], L * c + 4 + 1)
                    scores(c, s, 2)
                pe.wait_ge(g["cols_taken"], front_rows_done)
                pe.wait_ge(g["ug_taken"], 2 * c + 2)
                pe.wait_ge(g["am_ready"], c + 1)
                pe.wait_ge(g["qs_ready"], c + 1)
                pe.wait_ge(back_in[s], loads(back_in, c, s, 3))
                if sample:
                    pe.wait_ge(g["qm_ready"], 1)
                for h in range(H):
                    for b in range(NS):
                        q = qm["qs"][:, h, b * P:(b + 1) * P] if sample else qs[:, s, h, :]
                        pe.matmul(num(h), q, C[:, b, h, :], start=(b == 0), stop=False)
                    mm = pe.matmul(num(h), am[:, s, h, :], vin[:, s, h, :], start=False, stop=True)
                mm.then_inc(g["num_ready"], 1)
                pe.wait_ge(g["lvl_taken"], L * c + L + 1)
                pe.wait_ge(g["kdn_ready"], c + 1)
                if sample:
                    pe.wait_ge(g["vm_ready"], 1)
                for b in range(NS):
                    if b >= 2:
                        pe.wait_ge(g["um_taken"], b - 1)
                    for h in range(H):
                        v = vm["m"][:, b, h * VX:(h + 1) * VX] if sample else vin[:, s, h, :]
                        mm = pe.matmul(um_bank(b)[:, h // 2, (h % 2) * VX:(h % 2 + 1) * VX], ksn[:, s, h, :], v,
                                       start=True, stop=True)
                    mm.then_inc(g["um_ready"], 1)
                if following:
                    following()
                if sample:
                    pe.wait_ge(g["qm_ready"], 2)
                for h in range(H):
                    j = h // 2
                    for b in range(NS):
                        q = half(qm["qb"], h)[:, j, b * P:(b + 1) * P] if sample else half(qb, h)[:, s, j * P:(j + 1) * P]
                        pe.matmul(o_bank(h), q, half(S, h)[:, b, j, :], start=(b == 0), stop=False)
                    mm = pe.matmul(o_bank(h), gsc[:, h, :], nin[:, s, 0, h * P:(h + 1) * P],
                                   start=False, stop=True)
                mm.then_inc(g["o_ready"], 1)
                pe.wait_ge(g["mlstm_done"], c + 1)
                if sample:
                    pe.wait_ge(g["vm_ready"], 2)
                for b in range(NS):
                    if b >= 2:
                        pe.wait_ge(g["ug_taken"], 2 * (b - 1) + 2)
                    for h in range(H):
                        j = h // 2
                        v = vm["g"][:, b, h * P:(h + 1) * P] if sample else nin[:, s, 0, h * P:(h + 1) * P]
                        mm = pe.matmul(half(ug_out(b, j), h), kdn[:, j, (h % 2) * DK:(h % 2 + 1) * DK], v,
                                       start=True, stop=True)
                    mm.then_inc(g["ug_ready"], 1)

            def step(c, s):
                pe.wait_ge(g["am_ready"], c + 1)
                front_scores(c + 1, 1 - s)
                back_first(c, s)
                front_rows(c + 1, 1 - s)
                back_rest(c, s, c + 2, lambda: front_turn(c + 1, 1 - s))

            def back(c, s):
                back_first(c, s)
                back_rest(c, s, c + 1)

            pe.wait_ge(g["zeroed"], ZEROED)
            if sample:
                pe.wait_ge(state_in, 32)
            pipeline(pe, front, step, back)

        @block.vector
        def _(dve):
            def front_exponents(c, s, first=False):
                dve.wait_ge(front_in[s], loads(front_in, c, s, 4))
                if not first:
                    dve.wait_ge(g["ug_taken"], 2 * c)
                e = ex[:, s, :]
                keep = cs(C_KEEPB if sample else C_KEEP, 2 * P)
                la = tin[:, s, NT:NT + 2, :].rearrange("p j f -> p (j f)")
                dve.tensor_tensor_scan(e[:, E_B:E_B + 2 * P], keep, la, 0.0, ALU.mult, ALU.add).then_inc(g["b_ready"], 1)
                dec = rin[:, s, 2, :].rearrange("p (b f) -> p b f", f=LS)[:, :, LS - 1:LS]
                dve.tensor_tensor(dg[:, :, :], dec.to_broadcast([H, NS, H]),
                                  id4.unsqueeze(1).to_broadcast([H, NS, H]), ALU.mult).then_inc(g["dg_ready"], 1)
                dve.wait_ge(g["b_ready"], c + 1)
                for n in range(NL):
                    w = width(n)
                    b = e[:, E_B:E_B + 2 * P].rearrange("p (n w) -> p n w", w=2 * w)
                    at = E_LV + n * 2 * P
                    u = dve.tensor_tensor(packed(e[:, at:at + P], w), b[:, :, w:2 * w],
                                          b[:, :, w - 1:w].to_broadcast([P, P // w, w]), ALU.subtract)
                u.then_inc(g["upper_ready"], 1)
                dve.wait_ge(g["cols_ready"], c + 1)
                ps = bank[6][:, COLS:COLS + NCOL]
                dve.tensor_copy(col[:, s, 0:H], ps[:, 0:H])
                dve.tensor_scalar(col[:, s, H:2 * H], ps[:, H:2 * H], KSCALE, None, ALU.mult)
                dve.tensor_copy(col[:, s, 2 * H:NCOL], ps[:, 2 * H:NCOL]).then_inc(g["cols_taken"], 1)

            def front_weights(c, s):
                dve.wait_ge(g["qk_ready"], c + 1)
                dve.wait_ge(g["wt_ready"], c + 1)
                dve.scalar_tensor_tensor(out=am[:, s, :, :].rearrange("p h f -> p (h f)"), in0=bank[2], scalar=KSCALE,
                                         in1=wt[:, s, :, :].rearrange("p h f -> p (h f)"), op0=ALU.mult,
                                         op1=ALU.mult).then_inc(g["am_ready"], 1)

            def front_queries(c, s):
                dve.wait_ge(g["lv_exp"], c + 1)
                dve.wait_ge(g["q8_ready"], c + 1)
                for e in range(2):
                    r = slice(e * DK, (e + 1) * DK)
                    dve.tensor_tensor(qb[r, s, :].rearrange("p (j f) -> p j f", j=2),
                                      ex[r, s, E_B:E_B + 2 * P].rearrange("p (j f) -> p j f", j=2),
                                      q8[r, s, :, e, :], ALU.mult)
                for n in range(NL):
                    w = width(n)
                    at = E_LV + n * 2 * P
                    x = ex[:, s, at:at + P].rearrange("p (j n w) -> p j n w", j=2, w=w)
                    q = dve.tensor_tensor(
                        qx[:, s, n, :, :, :].rearrange("p j e (n w) -> p j e n w", w=w),
                        x.unsqueeze(2).to_broadcast([P, 2, 2, HP // w, w]),
                        q8[:, s, :, :, :].rearrange("p j e (n w) -> p j e n w", w=2 * w)[:, :, :, :, w:2 * w],
                        ALU.mult)
                q.then_inc(g["qx_ready"], 1)

            def back_scores(c, s):
                for gi, (levels, src) in enumerate(groups):
                    for v in levels:
                        if v == levels[0]:
                            dve.wait_ge(g["lvl_ready"], len(groups) * c + (gi + 1))
                        dve.wait_ge(g["lvl_taken"], L * c + (v + 1))
                        dve.sem_inc(g["lvl_seen"], 1)
                        x = src[:, :, :].rearrange("p j (e x) -> p (j e) x", x=2 * P)
                        if v < NL:
                            w = width(v)
                            at = (v - levels[0]) * HP
                            mask = cs(C_LV + (v + LV0) * HP, HP)
                            cp = dve.copy_predicated(
                                gsc[:, :, :].rearrange("p h (n w) -> p h n w", w=2 * w)[:, :, :, w:2 * w],
                                packed(mask, w).bitcast(I32).unsqueeze(1).to_broadcast([P, H, HP // w, w]),
                                x[:, :, at:at + HP].rearrange("p h (n w) -> p h n w", w=w))
                        else:
                            cp = dve.copy_predicated(gsc[:, :, :],
                                                     cs(C_DIAG, P).bitcast(I32).unsqueeze(1).to_broadcast([P, H, P]),
                                                     x[:, :, 0:P])
                        cp.then_inc(g["lvl_taken"], 1)

            def back_mlstm(c, s):
                dve.wait_ge(g["num_ready"], c + 1)
                d = bankm[:, :, 0:2 * VX].rearrange("p a (b v) -> p a b v", v=VX)[:, :, :, DH:VX]
                z = lambda n: dve.wait_ge(g["den_step"], 4 * c + n)
                dve.tensor_copy(den[1][:, :, :, :], d).then_inc(g["den_step"], 1)
                z(1)
                dve.scalar_tensor_tensor(out=den[0][:, :, :, :], in0=den[1][:, :, :, :], scalar=-1.0,
                                         in1=den[1][:, :, :, :], op0=ALU.mult, op1=ALU.max).then_inc(g["den_step"], 1)
                z(2)
                dve.tensor_tensor(den[1][:, :, :, :], den[0][:, :, :, :],
                                  col[:, s, 2 * H:3 * H].rearrange("p (a b) -> p a b", b=2).unsqueeze(3),
                                  ALU.max).then_inc(g["den_step"], 1)
                z(3)
                dve.reciprocal(den[2][:, :, :, :], den[1][:, :, :, :]).then_inc(g["den_step"], 1)
                z(4)
                for h in range(H):
                    m = dve.scalar_tensor_tensor(out=x9[:, tile_of(c), 512 + h * P:512 + (h + 1) * P],
                                                 in0=num(h)[:, 0:DH], scalar=den[2][:, h // 2, h % 2, :],
                                                 in1=nin[:, s, 2, h * P:(h + 1) * P], op0=ALU.mult, op1=ALU.mult)
                m.then_inc(g["mlstm_done"], 1)

            def back_memory(c, s):
                for b in range(NS):
                    dve.wait_ge(g["um_ready"], NS * c + (b + 1))
                    for h in range(H):
                        u = dve.scalar_tensor_tensor(
                            out=C[:, b, h, :], in0=C[:, b, h, :],
                            scalar=col[:, s, 3 * H + b * H + h:3 * H + b * H + h + 1],
                            in1=um_bank(b)[:, h // 2, (h % 2) * VX:(h % 2 + 1) * VX], op0=ALU.mult, op1=ALU.add)
                    u.then_inc(g["um_taken"], 1)

            def back_gla(c, s):
                dve.wait_ge(g["o_squared"], c + 1)
                dve.tensor_tensor(x9[:, tile_of(c), 0:512].rearrange("p (j e f) -> p j e f", j=2, e=2),
                                  lvl_b[:, :, 0:2 * P].rearrange("p e (j f) -> p j e f", j=2),
                                  nin[:, s, 1, :].rearrange("p (j e f) -> p j e f", j=2, e=2),
                                  ALU.mult).then_inc(g["o_taken"], 1)
                for b in range(NS):
                    dve.wait_ge(g["ug_ready"], NS * c + (b + 1))
                    for j in range(2):
                        last = E_B + j * P + (b + 1) * LS - 1
                        dve.scalar_tensor_tensor(out=S[:, b, j, :], in0=S[:, b, j, :],
                                                 scalar=ex[:, s, last:last + 1], in1=ug_out(b, j), op0=ALU.mult,
                                                 op1=ALU.add).then_inc(g["ug_taken"], 1)

            def masks(c, s):
                bm = cs(C_BM, NB).unsqueeze(2)
                dve.wait_ge(g["qs_ready"], 1)
                dve.wait_ge(g["qx_ready"], 1)
                dve.tensor_copy(stream_blocks(qm["qs"], H),
                                qs[:, s, :, :].rearrange("p h (b e) -> p h b e", e=LB)).then_inc(g["qm_ready"], 1)
                dve.tensor_copy(stream_blocks(qm["qb"], 2),
                                qb[:, s, :].rearrange("p (j b e) -> p j b e", j=2, e=LB)).then_inc(g["qm_ready"], 1)
                dve.wait_ge(back_in[s], loads(back_in, c, s, 3))
                for n, v, k in (("m", vin[:, s, :, :].rearrange("p h v -> p (h v)"), H * VX), ("g", nin[:, s, 0, :], 512)):
                    dve.tensor_tensor(vm[n][:, :, :], v.unsqueeze(1).to_broadcast([P, NB, k]),
                                      bm.to_broadcast([P, NB, k]), ALU.mult).then_inc(g["vm_ready"], 1)

            def front(c, s):
                front_exponents(c, s, first=True)
                front_weights(c, s)
                front_queries(c, s)
                if sample:
                    masks(c, s)

            def step(c, s):
                front_exponents(c + 1, 1 - s)
                back_scores(c, s)
                back_mlstm(c, s)
                front_weights(c + 1, 1 - s)
                back_memory(c, s)
                front_queries(c + 1, 1 - s)
                back_gla(c, s)

            def back(c, s):
                back_scores(c, s)
                back_mlstm(c, s)
                back_memory(c, s)
                back_gla(c, s)

            dve.wait_ge(const_in, 16)
            dve.wait_ge(g["zeroed"], ZEROED)
            if sample:
                dve.wait_ge(state_in, 32)
            pipeline(dve, front, step, back)


def stream_blocks(qm, n):
    return qm[:, 0:n, :].rearrange("p h (b e) -> p h b e", e=P + LB)[:, :, :, 0:LB]


def output(nc, a, x9, ssq, cols, hT, ident, bank):
    with ExitStack() as ctx:
        sb = lambda n, s, d=F32: ctx.enter_context(nc.sbuf_tensor(f"o_{n}", s, d))
        sem = Sems(nc, ctx, "o_")
        raw = sb("w_raw", [P, 2, PIECE])
        w_hi, w_lo = sb("w_hi", [P, KD, PIECE], F32R), sb("w_lo", [P, KD, PIECE], F32R)
        inv, rstd = sb("inv", [P, RT, 2 * H]), sb("rstd", [P, RT, 2 * H])
        x_loaded = [sem(f"x_loaded{r}") for r in range(RT)]
        raw_loaded = [sem(f"raw_loaded{s}") for s in range(2)]
        piece_hi, piece_split = sem("piece_hi"), sem("piece_split")
        inverted, rooted, scaled = sem("inverted"), sem("rooted"), sem("scaled")
        sums_ready, added, step = sem("sums_ready"), sem("added"), sem("step")
        turn = Turn(nc, sem, "mix", hT, ident, cols[:, K_MIX:K_MIX + KD], bank[6:8],
                    lambda rb, j, k: x9[:, rb * JR + j, k * P:(k + 1) * P])
        norm = Norm(nc, ctx, sem, "norm2", x9, hT, ident, cols[:, K_N2:K_N2 + KD], bank[6:8])
        block = ctx.enter_context(nc.Block())

        @block.sync
        def _(sp):
            for n in range(KD):
                if n >= 2:
                    sp.wait_ge(piece_split, n - 1)
                sp.dma_start(raw[:, n % 2, :], a["w"][PC_OUT + n]).then_inc(raw_loaded[n % 2], 16)
            for r in range(RT):
                if r % JR == 0:
                    sp.wait_ge(turn.turned, KD * (r // JR + 1))
                sp.dma_start(x9[:, r, :], a["x"][r]).then_inc(x_loaded[r], 16)

        @block.gpsimd
        def _(pool):
            for n in range(KD):
                pool.wait_ge(piece_hi, n + 1)
                pool.tensor_tensor(w_lo[:, n, :], raw[:, n % 2, :], w_hi[:, n, :].bitcast(F32),
                                   ALU.subtract).then_inc(piece_split, 1)

        @block.scalar
        def _(act):
            def weights(n):
                act.wait_ge(raw_loaded[n % 2], 16 * (n // 2 + 1))
                act.activation(w_hi[:, n, :], raw[:, n % 2, :], ACT.Copy).then_inc(piece_hi, 1)

            weights(0)
            weights(1)
            act.wait_ge(inverted, 1)
            act.activation(rstd[:, :, :], inv[:, :, :], ACT.Sqrt).then_inc(rooted, 1)
            for n in range(2, KD):
                weights(n)
                turn.act_hi(act, 0, (n - 2, n - 1) if n > 6 else (n - 2,))
            turn.act_hi(act, 0, (KD - 1,))
            turn.act_hi(act, 1)
            ready = lambda eng, r: eng.wait_ge(added, 2 * r + 2)
            norm.act_sums(act, 0, ready)
            norm.act_root(act, 0)
            turn.act_hi(act, 2)
            for rb in range(1, RB):
                norm.act_sums(act, rb, ready)
                norm.act_hi(act, rb - 1)
                norm.act_root(act, rb)
            norm.act_hi(act, RB - 1)

        @block.tensor
        def _(pe):
            def rows(rb):
                pe.wait_ge(turn.lo_done, KD * (rb + 1))
                for u in range(2 * JR * rb, 2 * JR * (rb + 1)):
                    r, n = divmod(u, 2)
                    if u >= 6:
                        pe.wait_ge(added, u - 5)
                    for k in range(KD):
                        if u == 0:
                            pe.wait_ge(piece_split, k + 1)
                        x = [h[:, k, r * P:(r + 1) * P] for h in hT]
                        w = [y[:, k, n * 512:(n + 1) * 512] for y in (w_hi, w_lo)]
                        mm = mm3(pe, bank[u % 6], x, w, k == 0, k == KD - 1)
                    mm.then_inc(sums_ready, 1)

            for rb in range(2):
                pe.wait_ge(scaled, JR * (rb + 1))
                turn.pe_turn(pe, rb)
            rows(0)
            pe.wait_ge(scaled, RT)
            turn.pe_turn(pe, 2)
            rows(1)
            pe.wait_ge(turn.lo_done, KD * RB)
            norm.pe_turn(pe, 0)
            rows(2)
            norm.pe_turn(pe, 1)
            norm.pe_turn(pe, 2)

        @block.vector
        def _(dve):
            chain = Count(dve, step)
            chain.link(dve.tensor_scalar(ssq[:, :, :], ssq[:, :, :], 1.0 / P, EPS, ALU.mult, ALU.add))
            dve.reciprocal(inv[:, :, :], ssq[:, :, :]).then_inc(inverted, 1)
            dve.wait_ge(rooted, 1)

            def scale(rb):
                for r in range(rb * JR, rb * JR + JR):
                    x = x9[:, r, :].rearrange("p (h v) -> p h v", v=DV)
                    dve.tensor_tensor(x, x, rstd[:, r, :].unsqueeze(2).to_broadcast([P, 2 * H, DV]),
                                      ALU.mult).then_inc(scaled, 1)

            def add(rb):
                for u in range(2 * JR * rb, 2 * JR * (rb + 1)):
                    r, n = divmod(u, 2)
                    if n == 0:
                        dve.wait_ge(x_loaded[r], 16)
                    dve.wait_ge(sums_ready, u + 1)
                    x = x9[:, r, n * 512:(n + 1) * 512]
                    dve.tensor_tensor(x, bank[u % 6], x, ALU.add).then_inc(added, 1)

            scale(0)
            scale(1)
            turn.dve_lo(dve, 0)
            scale(2)
            turn.dve_lo(dve, 1)
            add(0)
            norm.dve_invert(dve, 0, chain)
            norm.dve_scale(dve, 0)
            turn.dve_lo(dve, 2)
            add(1)
            norm.dve_invert(dve, 1, chain)
            norm.dve_lo(dve, 0)
            norm.dve_scale(dve, 1)
            add(2)
            norm.dve_invert(dve, 2, chain)
            norm.dve_lo(dve, 1)
            norm.dve_scale(dve, 2)
            norm.dve_lo(dve, 2)


def ffn(nc, a, o, x9, hT, bank):
    NP = NF // 2
    SX = LB + 2
    with ExitStack() as ctx:
        sb = lambda n, s, d=F32: ctx.enter_context(nc.sbuf_tensor(f"f_{n}", s, d))
        sem = Sems(nc, ctx, "f_")
        raw = sb("w_raw", [P, 3, PIECE])
        w_hi, w_lo = sb("w_hi", [P, 6, PIECE], F32R), sb("w_lo", [P, 6, PIECE], F32R)
        a_hi, a_lo = sb("a_hi", [P, 2, ROWS], F32R), sb("a_lo", [P, 2, ROWS], F32R)
        gp = sb("gate_prompt", [P, 2 + PROMPT])
        gs = sb("gate_sample", [P, NB, SX])
        gc = sb("gate_conv", [P, 2, RBW])
        cache, taps = sb("cache", [P, NF, 2 * NB]), sb("taps", [P, NF, 4])
        tails = sb("tails", [P, NF, 2 + 2 * NB])
        raw_loaded = [sem(f"raw_loaded{s}") for s in range(3)]
        small_in, tails_out = sem("small_in"), sem("tails_out")
        piece_hi, piece_split = sem("piece_hi"), sem("piece_split")
        up_ready = sem("up_ready")
        g_out = sem("g_out")
        conv_step, conv_done = sem("conv_step"), sem("conv_done")
        gelu_done, u_taken = sem("gelu_done"), sem("u_taken")
        ahi_done, a_split = sem("ahi_done"), sem("a_split")
        down_ready, down_added = sem("down_ready"), sem("down_added")
        tails_done, zeroed = sem("tails_done"), sem("zeroed")
        RAW, UP, CONV, GC, DOWN = 3, 3, 3, 2, 2
        NG = 5
        def splits_after(n, last):
            return () if last and n > 1 else ((0,), (1,), (), (2,), (3,), (4, 5))[n]

        block = ctx.enter_context(nc.Block())

        def pairs(eng, body):
            with eng.Fori(0, NP - 1) as i:
                body(i, False)
            body(NP - 1, True)

        @block.sync
        def _(sp):
            def load(m, slot):
                sp.wait_ge(piece_split, m + 1)
                sp.dma_start(raw[:, slot, :], a["w"][m + PC_FFN]).then_inc(raw_loaded[slot], 16)

            sp.dma_start(cache[:, :, :], a["cache"]).then_inc(small_in, 16)
            sp.dma_start(taps[:, :, :], a["taps"]).then_inc(small_in, 16)
            for m in range(4):
                load(m, m % 3)

            def body(i, last):
                for k in range(2 if last else 6):
                    load(6 * i + (4 + k), (4 + k) % 3)

            pairs(sp, body)
            sp.wait_ge(tails_done, 2 * NF)
            sp.dma_start(o["conv"], tails[:, :, :]).then_inc(tails_out, 16)
            sp.wait_ge(tails_out, 16)

        @block.gpsimd
        def _(pool):
            for s, n in ((piece_split, RAW), (u_taken, UP), (conv_done, CONV), (a_split, GC), (down_added, DOWN)):
                pool.sem_inc(s, n)
            pool.memset(gp[:, 0:2], 0.0).then_inc(zeroed, 1)

            def lo(m, unit, slot):
                pool.wait_ge(piece_hi, m + 1)
                pool.tensor_tensor(w_lo[:, unit, :], raw[:, slot, :], w_hi[:, unit, :].bitcast(F32),
                                   ALU.subtract).then_inc(piece_split, 1)

            for m in range(4):
                lo(m, m, m % 3)

            def body(i, last):
                for n in range(2 * RB):
                    q, rb = divmod(n, RB)
                    s = slice(rb * RBW, (rb + 1) * RBW)
                    pool.wait_ge(ahi_done, 6 * i + (n + 1))
                    pool.tensor_tensor(a_lo[:, q, s], gc[:, n % 2, :], a_hi[:, q, s].bitcast(F32),
                                       ALU.subtract).then_inc(a_split, 1)
                    for k in splits_after(n, last):
                        lo(6 * i + (4 + k), (4 + k) % 6, (4 + k) % 3)

            pairs(pool, body)

        @block.scalar
        def _(act):
            def hi(m, unit, slot, loads):
                act.wait_ge(raw_loaded[slot], loads)
                act.activation(w_hi[:, unit, :], raw[:, slot, :], ACT.Copy).then_inc(piece_hi, 1)

            for m in range(4):
                hi(m, m, m % 3, 16 * (m // 3 + 1))
            act.wait_ge(small_in, 32)

            def body(i, last):
                for n in range(2 * RB):
                    q, rb = divmod(n, RB)
                    f = 2 * i + q
                    act.wait_ge(up_ready, 12 * i + (2 * n + 1))
                    act.wait_ge(conv_done, 6 * i + (3 * q + (2 if rb == 0 else 3)))
                    g = bank[2 * rb]
                    if rb < 2:
                        act.activation(gp[:, 2 + rb * RBW:2 + (rb + 1) * RBW], g[:, 0:RBW], ACT.Copy).then_inc(g_out, 1)
                    else:
                        np_ = PROMPT - 2 * RBW
                        act.activation(gp[:, 2 + 2 * RBW:2 + PROMPT], g[:, 0:np_], ACT.Copy).then_inc(g_out, 1)
                        act.activation(gs[:, :, 2:SX], streams(g[:, np_:RBW]), ACT.Copy).then_inc(g_out, 1)
                        act.activation(gs[:, :, 0:2], cache[:, f, :].rearrange("p (b e) -> p b e", e=2),
                                       ACT.Copy).then_inc(g_out, 1)
                        act.wait_ge(g_out, 2 * NG * i + NG * (q + 1))
                        act.activation(tails[:, f, 0:2], gp[:, PROMPT:PROMPT + 2], ACT.Copy).then_inc(tails_done, 1)
                        act.activation(tails[:, f, 2:2 + 2 * NB].rearrange("p (b e) -> p b e", e=2),
                                       gs[:, :, LB:SX], ACT.Copy).then_inc(tails_done, 1)
                    act.wait_ge(conv_done, 6 * i + (n + 1 + CONV))
                    act.activation(gc[:, n % 2, :], gc[:, n % 2, :], ACT.Gelu_apprx_tanh).then_inc(gelu_done, 1)
                    act.wait_ge(u_taken, 6 * i + (n + 1 + UP))
                    act.activation(a_hi[:, q, rb * RBW:(rb + 1) * RBW], gc[:, n % 2, :], ACT.Copy).then_inc(ahi_done, 1)
                    for k in splits_after(n, last):
                        if k < 2:
                            act.wait_ge(up_ready, 12 * i + 1)
                        else:
                            act.wait_ge(up_ready, 12 * i + (5, 6, 11, 12)[k - 2])
                        hi(6 * i + (4 + k), (4 + k) % 6, (4 + k) % 3, 32 * i + 16 * ((4 + k) // 3 + 1))

            pairs(act, body)

        @block.tensor
        def _(pe):
            with pe.Fori(0, NP) as i:
                for q in range(2):
                    for rb in range(RB):
                        n = 3 * q + rb
                        pe.wait_ge(u_taken, 6 * i + (n + 1))
                        for m in range(2):
                            if rb == 0:
                                pe.wait_ge(piece_split, 6 * i + (2 * q + m + 1 + RAW))
                            for k in range(KD):
                                w = [y[:, 2 * q + m, k * P:(k + 1) * P] for y in (w_hi, w_lo)]
                                x = [h[:, k, rb * RBW:(rb + 1) * RBW] for h in hT]
                                mm = mm3(pe, bank[2 * rb + m][:, 0:RBW], w, x, k == 0, k == KD - 1)
                            mm.then_inc(up_ready, 1)
                pe.wait_ge(piece_split, 6 * i + (6 + RAW))
                for r in range(RT):
                    if r % JR == 0:
                        pe.wait_ge(a_split, 6 * i + (RB + r // JR + 1 + GC))
                    for half in range(2):
                        pe.wait_ge(down_added, 2 * RT * i + (2 * r + half + 1))
                        for q in range(2):
                            x = [y[:, q, r * P:(r + 1) * P] for y in (a_hi, a_lo)]
                            w = [y[:, 4 + q, half * 512:(half + 1) * 512] for y in (w_hi, w_lo)]
                            mm = mm3(pe, bank[6 + half], x, w, q == 0, q == 1)
                        mm.then_inc(down_ready, 1)

        @block.vector
        def _(dve):
            dve.wait_ge(small_in, 32)
            dve.wait_ge(zeroed, 1)
            with dve.Fori(0, NP) as i:
                chain = Count(dve, conv_step, 12 * i)
                for n in range(2 * RB):
                    q, rb = divmod(n, RB)
                    tap = [taps[:, 2 * i + q, j:j + 1] for j in range(4)]
                    np_ = min(RBW, PROMPT - rb * RBW)
                    out = gc[:, n % 2, :]
                    parts = [(lambda j: gp[:, rb * RBW + j:rb * RBW + j + np_], out[:, 0:np_])]
                    if np_ < RBW:
                        parts.append((lambda j: gs[:, :, j:j + LB], streams(out[:, np_:RBW])))
                    dve.wait_ge(g_out, 2 * NG * i + (NG * q + (rb + 1 if rb < 2 else NG)))
                    dve.wait_ge(a_split, 6 * i + (n + 1))
                    for src, dst in parts:
                        ins = dve.tensor_scalar(dst, src(2), tap[2], tap[3], ALU.mult, ALU.add)
                    chain.link(ins)
                    for src, dst in parts:
                        ins = dve.scalar_tensor_tensor(out=dst, in0=src(1), scalar=tap[1], in1=dst, op0=ALU.mult,
                                                       op1=ALU.add)
                    chain.link(ins)
                    for src, dst in parts:
                        ins = dve.scalar_tensor_tensor(out=dst, in0=src(0), scalar=tap[0], in1=dst, op0=ALU.mult,
                                                       op1=ALU.add)
                    ins.then_inc(conv_done, 1)
                    dve.wait_ge(gelu_done, 6 * i + (n + 1))
                    dve.wait_ge(up_ready, 12 * i + (2 * n + 2))
                    dve.tensor_tensor(out, bank[2 * rb + 1][:, 0:RBW], out, ALU.mult).then_inc(u_taken, 1)
                assert chain.n == 12
                for u in range(2 * RT):
                    r, half = divmod(u, 2)
                    x = x9[:, r, half * 512:(half + 1) * 512]
                    dve.wait_ge(down_ready, 2 * RT * i + (u + 1))
                    dve.tensor_tensor(x, bank[6 + half], x, ALU.add).then_inc(down_added, 1)

    with ExitStack() as ctx:
        sb = lambda n, s, d=F32: ctx.enter_context(nc.sbuf_tensor(f"e_{n}", s, d))
        sem = Sems(nc, ctx, "e_")
        SLOTS = 3
        gain = sb("gain", [P, D])
        yt, sq = sb("y", [P, SLOTS, D]), sb("sq", [P, D])
        ss, inv, rstd = sb("ss", [P, RT]), sb("inv", [P, RT]), sb("rstd", [P, RT])
        gain_in = sem("gain_in")
        stored = [sem(f"stored{s}") for s in range(SLOTS)]
        summed, shifted, inverted, rooted, y_ready = (sem(n) for n in "summed shifted inverted rooted y_ready".split())
        block = ctx.enter_context(nc.Block())

        @block.sync
        def _(sp):
            sp.dma_start(gain[:, :], a["norm_f"].to_broadcast([P, D])).then_inc(gain_in, 16)
            for r in range(RT):
                sp.wait_ge(y_ready, r + 1)
                sp.dma_start(o["y"][r], yt[:, r % SLOTS, :]).then_inc(stored[r % SLOTS], 16)
            for s in range(SLOTS):
                sp.wait_ge(stored[s], 16 * (RT // SLOTS))

        @block.scalar
        def _(act):
            for r in range(RT):
                if r:
                    act.wait_ge(summed, r)
                act.activation(sq[:, :], x9[:, r, :], ACT.Square, accum_out=ss[:, r:r + 1]).then_inc(summed, 1)
                if r % JR == JR - 1:
                    act.wait_ge(inverted, r // JR + 1)
                    s = slice(r - JR + 1, r + 1)
                    act.activation(rstd[:, s], inv[:, s], ACT.Sqrt).then_inc(rooted, 1)

        @block.vector
        def _(dve):
            dve.wait_ge(gain_in, 16)
            for r in range(RT):
                if r % JR == 0:
                    s = slice(r, r + JR)
                    dve.wait_ge(summed, r + JR)
                    dve.tensor_scalar(ss[:, s], ss[:, s], 1.0 / D, EPS, ALU.mult, ALU.add).then_inc(shifted, 1)
                    dve.wait_ge(shifted, r // JR + 1)
                    dve.reciprocal(inv[:, s], ss[:, s]).then_inc(inverted, 1)
                    dve.wait_ge(rooted, r // JR + 1)
                if r >= SLOTS:
                    dve.wait_ge(stored[r % SLOTS], 16 * (r // SLOTS))
                dve.scalar_tensor_tensor(out=yt[:, r % SLOTS, :], in0=x9[:, r, :], scalar=rstd[:, r:r + 1],
                                         in1=gain[:, :], op0=ALU.mult, op1=ALU.mult).then_inc(y_ready, 1)


def kernel(**inputs):
    import numpy as np
    import concourse.bacc as _bacc
    from concourse.bass_utils import run_bass_kernel_spmd as _run

    g = {n: np.asarray(v) for n, v in inputs.items()}
    f32 = np.float32
    w_in, w_out = g["w_in"][0], g["w_out"][0]
    QK, V, W = H * DK, H * DV, H * DH
    ofs = np.cumsum([0, QK, QK, V, V, RANK, W, W, W, W, H, H])
    gq, gk, gv, gr, gl, mq, mk, mv, mo, mi, mf = [w_in[:, ofs[i]:ofs[i + 1]] for i in range(11)]

    def piece(w):
        n = w.shape[1]
        per = PIECE // n
        return w.reshape(KD // per, per, P, n).transpose(0, 2, 1, 3).reshape(KD // per, P, PIECE)

    gate = np.zeros((D, P), f32)
    gate[:, 0:H], gate[:, 32:32 + H], gate[:, 64:64 + RANK] = mf, mi, gl
    trans = np.concatenate([gq, gk, mq, mk], axis=1)
    pieces = [piece(gate)]
    pieces += [piece(trans[:, t * P:(t + 1) * P]) for t in range(NT)]
    pieces += [piece(w) for w in (gv, mv, gr, mo)]
    pieces += [w_out.reshape(KD, P, D)]
    wg, wu, wd = g["w_g"][0], g["w_u"][0], g["w_d"][0].reshape(NF, P, D)
    up = [(piece(wg[:, f * P:(f + 1) * P]), piece(wu[:, f * P:(f + 1) * P])) for f in range(NF)]
    pieces += [*up[0], *up[1]]
    for i in range(0, NF, 2):
        pieces += [wd[i:i + 2]]
        if i + 2 < NF:
            pieces += [*up[i + 2], *up[i + 3]]
    ins = {"w": np.concatenate(pieces)}
    assert ins["w"].shape == (N_PIECES, P, PIECE)
    ins["x"] = np.concatenate([g["x_prompt"][0], g["x_sample"].reshape(-1, D)]).reshape(RT, P, D)
    cols = np.zeros((P, N_COL), f32)
    cols[:, K_N1:K_N1 + KD] = g["norm1"][0].reshape(KD, P).T
    cols[:, K_N2:K_N2 + KD] = g["norm2"][0].reshape(KD, P).T
    cols[:, K_MIX:K_MIX + H] = g["gla_norm"][0][:, None]
    cols[:, K_MIX + H:K_MIX + KD] = g["m_norm"][0][:, None]
    cols[:, K_BA:K_BA + 2] = g["b_gla_a"][0].reshape(2, P).T
    cols[0:H, K_BG], cols[32:32 + H, K_BG] = g["b_m_f"][0], g["b_m_i"][0]
    cols[0:H, K_M0:K_M0 + NB] = g["state_mlstm_m"][0].T
    ins["cols"] = cols
    ins["w_decay"] = g["w_gla_a"][0]
    keep = np.ones((H, ROWS), f32)
    keep[:, 0:PROMPT:P] = 0
    keep[:, PROMPT::LB] = 0
    ins["keep"] = keep
    ins["ident"] = np.eye(P, dtype=f32)
    s, t = np.arange(P)[:, None], np.arange(P)[None, :]
    const = np.zeros((P, N_CONST), f32)
    for lv in range(LEVELS):
        w = P >> (lv + 1)
        second = np.arange(P).reshape(-1, 2, w)[:, 1].reshape(1, -1)
        const[:, C_LV + lv * P // 2:C_LV + (lv + 1) * P // 2] = (s // (2 * w) == second // (2 * w)) & (s % (2 * w) < w)
    const[:, C_DIAG:C_DIAG + P] = s == t
    const[:, C_CAUS:C_CAUS + P] = np.where(s <= t, 0.0, NEG)
    const[:, C_CAUSB:C_CAUSB + P] = np.where((s <= t) & (s // LB == t // LB), 0.0, NEG)
    const[:, C_KEEP:C_KEEP + 2 * P] = np.arange(2 * P) % P != 0
    const[:, C_KEEPB:C_KEEPB + 2 * P] = np.arange(2 * P) % LB != 0
    const[:, C_BM:C_BM + NB] = s // LB == np.arange(NB)[None, :]
    const[:, C_ONE:C_ONE + P] = 1.0
    ins["const"] = const
    ins["cache"] = g["cache_ffn_conv"][0].reshape(NB * 2, NF, P).transpose(2, 1, 0)
    taps = np.concatenate([g["conv_w"][0], g["conv_b"]])
    ins["taps"] = taps.reshape(4, NF, P).transpose(2, 1, 0)
    ins["norm_f"] = g["norm_f"].reshape(1, D)
    ins["s_gla"] = g["state_gla"][0].reshape(NB, 2, 2, DK, DV).transpose(2, 3, 0, 1, 4).reshape(P, NB, 2, DV)
    ins["s_mc"] = np.concatenate([g["state_mlstm_C"][0].transpose(2, 0, 1, 3),
                                  g["state_mlstm_n"][0].transpose(2, 0, 1)[..., None]], axis=3)
    outs = {"y": (RT, P, D), "p_gla": (P, 2, DV), "p_mc": (P, H, VX), "mm": (H, EXT), "conv": (P, NF, 2 + 2 * NB),
            "q_gla": (P, NB, 2, DV), "q_mc": (P, NB, H, VX)}
    scratch = {"pT": (NT + 2, P, ROWS), "pN": (NN, RT, P, 512), "rows": (H, 5, ROWS)}
    nc = _bacc.Bacc("TRN2", target_bir_lowering=False, num_devices=1)
    ins = {n: np.ascontiguousarray(v) for n, v in ins.items()}
    a = {n: nc.dram_tensor(f"in_{n}", v.shape, F32, kind="ExternalInput").ap() for n, v in ins.items()}
    a.update({n: nc.dram_tensor(f"scratch_{n}", s, F32, kind="Internal").ap() for n, s in scratch.items()})
    o = {n: nc.dram_tensor(f"out_{n}", s, F32, kind="ExternalOutput").ap() for n, s in outs.items()}
    build(nc, a, o)
    r = _run(nc, [{f"in_{n}": v for n, v in ins.items()}], core_ids=[0]).results[0]
    y = r["out_y"].reshape(ROWS, D)
    mm = r["out_mm"]
    conv = r["out_conv"].transpose(2, 1, 0).reshape(2 + 2 * NB, F)

    def gla(s):
        return s.reshape(2, DK, -1, 2, DV).transpose(2, 3, 0, 1, 4).reshape(1, -1, H, DK, DV)

    def mc(s):
        s = s.reshape(P, -1, H, VX)
        return s[..., 0:DH].transpose(1, 2, 0, 3)[None], s[..., DH].transpose(1, 2, 0)[None]

    p_c, p_n = mc(r["out_p_mc"])
    q_c, q_n = mc(r["out_q_mc"])
    q_m = mm[:, 1 + PROMPT:].reshape(H, NB, LB + 1)[:, :, LB].T
    res = (y[0:PROMPT][None], y[PROMPT:].reshape(NB, LB, D),
           gla(r["out_p_gla"]), p_c, p_n, mm[:, PROMPT].reshape(1, 1, H), conv[0:2].reshape(1, 1, 2, F),
           gla(r["out_q_gla"]), q_c, q_n, q_m.reshape(1, NB, H), conv[2:].reshape(1, NB, 2, F))
    return tuple(np.ascontiguousarray(v) for v in res)
```

```python
from contextlib import ExitStack

import concourse.bass as bass
from concourse import mybir

F32 = mybir.dt.float32
F32R = mybir.dt.float32r
I32 = mybir.dt.int32
ALU = mybir.AluOpType
ACT = mybir.ActivationFunctionType
AX = mybir.AxisListType

P = 128
D = 1024
KD = D // P
PROMPT = 1024
NB, LB = 8, 16
ROWS = PROMPT + NB * LB
RT = ROWS // P
NC = PROMPT // P
RBW = 384
RB = ROWS // RBW
JR = RBW // P
EPS = 1e-6
H = 4
DK, DV, DH = 64, 128, 128
VX = DH + 1
RANK = 16
TAU = 16.0
F = 2816
NF = F // P
QSCALE = DK ** -0.5
KSCALE = DH ** -0.5
NT = 12
NN = 4
LEVELS = 7
PIECE = D
PC_GATE, PC_T, PC_N = 0, 1, 1 + NT
PC_OUT = PC_N + 4 * NN
PC_FFN = PC_OUT + KD
N_PIECES = PC_FFN + 3 * NF
EXT = 1 + PROMPT + NB * (LB + 1)
NEG = -1.0e30
C_CAUS = 0
C_KEEP = C_CAUS + P
C_LV = C_KEEP + 2 * P
C_DIAG = C_LV + LEVELS * P // 2
C_ONE = C_DIAG + P
C_SAMPLE = C_ONE + P
C_CAUSB = C_SAMPLE
C_KEEPB = C_CAUSB + P
C_PARITY = C_KEEPB + 2 * P
N_CONST = C_PARITY + 2
K_N1, K_N2, K_MIX, K_BA, K_BG = 0, 8, 16, 24, 26
K_M0 = 27
N_COL = K_M0 + NB


class Count:

    def __init__(self, eng, sem, base=0):
        self.eng, self.sem, self.base, self.n = eng, sem, base, 0

    def link(self, ins):
        ins.then_inc(self.sem, 1)
        self.n += 1
        self.eng.wait_ge(self.sem, self.base + self.n)


class Sems:

    def __init__(self, nc, ctx, prefix):
        self.nc, self.prefix, self.taken = nc, prefix, []
        ctx.callback(self.clear)

    def __call__(self, name):
        self.taken.append(self.nc.alloc_semaphore(name=self.prefix + name))
        return self.taken[-1]

    def clear(self):
        self.nc.clear_and_free_semaphores(self.taken)
        self.nc.all_engine_barrier()


def mm3(pe, out, stat, mov, start, stop):
    pe.matmul(out, stat[0], mov[0], start=start, stop=False)
    pe.matmul(out, stat[0], mov[1], start=False, stop=False)
    return pe.matmul(out, stat[1], mov[0], start=False, stop=stop)


class Turn:

    def __init__(self, nc, sem, name, hT, ident, gain, banks, source, spread=None, eight=None):
        self.spread, self.eight = spread, eight
        self.hT, self.ident, self.gain, self.banks, self.source = hT, ident, gain, banks, source
        self.nb = len(banks)
        self.turned, self.hi_done, self.lo_done = (sem(f"{name}_{n}") for n in ("turned", "hi", "lo"))

    def bank_of(self, rb, k):
        return self.eight[k] if rb == self.spread else self.banks[(rb * KD + k) % self.nb]

    def pe_turn(self, pe, rb, ks=range(KD)):
        for k in ks:
            n = rb * KD + k
            if rb == self.spread:
                if rb and k == 0:
                    pe.wait_ge(self.lo_done, n)
            elif n >= self.nb:
                pe.wait_ge(self.lo_done, n - self.nb + 1)
            for j in range(JR):
                t = pe.transpose(self.bank_of(rb, k)[:, j * P:(j + 1) * P], self.source(rb, j, k), self.ident)
            t.then_inc(self.turned, 1)

    def act_hi(self, act, rb, ks=range(KD)):
        for k in ks:
            n = rb * KD + k
            act.wait_ge(self.turned, n + 1)
            act.activation(self.hT[0][:, k, rb * RBW:(rb + 1) * RBW], self.bank_of(rb, k)[:, 0:RBW], ACT.Copy,
                           scale=self.gain[:, k:k + 1]).then_inc(self.hi_done, 1)

    def dve_lo(self, dve, rb, ks=range(KD)):
        for k in ks:
            n = rb * KD + k
            s = slice(rb * RBW, (rb + 1) * RBW)
            dve.wait_ge(self.hi_done, n + 1)
            dve.scalar_tensor_tensor(out=self.hT[1][:, k, s], in0=self.bank_of(rb, k)[:, 0:RBW],
                                     scalar=self.gain[:, k:k + 1], in1=self.hT[0][:, k, s].bitcast(F32),
                                     op0=ALU.mult, op1=ALU.subtract).then_inc(self.lo_done, 1)


class Norm(Turn):

    def __init__(self, nc, ctx, sem, name, rows, scaled, squares, hT, ident, gain, banks, **spread):
        sb = lambda n, s: ctx.enter_context(nc.sbuf_tensor(f"{name}_{n}", s, F32))
        self.rows, self.scaled_rows, self.squares = rows, scaled, squares
        self.ss = sb("sumsq", [P, RT])
        self.inv = sb("inv", [P, RT])
        self.rstd = sb("rstd", [P, RT])
        self.summed, self.inverted, self.rooted, self.scaled = (
            sem(f"{name}_{n}") for n in ("summed", "inverted", "rooted", "scaled"))
        super().__init__(nc, sem, name, hT, ident, gain, banks,
                         lambda rb, j, k: scaled(rb * JR + j)[:, k * P:(k + 1) * P], **spread)

    def pe_turn(self, pe, rb, ks=range(KD)):
        if ks[0] == 0:
            pe.wait_ge(self.scaled, rb * JR + JR)
        super().pe_turn(pe, rb, ks)

    def act_sums(self, act, rb, ready, js=range(JR)):
        for r in (rb * JR + j for j in js):
            ready(act, r)
            if r:
                act.wait_ge(self.summed, r)
            act.activation(self.squares, self.rows(r), ACT.Square,
                           accum_out=self.ss[:, r:r + 1]).then_inc(self.summed, 1)

    def act_root(self, act, rb):
        act.wait_ge(self.inverted, rb + 1)
        s = slice(rb * JR, rb * JR + JR)
        act.activation(self.rstd[:, s], self.inv[:, s], ACT.Sqrt).then_inc(self.rooted, 1)

    def dve_invert(self, dve, rb, chain):
        s = slice(rb * JR, rb * JR + JR)
        dve.wait_ge(self.summed, rb * JR + JR)
        chain.link(dve.tensor_scalar(self.ss[:, s], self.ss[:, s], 1.0 / D, EPS, ALU.mult, ALU.add))
        dve.reciprocal(self.inv[:, s], self.ss[:, s]).then_inc(self.inverted, 1)

    def dve_scale(self, dve, rb):
        dve.wait_ge(self.rooted, rb + 1)
        if rb:
            dve.wait_ge(self.turned, rb * KD)
        for j in range(JR):
            r = rb * JR + j
            dve.tensor_scalar(self.scaled_rows(r), self.rows(r), self.rstd[:, r:r + 1], None,
                              ALU.mult).then_inc(self.scaled, 1)


def build(nc, a, o):
    with ExitStack() as top:
        sb = lambda n, s, d=F32: top.enter_context(nc.sbuf_tensor(n, s, d))
        pb = [top.enter_context(nc.psum_tensor(f"bank{2 * i}", [P, 2, 512], F32)) for i in range(4)]
        bank = [pb[i // 2][:, i % 2, :] for i in range(8)]
        const = sb("ident", [P, P])
        cols = sb("cols", [P, N_COL])
        ident = const[:, :]

        def halves(ctx, name):
            return [ctx.enter_context(nc.sbuf_tensor(f"{name}_{n}", [P, KD, ROWS], F32R)) for n in ("hi", "lo")]

        with ExitStack() as ctx:
            hT = halves(ctx, "h1T")
            project(nc, a, o, const, cols, hT, bank)
        x9, ssq = sb("x9", [P, RT, D]), sb("ssq", [P, RT, 2 * H])
        mix(nc, a, o, ident, x9, ssq, pb, bank)
        hT = halves(top, "h2T")
        raw = sb("w_raw2", [P, 4, PIECE])
        output(nc, a, x9, ssq, cols, hT, ident, bank, raw)
        ffn(nc, a, o, x9, hT, bank, raw)


def split_spans(rb):
    a = rb * RBW
    n = min(PROMPT - a, RBW)
    return (0, n), (n, RBW - n)


def project(nc, a, o, const, cols, hT, bank):
    with ExitStack() as ctx:
        sb = lambda n, s, d=F32: ctx.enter_context(nc.sbuf_tensor(n, s, d))
        sem = Sems(nc, ctx, "")
        raw = sb("w_raw", [P, 4, PIECE])
        w_hi = sb("w_hi", [P, 8, PIECE], F32R)
        w_lo = sb("w_lo", [P, 8, PIECE], F32R)
        tout = sb("t_out", [P, 2, ROWS])
        nout = sb("n_out", [P, 2, 512])
        sig = sb("sig", [P, 512])
        wa = sb("w_decay", [RANK, 2 * P])
        glr = sb("glr", [RANK, ROWS])
        m_ext = sb("m_ext", [H, EXT])
        lf_ext = sb("lf_ext", [H, EXT])
        g_f = sb("g_f", [H, ROWS])
        g_u = sb("g_u", [P, ROWS])
        keep = sb("keep", [H, ROWS])
        raw_loaded = [sem(f"raw_loaded{s}") for s in range(4)]
        t_stored = [sem(f"t_stored{s}") for s in range(2)]
        n_stored = [sem(f"n_stored{s}") for s in range(2)]
        small_loaded, rows_stored = sem("small_loaded"), sem("rows_stored")
        piece_hi = sem("piece_hi")
        piece_split = sem("piece_split")
        sums_ready = sem("sums_ready")
        sums_taken = sem("sums_taken")
        n_filled, mo_filled = sem("n_filled"), sem("mo_filled")
        sig_ready = sem("sig_ready")
        step, act_step = sem("gate_step"), sem("gate_act_step")
        z_ready, z_taken = sem("z_ready"), sem("z_taken")
        abs_ready, ln_ready, decay_ready = sem("abs_ready"), sem("ln_ready"), sem("decay_ready")
        expo_ready, rows_ready = sem("expo_ready"), sem("rows_ready")
        RAW_CREDIT, BANK_CREDIT = 4, 6
        T_USES = 3 * (1 + NT)
        NUNIT = ((0, 3, 4, 5), (6, 7, 1, 2))
        x_loaded = [sem(f"x_loaded{r}") for r in range(RT)]
        const_loaded = sem("const_loaded")

        def x_row(r):
            if r // JR == 1:
                return raw[:, 1 + r % JR, :]
            return (tout[:, 0, 0:D], tout[:, 1, 0:D], nout[:, :, :].rearrange("p a b -> p (a b)"))[r % JR]

        norm = Norm(nc, ctx, sem, "norm1", x_row, x_row, g_u[:, 0:D], hT, const[:, :], cols[:, K_N1:K_N1 + KD],
                    bank[4:8])
        block = ctx.enter_context(nc.Block())

        def n_unit(n):
            t, q = divmod(n - PC_N, 4)
            return NUNIT[t % 2][q]

        def n_before(n):
            t, q = divmod(n - PC_N, 4)
            return ((3 * NT, 0, 0, 0), (0, 3, T_USES, 0))[t][q] if t < 2 else T_USES + (t - 1) * RT

        @block.sync
        def _(sp):
            def load(n):
                sp.wait_ge(piece_split, n + 1)
                sp.dma_start(raw[:, n % 4, :], a["w"][n]).then_inc(raw_loaded[n % 4], 16)

            def load_x(rb):
                for r in range(rb * JR, (rb + 1) * JR):
                    sp.dma_start(x_row(r), a["x"][r]).then_inc(x_loaded[r], 16)

            load_x(0)
            sp.dma_start(const[:, :], a["ident"]).then_inc(const_loaded, 16)
            sp.dma_start(cols[:, :], a["cols"]).then_inc(const_loaded, 16)
            load(0)
            load_x(1)
            sp.wait_ge(norm.turned, KD)
            load_x(2)
            sp.wait_ge(norm.turned, 2 * KD)
            for n in range(1, 4):
                load(n)
            sp.dma_start(wa[:, :], a["w_decay"]).then_inc(small_loaded, 16)
            sp.dma_start(keep[:, :], a["keep"]).then_inc(small_loaded, 16)
            with sp.Fori(0, NT // 4) as four:
                i = 4 * four
                for q in range(4):
                    sp.wait_ge(piece_split, i + (5 + q))
                    sp.dma_start(raw[:, q, :], a["w"][i + (4 + q)]).then_inc(raw_loaded[q], 16)
                    sp.wait_ge(sums_taken, 3 * i + (BANK_CREDIT + 3 * (q + 2)))
                    sp.dma_start(a["pT"][i + q], tout[:, q % 2, :]).then_inc(t_stored[q % 2], 16)

            load(NT + 4)
            for t in range(NN):
                if t < NN - 1:
                    for q in range(4):
                        load(PC_N + 4 * (t + 1) + q)
                if t == 1:
                    for j in range(2):
                        sp.wait_ge(decay_ready, j + 1)
                        sp.dma_start(a["pT"][NT + j], tout[:, j, :]).then_inc(t_stored[j], 16)
                if t == 2:
                    sp.wait_ge(rows_ready, 4)
                    for q, row in enumerate((g_f, g_u, lf_ext, keep, glr)):
                        sp.dma_start(a["rows"][:, q, :], row[0:H, 0:ROWS]).then_inc(rows_stored, 16)
                    sp.dma_start(o["mm"], m_ext[:, :]).then_inc(rows_stored, 16)
                for r in range(RT):
                    u = t * RT + r
                    if t < NN - 1:
                        sp.wait_ge(n_filled, u + 1)
                    else:
                        sp.wait_ge(mo_filled, r + 1)
                    sp.dma_start(a["pN"][t, r], nout[:, u % 2, :]).then_inc(n_stored[u % 2], 16)
            sp.wait_ge(rows_stored, 6 * 16)
            for s in range(2):
                sp.wait_ge(t_stored[s], 16 * (NT // 2 + 2))
                sp.wait_ge(n_stored[s], 16 * (NN * RT // 2))

        @block.gpsimd
        def _(pool):
            pool.sem_inc(piece_split, RAW_CREDIT)
            pool.sem_inc(sums_taken, BANK_CREDIT)
            pool.sem_inc(t_stored[0], 16)
            pool.sem_inc(t_stored[1], 16)

            def lo(n, unit, slot):
                pool.wait_ge(piece_hi, n + 1)
                pool.tensor_tensor(w_lo[:, unit, :], raw[:, slot, :], w_hi[:, unit, :].bitcast(F32),
                                   ALU.subtract).then_inc(piece_split, 1)

            lo(0, 7, 0)
            lo(1, 0, 1)
            with pool.Fori(0, NT // 4) as four:
                i = 4 * four
                for q in range(4):
                    lo(i + (q + 2), (q + 1) % 2, (q + 2) % 4)
            for n in range(PC_N + 1, PC_OUT):
                lo(n, n_unit(n), n % 4)

        @block.scalar
        def _(act):
            def hi(n, unit, slot, loads):
                act.wait_ge(raw_loaded[slot], loads)
                act.activation(w_hi[:, unit, :], raw[:, slot, :], ACT.Copy).then_inc(piece_hi, 1)

            ready = lambda eng, r: eng.wait_ge(x_loaded[r], 16)
            norm.act_sums(act, 0, ready)
            norm.act_root(act, 0)
            act.wait_ge(const_loaded, 32)
            norm.act_hi(act, 0)
            hi(0, 7, 0, 16)
            norm.act_sums(act, 1, ready)
            norm.act_root(act, 1)
            norm.act_hi(act, 1)
            hi(1, 0, 1, 16)
            norm.act_sums(act, 2, ready)
            norm.act_root(act, 2)
            norm.act_hi(act, 2)
            with act.Fori(0, NT // 4) as four:
                i = 4 * four
                for q in range(4):
                    act.wait_ge(sums_ready, 3 * i + 3 * (q + 1))
                    hi(i + (q + 2), (q + 1) % 2, (q + 2) % 4, 4 * i + 16 * ((q + 2) // 4 + 1))

            def hi_n(n):
                if n_before(n):
                    act.wait_ge(sums_ready, n_before(n))
                hi(n, n_unit(n), n % 4, 16 * (n // 4 + 1))

            for n in range(PC_N + 1, PC_N + 4):
                hi_n(n)
            for j in range(2):
                act.wait_ge(abs_ready, j + 1)
                act.activation(g_u[:, :], g_u[:, :], ACT.Exp).then_inc(act_step, 1)
                act.wait_ge(act_step, 2 * j + 1)
                act.activation(g_u[:, :], g_u[:, :], ACT.Ln, bias=1.0).then_inc(ln_ready, 1)
                act.sem_inc(act_step, 1)
            for n in range(PC_N + 4, PC_N + 8):
                hi_n(n)
            act.wait_ge(abs_ready, 3)
            act.activation(g_u[0:H, :], g_u[0:H, :], ACT.Exp).then_inc(act_step, 1)
            act.wait_ge(act_step, 5)
            act.activation(g_u[0:H, :], g_u[0:H, :], ACT.Ln, bias=1.0).then_inc(ln_ready, 1)
            act.wait_ge(expo_ready, 1)
            act.activation(lf_ext[:, 0:ROWS], lf_ext[:, 0:ROWS], ACT.Exp).then_inc(rows_ready, 1)
            act.activation(keep[:, :], keep[:, :], ACT.Exp).then_inc(rows_ready, 1)
            m_p, m_s = ext_views(m_ext)
            act.activation(glr[0:H, 0:PROMPT], m_p, ACT.Exp, scale=-1.0).then_inc(rows_ready, 1)
            act.activation(streams(glr[0:H, PROMPT:ROWS]), m_s, ACT.Exp, scale=-1.0).then_inc(rows_ready, 1)
            for n in range(PC_N + 8, PC_N + 12):
                hi_n(n)
            for n in range(PC_N + 12, PC_OUT):
                hi_n(n)
            for t in (2, 3):
                for r in range(RT):
                    u = t * RT + r
                    act.wait_ge(sums_ready, T_USES + u + 1)
                    psum = bank[(T_USES + u) % 6][:, :]
                    if t == 2:
                        act.wait_ge(n_filled, u)
                        act.activation(sig[:, :], psum, ACT.Sigmoid).then_inc(sig_ready, 1)
                    else:
                        act.wait_ge(n_stored[u % 2], 16 * (u // 2))
                        act.activation(nout[:, u % 2, :], psum, ACT.Sigmoid).then_inc(mo_filled, 1)

        @block.tensor
        def _(pe):
            def block_t(unit, rb, use_bank):
                for k in range(KD):
                    w = [x[:, unit, k * P:(k + 1) * P] for x in (w_hi, w_lo)]
                    x = [h[:, k, rb * RBW:(rb + 1) * RBW] for h in hT]
                    mm = mm3(pe, bank[use_bank + rb][:, 0:RBW], w, x, k == 0, k == KD - 1)
                mm.then_inc(sums_ready, 1)

            def tile_t(n, unit, use, use_bank):
                pe.wait_ge(piece_split, n + (RAW_CREDIT + 1))
                for rb in range(RB):
                    pe.wait_ge(sums_taken, use + (rb + 1))
                    block_t(unit, rb, use_bank)

            def decays(j):
                for rb in range(RB):
                    n = j * RB + rb
                    if n >= 2:
                        pe.wait_ge(z_taken, n - 1)
                    pe.matmul(bank[6 + n % 2][:, 0:RBW], wa[:, j * P:(j + 1) * P],
                              glr[:, rb * RBW:(rb + 1) * RBW], start=True, stop=True).then_inc(z_ready, 1)

            pe.wait_ge(const_loaded, 32)
            norm.pe_turn(pe, 0)
            pe.wait_ge(piece_split, RAW_CREDIT + 1)
            for rb in range(RB):
                pe.wait_ge(norm.lo_done, KD * (rb + 1))
                block_t(7, rb, 0)
                if rb < RB - 1:
                    norm.pe_turn(pe, rb + 1)
            with pe.Fori(0, NT // 4) as four:
                i = 4 * four
                for q in range(4):
                    tile_t(i + (q + 1), q % 2, 3 * i + 3 * (q + 1), 3 * ((q + 1) % 2))
            pe.wait_ge(small_loaded, 32)
            pe.wait_ge(sums_taken, BANK_CREDIT + RB)
            decays(0)
            for t in range(NN):
                units = NUNIT[t % 2]
                for r in range(RT):
                    u = t * RT + r
                    if u < 6:
                        pe.wait_ge(sums_taken, T_USES + u + 1)
                    elif u - 6 < (NN - 1) * RT:
                        pe.wait_ge(n_filled, u - 5)
                    else:
                        pe.wait_ge(mo_filled, u - 5 - (NN - 1) * RT)
                    for k in range(KD):
                        if r == 0 and k % 2 == 0:
                            pe.wait_ge(piece_split, PC_N + 4 * t + k // 2 + 1 + RAW_CREDIT)
                        x = [h[:, k, r * P:(r + 1) * P] for h in hT]
                        w = [y[:, units[k // 2], (k % 2) * 512:(k % 2 + 1) * 512] for y in (w_hi, w_lo)]
                        mm = mm3(pe, bank[(T_USES + u) % 6], x, w, k == 0, k == KD - 1)
                    mm.then_inc(sums_ready, 1)
                    if u == 2:
                        decays(1)

        @block.vector
        def _(dve):
            chain = Count(dve, step)
            bf = cols[0:H, K_BG:K_BG + 1]
            bi = cols[32:32 + H, K_BG:K_BG + 1]
            i_p, i_s = ext_views(m_ext)
            lf_p, lf_s = ext_views(lf_ext)
            dve.memset(m_ext[:, :], 0.0).then_inc(step, 1)
            dve.memset(lf_ext[:, :], NEG).then_inc(step, 1)
            chain.n = 2
            dve.wait_ge(step, 2)
            norm.dve_invert(dve, 0, chain)
            norm.dve_scale(dve, 0)
            dve.wait_ge(const_loaded, 32)
            for rb in range(RB):
                norm.dve_lo(dve, rb)
                if rb < RB - 1:
                    norm.dve_invert(dve, rb + 1, chain)
                    norm.dve_scale(dve, rb + 1)
            for rb in range(RB):
                dve.wait_ge(sums_ready, rb + 1)
                s = slice(rb * RBW, (rb + 1) * RBW)
                (p0, pn), (s0, sn) = split_spans(rb)
                dve.tensor_scalar(g_f[:, s], bank[rb][0:H, 0:RBW], bf, None, ALU.add)
                dve.tensor_scalar(i_p[:, rb * RBW:rb * RBW + pn], bank[rb][32:32 + H, 0:pn], bi, None, ALU.add)
                if sn:
                    dve.tensor_scalar(i_s, streams(bank[rb][32:32 + H, s0:s0 + sn]), bi, None, ALU.add)
                dve.tensor_copy(glr[:, s], bank[rb][64:64 + RANK, 0:RBW]).then_inc(sums_taken, 1)
            with dve.Fori(0, NT // 4) as four:
                i = 4 * four
                for q in range(4):
                    dve.wait_ge(t_stored[q % 2], 8 * i + 16 * (q // 2 + 1))
                    for rb in range(RB):
                        dve.wait_ge(sums_ready, 3 * i + (3 * (q + 1) + rb + 1))
                        dve.tensor_copy(tout[:, q % 2, rb * RBW:(rb + 1) * RBW],
                                        bank[3 * ((q + 1) % 2) + rb][:, 0:RBW]).then_inc(sums_taken, 1)
            for j in range(2):
                dve.wait_ge(t_stored[j], 16 * (NT // 2 + 1))
                for rb in range(RB):
                    n = j * RB + rb
                    dve.wait_ge(z_ready, n + 1)
                    dve.tensor_scalar(tout[:, j, rb * RBW:(rb + 1) * RBW], bank[6 + n % 2][:, 0:RBW],
                                      cols[:, K_BA + j:K_BA + j + 1], None, ALU.add).then_inc(z_taken, 1)
                dve.wait_ge(z_taken, RB * (j + 1))
                z = tout[:, j, :]
                if j:
                    dve.wait_ge(decay_ready, j)
                dve.scalar_tensor_tensor(out=g_u[:, :], in0=z, scalar=-1.0, in1=z, op0=ALU.mult,
                                         op1=ALU.min).then_inc(abs_ready, 1)
                dve.wait_ge(ln_ready, j + 1)
                dve.scalar_tensor_tensor(out=z, in0=z, scalar=0.0, in1=g_u[:, :], op0=ALU.min,
                                         op1=ALU.subtract).then_inc(decay_ready, 1)

            def take(t):
                for r in range(RT):
                    u = t * RT + r
                    dve.wait_ge(sums_ready, T_USES + u + 1)
                    if u >= 2:
                        dve.wait_ge(n_stored[u % 2], 16 * (u // 2))
                    psum = bank[(T_USES + u) % 6][:, :]
                    if t < 2:
                        dve.tensor_copy(nout[:, u % 2, :], psum).then_inc(n_filled, 1)
                    else:
                        dve.wait_ge(sig_ready, r + 1)
                        dve.tensor_tensor(nout[:, u % 2, :], psum, sig[:, :], ALU.mult).then_inc(n_filled, 1)

            take(0)
            dve.wait_ge(small_loaded, 32)
            dve.wait_ge(decay_ready, 2)
            u4 = g_u[0:H, :]
            dve.scalar_tensor_tensor(out=u4, in0=g_f[:, :], scalar=-1.0, in1=g_f[:, :], op0=ALU.mult,
                                     op1=ALU.min).then_inc(abs_ready, 1)
            dve.wait_ge(ln_ready, 3)
            chain.link(dve.scalar_tensor_tensor(out=u4, in0=g_f[:, :], scalar=0.0, in1=u4, op0=ALU.min,
                                                op1=ALU.subtract))
            dve.tensor_copy(lf_p, u4[:, 0:PROMPT])
            dve.tensor_copy(lf_s, streams(u4[:, PROMPT:ROWS]))
            chain.link(dve.tensor_copy(first_slots(m_ext), cols[0:H, K_M0:K_M0 + NB]))
            chain.link(dve.tensor_tensor_scan(g_f[:, :], keep[:, :], u4, 0.0, ALU.mult, ALU.add))
            dve.tensor_tensor(u4[:, 0:PROMPT], i_p, g_f[:, 0:PROMPT], ALU.subtract)
            chain.link(dve.tensor_tensor(streams(u4[:, PROMPT:ROWS]), i_s, streams(g_f[:, PROMPT:ROWS]),
                                         ALU.subtract))
            chain.link(dve.tensor_tensor_scan(m_ext[:, :], lf_ext[:, :], m_ext[:, :], 0.0, ALU.add, ALU.max))
            dve.tensor_tensor(g_f[:, 0:PROMPT], g_f[:, 0:PROMPT], i_p, ALU.subtract)
            chain.link(dve.tensor_tensor(streams(g_f[:, PROMPT:ROWS]), streams(g_f[:, PROMPT:ROWS]), i_s,
                                         ALU.subtract))
            rp, rs = chunks(g_f[:, 0:PROMPT]), streams(g_f[:, PROMPT:ROWS])
            dve.tensor_tensor(chunks(lf_ext[:, 0:PROMPT]), rp,
                              chunks(m_ext[:, 0:PROMPT])[:, :, 0:1].to_broadcast([H, NC, P]), ALU.add)
            dve.tensor_tensor(streams(lf_ext[:, PROMPT:ROWS]), rs,
                              first_slots(m_ext).unsqueeze(2).to_broadcast([H, NB, LB]), ALU.add)
            dve.tensor_tensor(chunks(keep[:, 0:PROMPT]), chunks(u4[:, 0:PROMPT]),
                              rp[:, :, P - 1:P].to_broadcast([H, NC, P]), ALU.add)
            dve.tensor_tensor(streams(keep[:, PROMPT:ROWS]), streams(u4[:, PROMPT:ROWS]),
                              rs[:, :, LB - 1:LB].to_broadcast([H, NB, LB]), ALU.add).then_inc(expo_ready, 1)
            take(1)
            take(2)


def streams(ap):
    return ap.rearrange("h (b e) -> h b e", e=LB)


def chunks(ap):
    return ap.rearrange("h (c e) -> h c e", e=P)


def ext_views(ext):
    return (ext[0:H, 1:1 + PROMPT],
            ext[0:H, 1 + PROMPT:EXT].rearrange("h (b e) -> h b e", e=LB + 1)[:, :, 1:LB + 1])


def first_slots(ext):
    return ext[0:H, 1 + PROMPT:EXT].rearrange("h (b e) -> h b e", e=LB + 1)[:, :, 0]


def mix(nc, a, o, ident, x9, ssq, pb, bank):
    SLOTS = 2
    HP = P // 2
    E_B, E_LAST, E_LV = 0, 2 * P, 4 * P
    L = LEVELS + 1
    with ExitStack() as ctx:
        sb = lambda n, s, d=F32: ctx.enter_context(nc.sbuf_tensor(f"m_{n}", s, d))
        sem = Sems(nc, ctx, "m_")
        const = sb("const", [P, N_CONST])
        tin = sb("t_in", [P, SLOTS, NT + 2, P])
        rin = sb("r_in", [H, SLOTS, 5, P])
        wt = sb("wt", [P, SLOTS, H, P])
        wq = sb("wq", [P, SLOTS, H, P])
        nin = sb("n_in", [P, SLOTS, 3, 512])
        vin = sb("v_in", [P, SLOTS, H, VX])
        ex = sb("ex", [P, SLOTS, E_LV + LEVELS * 2 * P])
        q8 = sb("q8", [P, SLOTS, 2, 2, P])
        qb = sb("qb", [P, SLOTS, 2 * P])
        qx = sb("qx", [P, SLOTS, LEVELS, 2, 2, HP])
        kx = sb("kx", [P, SLOTS, LEVELS + 2, 2 * P])
        qs = sb("qs", [P, SLOTS, H, P])
        dg = sb("dg", [H, NB, H])
        col = sb("col", [P, SLOTS, 3 * H + NB * H])
        am = sb("am", [P, SLOTS, H, P])
        ksn = sb("ks", [P, SLOTS, H, DH])
        gsc = sb("gla_scores", [P, H, P])
        kdn = sb("k_decayed", [P, 2, P])
        den = [sb(f"den{i}", [P, 2, 2, 1]) for i in range(3)]
        sq = sb("sq", [P, 2 * H, P])
        qsm, qbm = sb("qs_masked", [P, H, NB, 2 * LB]), sb("qb_masked", [P, 2, NB, 2 * LB])
        vmm, vgm = sb("mv_masked", [P, 2, H * VX]), sb("gv_masked", [P, 2, 512])

        class Kind:

            def __init__(self, name, states, frames, lv0, caus, keep):
                self.sample = states > 1
                self.NS, self.LS, self.LV0, self.NL = states, frames, lv0, LEVELS - lv0
                self.caus, self.keep = caus, keep
                self.NCOL = 3 * H + states * H
                self.S, self.C = sb(f"S_{name}", [P, states, 2, DV]), sb(f"C_{name}", [P, states, H, VX])
                self.groups = [(range(0, 4), lvl_a)] + ([] if self.sample else [(range(4, self.NL), lvl_b)])
                self.groups += [(range(self.NL, self.NL + 1), lvl_b if self.sample else lvl_a)]

            def width(self, n):
                return P >> (n + self.LV0 + 1)

            def ug_out(self, b, j):
                return bank[6 + b % 2][:, j * P:(j + 1) * P] if self.sample else bankm[:, j, UG:UG + P]

        COLS = 2 * VX
        UG = 3 * P
        lvl_b, lvl_a, bankm = pb[0], pb[2], pb[3]
        PR = Kind("prompt", 1, P, 0, C_CAUS, C_KEEP)
        SA = Kind("sample", NB, LB, 3, C_CAUSB, C_KEEPB)
        decays_in = [sem(f"decays_in{s}") for s in range(SLOTS)]
        front_in = [sem(f"front_in{s}") for s in range(SLOTS)]
        back_in = [sem(f"back_in{s}") for s in range(SLOTS)]
        keep_in, const_in, state_in, state_out = sem("keep_in"), sem("const_in"), sem("state_in"), sem("state_out")
        names = ("zeroed b_ready upper_ready lower_ready lv_exp q8_ready rmask_ready kx_ready qs_ready "
                 "dg_ready cols_ready cols_taken qk_ready kt_ready wt_ready am_ready ksn_ready qx_ready "
                 "kdt_ready kdn_ready lvl_ready lvl_taken lvl_seen num_ready den_step mlstm_done um_ready "
                 "um_taken o_ready o_squared o_taken ug_ready ug_taken qm_ready vm_ready cleared")
        g = {n: sem(n) for n in names.split()}
        cs = lambda k, n: const[:, k:k + n]
        ones4 = cs(C_ONE, P)[0:H, :]
        id4 = ident[0:H, 0:H]
        ZEROED = 8
        o_bank = lambda h: lvl_b[:, h % 2, (h // 2) * P:(h // 2 + 1) * P]
        half = lambda ap, h: ap[(h % 2) * DK:(h % 2 + 1) * DK]
        num = lambda h: bankm[:, h // 2, (h % 2) * VX:(h % 2 + 1) * VX]
        um_bank = lambda b: pb[2 - b % 2]
        lowers = lambda ap, w: ap.rearrange("p (n w) -> p n w", w=2 * w)[:, :, 0:w]
        packed = lambda ap, w: ap.rearrange("p (n w) -> p n w", w=w)
        block = ctx.enter_context(nc.Block())

        def pipeline(eng, front, step, back):
            front(PR, 0, 0)
            with eng.Fori(0, (NC - 2) // 2) as two:
                step(PR, PR, 2 * two, 0)
                step(PR, PR, 2 * two + 1, 1)
            step(PR, PR, NC - 2, 0)
            step(PR, SA, NC - 1, 1)
            back(SA, NC, 0)

        def loads(c, s, n):
            return 8 * n * (c + (2 if s == 0 else 1))

        @block.sync
        def _(sp):
            def front(c, s):
                r = bass.ts(c, P)
                for tiles, loaded in ((slice(NT, NT + 2), decays_in), (slice(0, NT), front_in)):
                    sp.dma_start(tin[:, s, tiles, :], a["pT"][tiles, :, r].rearrange("t p f -> p t f"))\
                      .then_inc(loaded[s], 16)
                sp.dma_start(rin[:, s, :, :], a["rows"][:, :, r]).then_inc(front_in[s], 16)
                for dst, q in ((wt, 0), (wq, 2)):
                    sp.dma_start(dst[:, s, :, :], a["rows"][:, q, r].unsqueeze(0).to_broadcast([P, H, P]))\
                      .then_inc(front_in[s], 16)

            def back(c, s):
                sp.dma_start(vin[:, s, :, 0:DH], a["pN"][1, c].rearrange("p (h v) -> p h v", h=H)).then_inc(back_in[s], 16)
                sp.dma_start(nin[:, s, 0, :], a["pN"][0, c]).then_inc(back_in[s], 16)
                sp.dma_start(nin[:, s, 1:3, :], a["pN"][2:4, c].rearrange("q p v -> p q v")).then_inc(back_in[s], 16)

            def two_on(c, s):
                for n in ("am_ready", "qs_ready", "q8_ready", "kt_ready"):
                    sp.wait_ge(g[n], c + 1)
                front(c + 2, s)
                sp.wait_ge(g["ug_taken"], 2 * c + 2 + 2)
                back(c + 2, s)

            sp.dma_start(const[:, C_KEEP:C_KEEP + 2 * P], a["const"][:, C_KEEP:C_KEEP + 2 * P]).then_inc(keep_in, 16)
            front(0, 0)
            for cut in (slice(0, C_KEEP), slice(C_KEEP + 2 * P, N_CONST)):
                sp.dma_start(const[:, cut], a["const"][:, cut]).then_inc(const_in, 16)
            back(0, 0)
            front(1, 1)
            back(1, 1)
            sp.dma_start(SA.C[:, :, :, :], a["s_mc"]).then_inc(state_in, 16)
            sp.dma_start(SA.S[:, :, :, :], a["s_gla"]).then_inc(state_in, 16)
            with sp.Fori(0, (NC - 2) // 2) as two:
                two_on(2 * two, 0)
                two_on(2 * two + 1, 1)
            two_on(NC - 2, 0)
            sp.wait_ge(g["ug_taken"], 2 * NC + 2)
            sp.dma_start(o["p_mc"].unsqueeze(1), PR.C[:, :, :, :]).then_inc(state_out, 16)
            sp.dma_start(o["p_gla"].unsqueeze(1), PR.S[:, :, :, :]).then_inc(state_out, 16)
            for half_ in range(2):
                b = slice(half_ * NB // 2, (half_ + 1) * NB // 2)
                sp.wait_ge(g["um_taken"], NC + b.stop)
                sp.dma_start(o["q_mc"][:, b], SA.C[:, b, :, :]).then_inc(state_out, 16)
            for b in (slice(0, NB // 2), slice(NB // 2, NB)):
                sp.wait_ge(g["ug_taken"], 2 * (NC + b.stop) + 2)
                sp.dma_start(o["q_gla"][:, b], SA.S[:, b, :, :]).then_inc(state_out, 16)
            sp.wait_ge(state_out, 6 * 16)

        @block.gpsimd
        def _(pool):
            pool.sem_inc(g["lvl_taken"], 1)
            pool.sem_inc(g["ug_taken"], 2)
            pool.sem_inc(g["o_taken"], 1)
            for s in range(SLOTS):
                pool.memset(q8[:, s, :, :, :], 0.0).then_inc(g["zeroed"], 1)
            for x in (kx[:, 1, :, :], PR.S[:, :, :, :]):
                pool.memset(x, 0.0).then_inc(g["zeroed"], 1)
            pool.memset(vin[:, :, :, DH:VX], 1.0).then_inc(g["zeroed"], 1)
            pool.wait_ge(g["zeroed"], ZEROED)

            def front(v, c, s, first=False):
                e = ex[:, s, :]
                NL, LS, width = v.NL, v.LS, v.width
                pool.wait_ge(g["b_ready"], c + 1)
                for n in range(NL):
                    w = width(n)
                    b = e[:, E_B:E_B + 2 * P].rearrange("p (n w) -> p n w", w=2 * w)
                    at = E_LV + n * 2 * P + P
                    pool.tensor_tensor(packed(e[:, at:at + P], w), b[:, :, w - 1:w].to_broadcast([P, P // w, w]),
                                       b[:, :, 0:w], ALU.subtract)
                b = e[:, E_B:E_B + 2 * P].rearrange("p (n w) -> p n w", w=LS)
                pool.tensor_tensor(packed(e[:, E_LAST:E_LAST + 2 * P], LS),
                                   b[:, :, LS - 1:LS].to_broadcast([P, 2 * P // LS, LS]), b,
                                   ALU.subtract).then_inc(g["lower_ready"], 1)
                pool.wait_ge(const_in, 32)
                pool.wait_ge(front_in[s], loads(c, s, 4))
                caus = cs(v.caus, P)
                pool.tensor_tensor(wt[:, s, :, :], wt[:, s, :, :], caus.unsqueeze(1).to_broadcast([P, H, P]),
                                   ALU.add).then_inc(g["rmask_ready"], 1)
                if first:
                    for x in (qsm, qbm):
                        pool.memset(x[:, :, :, :], 0.0).then_inc(g["zeroed"], 1)
                pool.wait_ge(g["lv_exp"], c + 1)
                k = tin[:, s, 2:4, :].rearrange("p j f -> p (j f)")
                for n in range(NL):
                    w = width(n)
                    at = E_LV + n * 2 * P + P
                    pool.tensor_tensor(lowers(kx[:, s, n, :], w), packed(e[:, at:at + P], w), lowers(k, w), ALU.mult)
                pool.tensor_tensor(kx[:, s, NL, :], e[:, E_LAST:E_LAST + 2 * P], k, ALU.mult)\
                    .then_inc(g["kx_ready"], 1)
                pool.tensor_tensor(qs[:, s, :, :], tin[:, s, 4:8, :], wq[:, s, :, :], ALU.mult)
                pool.wait_ge(g["q8_ready"], c + 1)
                pool.tensor_tensor(qb[:, s, :], e[:, E_B:E_B + 2 * P], qb[:, s, :], ALU.mult).then_inc(g["qs_ready"], 1)
                if v.sample:
                    parity = cs(C_PARITY, 2).unsqueeze(2)
                    pool.wait_ge(back_in[s], loads(c, s, 3))
                    for dst, x in ((vmm, vin[:, s, :, :].rearrange("p h v -> p (h v)")), (vgm, nin[:, s, 0, :])):
                        k = dst.shape[2]
                        pool.tensor_tensor(dst[:, :, :], x.unsqueeze(1).to_broadcast([P, 2, k]),
                                           parity.to_broadcast([P, 2, k]), ALU.mult).then_inc(g["vm_ready"], 1)

            pipeline(pool, lambda v, c, s: front(v, c, s, first=True), lambda vb, vf, c, s: front(vf, c + 1, 1 - s),
                     lambda v, c, s: None)

        @block.scalar
        def _(act):
            def front_queries(v, c, s):
                act.wait_ge(front_in[s], loads(c, s, 4))
                act.wait_ge(g["b_ready"], c + 1)
                act.activation(kx[:, s, v.NL + 1, :], tin[:, s, 2:4, :].rearrange("p j f -> p (j f)"), ACT.Copy)
                for e in range(2):
                    act.activation(q8[e * DK:(e + 1) * DK, s, :, e, :], tin[e * DK:(e + 1) * DK, s, 0:2, :],
                                   ACT.Copy, scale=QSCALE)
                act.activation(qb[:, s, :], tin[:, s, 0:2, :].rearrange("p j f -> p (j f)"), ACT.Copy,
                               scale=QSCALE).then_inc(g["q8_ready"], 1)

            def front_powers(v, c, s):
                act.wait_ge(g["upper_ready"], c + 1)
                act.wait_ge(g["lower_ready"], c + 1)
                x = ex[:, s, 0:E_LV + v.NL * 2 * P]
                act.activation(x, x, ACT.Exp, scale=1.0 / TAU).then_inc(g["lv_exp"], 1)

            def front_weights(v, c, s):
                act.wait_ge(g["rmask_ready"], c + 1)
                act.wait_ge(g["cols_taken"], c + 1)
                for h in range(H):
                    w = act.activation(wt[:, s, h, :], wt[:, s, h, :], ACT.Exp, bias=col[:, s, h:h + 1])
                w.then_inc(g["wt_ready"], 1)

            def front_keys(v, c, s):
                act.wait_ge(g["kt_ready"], c + 1)
                for h in range(H):
                    k = act.activation(ksn[:, s, h, :], bank[3][:, h * P:(h + 1) * P], ACT.Copy,
                                       scale=col[:, s, H + h:H + h + 1])
                k.then_inc(g["ksn_ready"], 1)

            def back_decayed(v, c, s):
                act.wait_ge(g["kdt_ready"], c + 1)
                act.activation(kdn[:, :, :], bank[3][:, 0:2 * P].rearrange("p (j f) -> p j f", j=2),
                               ACT.Copy).then_inc(g["kdn_ready"], 1)

            def back_squares(v, c, s):
                act.wait_ge(g["mlstm_done"], c + 1)
                for h in range(H):
                    act.activation(sq[:, H + h, :], x9[:, c, 512 + h * P:512 + (h + 1) * P], ACT.Square,
                                   accum_out=ssq[:, c, H + h:H + h + 1])
                act.wait_ge(g["o_ready"], c + 1)
                for h in range(H):
                    q = act.activation(sq[:, h, :], o_bank(h), ACT.Square,
                                       accum_out=ssq[:, c, h:h + 1])
                q.then_inc(g["o_squared"], 1)

            def front(v, c, s):
                front_queries(v, c, s)
                front_powers(v, c, s)
                front_weights(v, c, s)
                front_keys(v, c, s)

            def step(vb, vf, c, s):
                front_queries(vf, c + 1, 1 - s)
                back_decayed(vb, c, s)
                front_powers(vf, c + 1, 1 - s)
                front_weights(vf, c + 1, 1 - s)
                back_squares(vb, c, s)
                front_keys(vf, c + 1, 1 - s)

            def back(v, c, s):
                back_decayed(v, c, s)
                back_squares(v, c, s)

            act.wait_ge(g["zeroed"], ZEROED)
            act.activation(sq[:, 0, 0:1], vin[:, 0, 0, DH:VX], ACT.Exp)
            pipeline(act, front, step, back)

        @block.tensor
        def _(pe):
            def front_scores(v, c, s):
                pe.wait_ge(front_in[s], loads(c, s, 4))
                for h in range(H):
                    mm = pe.matmul(bank[2][:, h * P:(h + 1) * P], tin[:, s, 8 + h, :], tin[:, s, 4 + h, :],
                                   start=True, stop=True)
                mm.then_inc(g["qk_ready"], 1)

            def front_rows(v, c, s):
                pe.wait_ge(const_in, 32)
                pe.wait_ge(g["dg_ready"], c + 1)
                for n, q in enumerate((1, 3, 4)):
                    pe.matmul(bank[6][:, COLS + H * n:COLS + H * (n + 1)], rin[:, s, q, :], id4, start=True, stop=True)
                pe.matmul(bank[6][:, COLS + 3 * H:COLS + v.NCOL], ones4, dg[:, 0:v.NS, :].rearrange("p b h -> p (b h)"),
                          start=True, stop=True).then_inc(g["cols_ready"], 1)

            def front_turn(v, c, s):
                for h in range(H):
                    mm = pe.transpose(bank[3][:, h * P:(h + 1) * P], tin[:, s, 8 + h, :], ident)
                mm.then_inc(g["kt_ready"], 1)

            def front(v, c, s):
                front_scores(v, c, s)
                front_rows(v, c, s)
                front_turn(v, c, s)

            def scores(v, c, s, n):
                levels, out = v.groups[n]
                for lv in levels:
                    for j in range(2):
                        at = (lv - levels[0]) * HP
                        dst = out[:, j, :].rearrange("p (e x) -> p e x", e=2)
                        if lv < v.NL:
                            mm = pe.matmul(dst[:, :, at:at + HP], kx[:, s, lv, j * P:(j + 1) * P], qx[:, s, lv, j, :, :],
                                           start=True, stop=True)
                        else:
                            mm = pe.matmul(dst[:, :, 0:P], kx[:, s, v.NL + 1, j * P:(j + 1) * P], q8[:, s, j, :, :],
                                           start=True, stop=True)
                mm.then_inc(g["lvl_ready"], 1)

            def back_first(v, c, s):
                pe.wait_ge(g["kx_ready"], c + 1)
                pe.wait_ge(g["qx_ready"], 2 * c + 1)
                scores(v, c, s, 0)

            def from_states(out, queries, states, frames):
                for b in range(NB):
                    i = b // 2
                    mm = pe.matmul(out[i * frames:(i + 1) * frames], queries(b), states(b), start=False,
                                   stop=True, skip_group_check=True)
                return mm

            def back_rest(v, c, s, front_rows_done, rows=None, following=None):
                pe.wait_ge(g["ksn_ready"], c + 1)
                for j in range(2):
                    mm = pe.transpose(bank[3][:, j * P:(j + 1) * P], kx[:, s, v.NL, j * P:(j + 1) * P], ident)
                mm.then_inc(g["kdt_ready"], 1)
                pe.wait_ge(g["o_taken"], c + 1)
                if not v.sample:
                    pe.wait_ge(g["qx_ready"], 2 * c + 2)
                scores(v, c, s, 1)
                if rows:
                    rows()
                if len(v.groups) > 2:
                    pe.wait_ge(g["lvl_taken"], L * c + 4 + 1)
                    scores(v, c, s, 2)
                pe.wait_ge(g["cols_taken"], front_rows_done)
                pe.wait_ge(g["ug_taken"], 2 * c + 2)
                pe.wait_ge(g["am_ready"], c + 1)
                pe.wait_ge(g["qs_ready"], c + 1)
                pe.wait_ge(back_in[s], loads(c, s, 3))
                if v.sample:
                    pe.wait_ge(g["qm_ready"], 1)
                    pe.wait_ge(state_in, 32)
                for h in range(H):
                    if v.sample:
                        pe.matmul(num(h), am[:, s, h, :], vin[:, s, h, :], start=True, stop=True)
                        mm = from_states(num(h), lambda b: qsm[:, h, b, :], lambda b: v.C[:, b, h, :], 2 * LB)
                    else:
                        pe.matmul(num(h), qs[:, s, h, :], v.C[:, 0, h, :], start=True, stop=False)
                        mm = pe.matmul(num(h), am[:, s, h, :], vin[:, s, h, :], start=False, stop=True)
                mm.then_inc(g["num_ready"], 1)
                pe.wait_ge(g["lvl_taken"], L * c + v.NL + 1 + 1)
                pe.wait_ge(g["kdn_ready"], c + 1)
                if v.sample:
                    pe.wait_ge(g["vm_ready"], 1)
                for b in range(v.NS):
                    if b >= 2:
                        pe.wait_ge(g["um_taken"], c + b - 1)
                    r = slice(b // 2 * 2 * LB, (b // 2 + 1) * 2 * LB) if v.sample else slice(0, P)
                    for h in range(H):
                        x = vmm[r, b % 2, h * VX:(h + 1) * VX] if v.sample else vin[:, s, h, :]
                        mm = pe.matmul(um_bank(b)[:, h // 2, (h % 2) * VX:(h % 2 + 1) * VX], ksn[r, s, h, :], x,
                                       start=True, stop=True)
                    mm.then_inc(g["um_ready"], 1)
                if following:
                    following()
                if v.sample:
                    pe.wait_ge(g["qm_ready"], 2)
                for h in range(H):
                    j = h // 2
                    if v.sample:
                        pe.matmul(o_bank(h), gsc[:, h, :], nin[:, s, 0, h * P:(h + 1) * P], start=True, stop=True)
                        mm = from_states(o_bank(h), lambda b: half(qbm, h)[:, j, b, :], lambda b: half(v.S, h)[:, b, j, :],
                                         2 * LB)
                    else:
                        pe.matmul(o_bank(h), half(qb, h)[:, s, j * P:(j + 1) * P], half(v.S, h)[:, 0, j, :], start=True,
                                  stop=False)
                        mm = pe.matmul(o_bank(h), gsc[:, h, :], nin[:, s, 0, h * P:(h + 1) * P],
                                       start=False, stop=True)
                mm.then_inc(g["o_ready"], 1)
                pe.wait_ge(g["mlstm_done"], c + 1)
                if v.sample:
                    pe.wait_ge(g["vm_ready"], 2)
                for b in range(v.NS):
                    if b >= 2:
                        pe.wait_ge(g["ug_taken"], 2 * c + 2 * (b - 1) + 2)
                    r = slice(b // 2 * 2 * LB, (b // 2 + 1) * 2 * LB) if v.sample else slice(0, P)
                    for h in range(H):
                        j = h // 2
                        x = vgm[r, b % 2, h * P:(h + 1) * P] if v.sample else nin[:, s, 0, h * P:(h + 1) * P]
                        mm = pe.matmul(half(v.ug_out(b, j), h), kdn[r, j, (h % 2) * DK:(h % 2 + 1) * DK], x,
                                       start=True, stop=True)
                    mm.then_inc(g["ug_ready"], 1)

            def step(vb, vf, c, s):
                pe.wait_ge(g["am_ready"], c + 1)
                front_scores(vf, c + 1, 1 - s)
                back_first(vb, c, s)
                back_rest(vb, c, s, c + 2, lambda: front_rows(vf, c + 1, 1 - s), lambda: front_turn(vf, c + 1, 1 - s))

            def back(v, c, s):
                back_first(v, c, s)
                back_rest(v, c, s, c + 1)

            pe.wait_ge(g["zeroed"], ZEROED)
            pipeline(pe, front, step, back)

        @block.vector
        def _(dve):
            def front_exponents(v, c, s, first=False):
                dve.wait_ge(decays_in[s], loads(c, s, 1))
                if not first:
                    dve.wait_ge(g["ug_taken"], 2 * c)
                e = ex[:, s, :]
                keep = cs(v.keep, 2 * P)
                la = tin[:, s, NT:NT + 2, :].rearrange("p j f -> p (j f)")
                dve.tensor_tensor_scan(e[:, E_B:E_B + 2 * P], keep, la, 0.0, ALU.mult, ALU.add).then_inc(g["b_ready"], 1)

            def front_diagonal(v, c, s):
                NS, LS = v.NS, v.LS
                dve.wait_ge(front_in[s], loads(c, s, 4))
                dec = rin[:, s, 2, :].rearrange("p (b f) -> p b f", f=LS)[:, :, LS - 1:LS]
                dve.tensor_tensor(dg[:, 0:NS, :], dec.to_broadcast([H, NS, H]),
                                  id4.unsqueeze(1).to_broadcast([H, NS, H]), ALU.mult).then_inc(g["dg_ready"], 1)

            def front_uppers(v, c, s):
                e = ex[:, s, :]
                dve.wait_ge(g["b_ready"], c + 1)
                for n in range(v.NL):
                    w = v.width(n)
                    b = e[:, E_B:E_B + 2 * P].rearrange("p (n w) -> p n w", w=2 * w)
                    at = E_LV + n * 2 * P
                    u = dve.tensor_tensor(packed(e[:, at:at + P], w), b[:, :, w:2 * w],
                                          b[:, :, w - 1:w].to_broadcast([P, P // w, w]), ALU.subtract)
                u.then_inc(g["upper_ready"], 1)

            def front_columns(v, c, s):
                NCOL = v.NCOL
                dve.wait_ge(g["cols_ready"], c + 1)
                ps = bank[6][:, COLS:COLS + NCOL]
                dve.tensor_copy(col[:, s, 0:H], ps[:, 0:H])
                dve.tensor_scalar(col[:, s, H:2 * H], ps[:, H:2 * H], KSCALE, None, ALU.mult)
                dve.tensor_copy(col[:, s, 2 * H:NCOL], ps[:, 2 * H:NCOL]).then_inc(g["cols_taken"], 1)

            def front_weights(v, c, s):
                dve.wait_ge(g["qk_ready"], c + 1)
                dve.wait_ge(g["wt_ready"], c + 1)
                dve.scalar_tensor_tensor(out=am[:, s, :, :].rearrange("p h f -> p (h f)"), in0=bank[2], scalar=KSCALE,
                                         in1=wt[:, s, :, :].rearrange("p h f -> p (h f)"), op0=ALU.mult,
                                         op1=ALU.mult).then_inc(g["am_ready"], 1)

            def level_queries(v, c, s, levels):
                for n in levels:
                    w = v.width(n)
                    at = E_LV + n * 2 * P
                    x = ex[:, s, at:at + P].rearrange("p (j n w) -> p j n w", j=2, w=w)
                    q = dve.tensor_tensor(
                        qx[:, s, n, :, :, :].rearrange("p j e (n w) -> p j e n w", w=w),
                        x.unsqueeze(2).to_broadcast([P, 2, 2, HP // w, w]),
                        q8[:, s, :, :, :].rearrange("p j e (n w) -> p j e n w", w=2 * w)[:, :, :, :, w:2 * w],
                        ALU.mult)
                return q

            def front_queries_first(v, c, s):
                dve.wait_ge(g["lv_exp"], c + 1)
                dve.wait_ge(g["q8_ready"], c + 1)
                level_queries(v, c, s, v.groups[0][0]).then_inc(g["qx_ready"], 1)

            def front_queries_rest(v, c, s):
                if not v.sample:
                    level_queries(v, c, s, range(4, v.NL)).then_inc(g["qx_ready"], 1)

            def back_scores(v, c, s, after_first=None):
                if v.sample:
                    dve.wait_ge(g["o_ready"], c)
                    dve.memset(gsc[:, :, :], 0.0).then_inc(g["cleared"], 1)
                    dve.wait_ge(g["cleared"], 1)
                for n, (levels, src) in enumerate(v.groups):
                    for lv in levels:
                        if lv == levels[0]:
                            dve.wait_ge(g["lvl_ready"], len(PR.groups) * c + (n + 1))
                        dve.wait_ge(g["lvl_taken"], L * c + (lv + 1))
                        dve.sem_inc(g["lvl_seen"], 1)
                        x = src[:, :, :].rearrange("p j (e x) -> p (j e) x", x=2 * P)
                        if lv < v.NL:
                            w = v.width(lv)
                            at = (lv - levels[0]) * HP
                            mask = cs(C_LV + (lv + v.LV0) * HP, HP)
                            cp = dve.copy_predicated(
                                gsc[:, :, :].rearrange("p h (n w) -> p h n w", w=2 * w)[:, :, :, w:2 * w],
                                packed(mask, w).bitcast(I32).unsqueeze(1).to_broadcast([P, H, HP // w, w]),
                                x[:, :, at:at + HP].rearrange("p h (n w) -> p h n w", w=w))
                        else:
                            cp = dve.copy_predicated(gsc[:, :, :],
                                                     cs(C_DIAG, P).bitcast(I32).unsqueeze(1).to_broadcast([P, H, P]),
                                                     x[:, :, 0:P])
                        cp.then_inc(g["lvl_taken"], 1)
                    if after_first and n == 0:
                        after_first()

            def back_mlstm(v, c, s):
                dve.wait_ge(g["num_ready"], c + 1)
                d = bankm[:, :, 0:2 * VX].rearrange("p a (b v) -> p a b v", v=VX)[:, :, :, DH:VX]
                z = lambda n: dve.wait_ge(g["den_step"], 4 * c + n)
                dve.tensor_copy(den[1][:, :, :, :], d).then_inc(g["den_step"], 1)
                z(1)
                dve.scalar_tensor_tensor(out=den[0][:, :, :, :], in0=den[1][:, :, :, :], scalar=-1.0,
                                         in1=den[1][:, :, :, :], op0=ALU.mult, op1=ALU.max).then_inc(g["den_step"], 1)
                z(2)
                dve.tensor_tensor(den[1][:, :, :, :], den[0][:, :, :, :],
                                  col[:, s, 2 * H:3 * H].rearrange("p (a b) -> p a b", b=2).unsqueeze(3),
                                  ALU.max).then_inc(g["den_step"], 1)
                z(3)
                dve.reciprocal(den[2][:, :, :, :], den[1][:, :, :, :]).then_inc(g["den_step"], 1)
                z(4)
                for h in range(H):
                    m = dve.scalar_tensor_tensor(out=x9[:, c, 512 + h * P:512 + (h + 1) * P],
                                                 in0=num(h)[:, 0:DH], scalar=den[2][:, h // 2, h % 2, :],
                                                 in1=nin[:, s, 2, h * P:(h + 1) * P], op0=ALU.mult, op1=ALU.mult)
                m.then_inc(g["mlstm_done"], 1)

            def back_memory(v, c, s):
                for b in range(v.NS):
                    dve.wait_ge(g["um_ready"], c + (b + 1))
                    for h in range(H):
                        u = dve.scalar_tensor_tensor(
                            out=v.C[:, b, h, :], in0=v.C[:, b, h, :],
                            scalar=col[:, s, 3 * H + b * H + h:3 * H + b * H + h + 1],
                            in1=um_bank(b)[:, h // 2, (h % 2) * VX:(h % 2 + 1) * VX], op0=ALU.mult, op1=ALU.add)
                    u.then_inc(g["um_taken"], 1)

            def back_gla(v, c, s):
                dve.wait_ge(g["o_squared"], c + 1)
                dve.tensor_tensor(x9[:, c, 0:512].rearrange("p (j e f) -> p j e f", j=2, e=2),
                                  lvl_b[:, :, 0:2 * P].rearrange("p e (j f) -> p j e f", j=2),
                                  nin[:, s, 1, :].rearrange("p (j e f) -> p j e f", j=2, e=2),
                                  ALU.mult).then_inc(g["o_taken"], 1)
                for b in range(v.NS):
                    dve.wait_ge(g["ug_ready"], c + (b + 1))
                    for j in range(2):
                        last = E_B + j * P + (b + 1) * v.LS - 1
                        dve.scalar_tensor_tensor(out=v.S[:, b, j, :], in0=v.S[:, b, j, :],
                                                 scalar=ex[:, s, last:last + 1], in1=v.ug_out(b, j), op0=ALU.mult,
                                                 op1=ALU.add).then_inc(g["ug_taken"], 1)

            def masks(c, s):
                dve.wait_ge(g["zeroed"], ZEROED + 2)
                dve.wait_ge(g["qs_ready"], c + 1)
                for dst, x in ((qsm, qs[:, s, :, :]), (qbm, qb[:, s, :].rearrange("p (j f) -> p j f", j=2))):
                    for odd in range(2):
                        q = dve.tensor_copy(dst[:, :, odd:NB:2, odd * LB:(odd + 1) * LB],
                                            x.rearrange("p h (i q e) -> p h i q e", q=2, e=LB)[:, :, :, odd, :])
                    q.then_inc(g["qm_ready"], 1)

            def front(v, c, s):
                front_exponents(v, c, s, first=True)
                front_uppers(v, c, s)
                front_diagonal(v, c, s)
                front_columns(v, c, s)
                front_weights(v, c, s)
                front_queries_first(v, c, s)
                front_queries_rest(v, c, s)

            def step(vb, vf, c, s):
                front_exponents(vf, c + 1, 1 - s)
                front_diagonal(vf, c + 1, 1 - s)
                back_scores(vb, c, s, lambda: (front_uppers(vf, c + 1, 1 - s), front_columns(vf, c + 1, 1 - s)))
                back_mlstm(vb, c, s)
                front_weights(vf, c + 1, 1 - s)
                back_memory(vb, c, s)
                front_queries_first(vf, c + 1, 1 - s)
                back_gla(vb, c, s)
                front_queries_rest(vf, c + 1, 1 - s)
                if vf.sample:
                    masks(c + 1, 1 - s)

            def back(v, c, s):
                back_scores(v, c, s)
                back_mlstm(v, c, s)
                back_memory(v, c, s)
                back_gla(v, c, s)

            for x in (kx[:, 0, :, :], PR.C[:, :, :, :], gsc[:, :, :]):
                dve.memset(x, 0.0).then_inc(g["zeroed"], 1)
            dve.wait_ge(keep_in, 16)
            dve.wait_ge(g["zeroed"], ZEROED)
            pipeline(dve, front, step, back)


def output(nc, a, x9, ssq, cols, hT, ident, bank, raw):
    with ExitStack() as ctx:
        sb = lambda n, s, d=F32: ctx.enter_context(nc.sbuf_tensor(f"o_{n}", s, d))
        sem = Sems(nc, ctx, "o_")
        SLOTS = 4
        w_hi, w_lo = sb("w_hi", [P, KD, PIECE], F32R), sb("w_lo", [P, KD, PIECE], F32R)
        inv, rstd = sb("inv", [P, RT, 2 * H]), sb("rstd", [P, RT, 2 * H])
        x_loaded = [sem(f"x_loaded{r}") for r in range(RT)]
        raw_loaded = [sem(f"raw_loaded{s}") for s in range(SLOTS)]
        piece_hi, piece_split = sem("piece_hi"), sem("piece_split")
        inverted, rooted = sem("inverted"), sem("rooted")
        scaled, last_scaled = sem("scaled"), sem("last_scaled")
        next_loaded = sem("next_loaded")
        sums_ready, added, step = sem("sums_ready"), sem("added"), sem("step")
        turn = Turn(nc, sem, "mix", hT, ident, cols[:, K_MIX:K_MIX + KD], bank[6:8],
                    lambda rb, j, k: x9[:, rb * JR + j, k * P:(k + 1) * P], spread=0, eight=bank)
        TURNS = ((0, 1), (2,), (3, 4), (5,), (6,), (7,))
        xs, sq = sb("x_scaled", [P, JR, D]), sb("squares", [P, D])
        norm = Norm(nc, ctx, sem, "norm2", lambda r: x9[:, r, :], lambda r: xs[:, r % JR, :], sq[:, :], hT, ident,
                    cols[:, K_N2:K_N2 + KD], bank[6:8], spread=RB - 1, eight=bank)
        block = ctx.enter_context(nc.Block())

        @block.sync
        def _(sp):
            for n in range(KD):
                if n >= SLOTS:
                    sp.wait_ge(piece_split, n - SLOTS + 1)
                sp.dma_start(raw[:, n % SLOTS, :], a["w"][PC_OUT + n]).then_inc(raw_loaded[n % SLOTS], 16)
            for r in range(RT):
                if r % JR == 0:
                    sp.wait_ge(turn.turned, KD * (r // JR + 1))
                sp.dma_start(x9[:, r, :], a["x"][r]).then_inc(x_loaded[r], 16)
            sp.wait_ge(piece_split, KD)
            for m in range(3):
                sp.dma_start(raw[:, m, :], a["w"][PC_FFN + m]).then_inc(next_loaded, 16)
            sp.wait_ge(next_loaded, 3 * 16)

        def scale(eng, r):
            x = x9[:, r, :].rearrange("p (h v) -> p h v", v=DV)
            return eng.tensor_tensor(x, x, rstd[:, r, :].unsqueeze(2).to_broadcast([P, 2 * H, DV]), ALU.mult)

        @block.gpsimd
        def _(pool):
            pool.wait_ge(rooted, 1)
            scale(pool, JR - 1).then_inc(last_scaled, 1)
            for n in range(KD):
                pool.wait_ge(piece_hi, n + 1)
                pool.tensor_tensor(w_lo[:, n, :], raw[:, n % SLOTS, :], w_hi[:, n, :].bitcast(F32),
                                   ALU.subtract).then_inc(piece_split, 1)

        @block.scalar
        def _(act):
            def weights(n):
                act.wait_ge(raw_loaded[n % SLOTS], 16 * (n // SLOTS + 1))
                act.activation(w_hi[:, n, :], raw[:, n % SLOTS, :], ACT.Copy).then_inc(piece_hi, 1)

            ready = lambda eng, r: eng.wait_ge(added, 2 * r + 2)
            act.wait_ge(inverted, 1)
            act.activation(rstd[:, :, :], inv[:, :, :], ACT.Sqrt).then_inc(rooted, 1)
            turn.act_hi(act, 0, range(0, 2))
            weights(0)
            turn.act_hi(act, 0, range(2, KD))
            for k in range(1, 4):
                weights(k)
            for k in range(KD):
                if k < 4:
                    weights(4 + k)
                turn.act_hi(act, 1, (k,))
            for n in range(2 * JR):
                turn.act_hi(act, 2, TURNS[n])
                if n < JR:
                    norm.act_sums(act, 0, ready, (n,))
                elif n > JR:
                    norm.act_sums(act, 1, ready, (n - JR - 1,))
                if n == JR - 1:
                    norm.act_root(act, 0)
            norm.act_sums(act, 1, ready, (JR - 1,))
            norm.act_root(act, 1)
            for n in range(2 * JR):
                norm.act_hi(act, n // JR, (range(0, 3), range(3, 6), range(6, 8))[n % JR])
                if n % 2:
                    norm.act_sums(act, 2, ready, (n // 2,))
            norm.act_root(act, 2)
            norm.act_hi(act, 2)

        @block.tensor
        def _(pe):
            def product(u, k):
                r, n = divmod(u, 2)
                x = [h[:, k, r * P:(r + 1) * P] for h in hT]
                w = [y[:, k, n * 512:(n + 1) * 512] for y in (w_hi, w_lo)]
                return mm3(pe, bank[u % 6], x, w, k == 0, k == KD - 1)

            def rows(rb, beside):
                pe.wait_ge(turn.lo_done, KD * (rb + 1))
                for n, u in enumerate(range(2 * JR * rb, 2 * JR * (rb + 1))):
                    pe.wait_ge(added, u - 5)
                    for k in range(KD):
                        mm = product(u, k)
                    mm.then_inc(sums_ready, 1)
                    beside(n)

            pe.wait_ge(scaled, JR - 1)
            pe.wait_ge(last_scaled, 1)
            turn.pe_turn(pe, 0)
            pe.wait_ge(turn.lo_done, KD)
            for k in range(KD):
                pe.wait_ge(piece_split, k + 1)
                for u in range(2 * JR):
                    mm = product(u, k)
                    if k == KD - 1:
                        mm.then_inc(sums_ready, 1)
                if k == 0:
                    pe.wait_ge(scaled, 2 * JR - 1)
                turn.pe_turn(pe, 1, (k,))
            pe.wait_ge(scaled, RT - 1)
            rows(1, lambda n: turn.pe_turn(pe, 2, TURNS[n]))
            pe.wait_ge(turn.lo_done, KD * RB)
            rows(2, lambda n: norm.pe_turn(pe, n // JR, (range(0, 3), range(3, 6), range(6, 8))[n % JR]))
            norm.pe_turn(pe, 2)

        @block.vector
        def _(dve):
            chain = Count(dve, step)
            chain.link(dve.tensor_scalar(ssq[:, :, :], ssq[:, :, :], 1.0 / P, EPS, ALU.mult, ALU.add))
            dve.reciprocal(inv[:, :, :], ssq[:, :, :]).then_inc(inverted, 1)
            dve.wait_ge(rooted, 1)

            def add(rb, ns=range(2 * JR)):
                for u in (2 * JR * rb + n for n in ns):
                    r, n = divmod(u, 2)
                    if n == 0:
                        dve.wait_ge(x_loaded[r], 16)
                    dve.wait_ge(sums_ready, u + 1)
                    x = x9[:, r, n * 512:(n + 1) * 512]
                    dve.tensor_tensor(x, bank[u % 6], x, ALU.add).then_inc(added, 1)

            for r in range(JR - 1):
                scale(dve, r).then_inc(scaled, 1)
            turn.dve_lo(dve, 0)
            for r in range(JR, RT):
                scale(dve, r).then_inc(scaled, 1)
            turn.dve_lo(dve, 1)
            add(0)
            for n in range(2 * JR):
                turn.dve_lo(dve, 2, TURNS[n])
                add(1, (n,))
                if n == JR - 1:
                    norm.dve_invert(dve, 0, chain)
                    norm.dve_scale(dve, 0)
            norm.dve_invert(dve, 1, chain)
            for n in range(2 * JR):
                add(2, (n,))
                norm.dve_lo(dve, n // JR, (range(0, 3), range(3, 6), range(6, 8))[n % JR])
                if n == JR - 1:
                    norm.dve_scale(dve, 1)
            norm.dve_invert(dve, 2, chain)
            norm.dve_scale(dve, 2)
            norm.dve_lo(dve, 2)


def ffn(nc, a, o, x9, hT, bank, raw):
    NP = NF // 2
    SX = LB + 2
    with ExitStack() as ctx:
        sb = lambda n, s, d=F32: ctx.enter_context(nc.sbuf_tensor(f"f_{n}", s, d))
        sem = Sems(nc, ctx, "f_")
        w_hi, w_lo = sb("w_hi", [P, 6, PIECE], F32R), sb("w_lo", [P, 6, PIECE], F32R)
        a_hi, a_lo = sb("a_hi", [P, 2, ROWS], F32R), sb("a_lo", [P, 2, ROWS], F32R)
        gp = sb("gate_prompt", [P, 2 + PROMPT])
        gs = sb("gate_sample", [P, NB, SX])
        gc = sb("gate_conv", [P, 2, RBW])
        cache, taps = sb("cache", [P, NF, 2 * NB]), sb("taps", [P, NF, 4])
        tails = sb("tails", [P, NF, 2 + 2 * NB])
        raw_loaded = [sem(f"raw_loaded{s}") for s in range(3)]
        small_in, tails_out = sem("small_in"), sem("tails_out")
        piece_hi, piece_split = sem("piece_hi"), sem("piece_split")
        up_ready = sem("up_ready")
        g_out = sem("g_out")
        conv_step, conv_done = sem("conv_step"), sem("conv_done")
        gelu_done, u_taken = sem("gelu_done"), sem("u_taken")
        ahi_done, a_split = sem("ahi_done"), sem("a_split")
        down_ready, down_added = sem("down_ready"), sem("down_added")
        tails_done, zeroed = sem("tails_done"), sem("zeroed")
        ss, inv, rstd = sb("ss", [P, RT]), sb("inv", [P, RT]), sb("rstd", [P, RT])
        gain_in, y_stored = sem("gain_in"), sem("y_stored")
        summed, shifted, inverted, rooted, y_ready = (sem(n) for n in "summed shifted inverted rooted y_ready".split())
        RAW, UP, CONV, GC, DOWN = 3, 3, 3, 2, 2
        NG = 5
        def splits_after(n, last):
            return () if last and n > 1 else ((0,), (1,), (), (2,), (3,), (4, 5))[n]

        block = ctx.enter_context(nc.Block())

        def pairs(eng, body):
            with eng.Fori(0, NP - 1) as i:
                body(i, False)
            body(NP - 1, True)

        @block.sync
        def _(sp):
            def load(m, slot):
                sp.wait_ge(piece_split, m + 1)
                sp.dma_start(raw[:, slot, :], a["w"][m + PC_FFN]).then_inc(raw_loaded[slot], 16)

            sp.dma_start(cache[:, :, :], a["cache"]).then_inc(small_in, 16)
            sp.dma_start(taps[:, :, :], a["taps"]).then_inc(small_in, 16)
            load(3, 0)

            def body(i, last):
                for k in range(2 if last else 6):
                    load(6 * i + (4 + k), (4 + k) % 3)

            pairs(sp, body)
            sp.wait_ge(piece_split, 6 * NP + RAW)
            sp.dma_start(raw[:, 0, :], a["norm_f"].to_broadcast([P, D])).then_inc(gain_in, 16)
            sp.wait_ge(tails_done, 2 * NF)
            sp.dma_start(o["conv"], tails[:, :, :]).then_inc(tails_out, 16)
            for r in range(RT):
                sp.wait_ge(y_ready, r + 1)
                sp.dma_start(o["y"][r], x9[:, r, :]).then_inc(y_stored, 16)
            sp.wait_ge(tails_out, 16)
            sp.wait_ge(y_stored, 16 * RT)

        @block.gpsimd
        def _(pool):
            for s, n in ((piece_split, RAW), (u_taken, UP), (conv_done, CONV), (a_split, GC), (down_added, DOWN)):
                pool.sem_inc(s, n)
            for s in raw_loaded:
                pool.sem_inc(s, 16)
            pool.memset(gp[:, 0:2], 0.0).then_inc(zeroed, 1)

            def lo(m, unit, slot):
                pool.wait_ge(piece_hi, m + 1)
                pool.tensor_tensor(w_lo[:, unit, :], raw[:, slot, :], w_hi[:, unit, :].bitcast(F32),
                                   ALU.subtract).then_inc(piece_split, 1)

            for m in range(4):
                lo(m, m, m % 3)

            def body(i, last):
                for n in range(2 * RB):
                    q, rb = divmod(n, RB)
                    s = slice(rb * RBW, (rb + 1) * RBW)
                    pool.wait_ge(ahi_done, 6 * i + (n + 1))
                    pool.tensor_tensor(a_lo[:, q, s], gc[:, n % 2, :], a_hi[:, q, s].bitcast(F32),
                                       ALU.subtract).then_inc(a_split, 1)
                    for k in splits_after(n, last):
                        lo(6 * i + (4 + k), (4 + k) % 6, (4 + k) % 3)

            pairs(pool, body)

        @block.scalar
        def _(act):
            def hi(m, unit, slot, loads):
                act.wait_ge(raw_loaded[slot], loads)
                act.activation(w_hi[:, unit, :], raw[:, slot, :], ACT.Copy).then_inc(piece_hi, 1)

            for m in range(4):
                hi(m, m, m % 3, 16 * (m // 3 + 1))
            act.wait_ge(small_in, 32)

            def body(i, last):
                for n in range(2 * RB):
                    q, rb = divmod(n, RB)
                    f = 2 * i + q
                    act.wait_ge(up_ready, 12 * i + (2 * n + 1))
                    act.wait_ge(conv_done, 6 * i + (3 * q + (2 if rb == 0 else 3)))
                    g = bank[2 * rb]
                    if rb < 2:
                        act.activation(gp[:, 2 + rb * RBW:2 + (rb + 1) * RBW], g[:, 0:RBW], ACT.Copy).then_inc(g_out, 1)
                    else:
                        np_ = PROMPT - 2 * RBW
                        act.activation(gp[:, 2 + 2 * RBW:2 + PROMPT], g[:, 0:np_], ACT.Copy).then_inc(g_out, 1)
                        act.activation(gs[:, :, 2:SX], streams(g[:, np_:RBW]), ACT.Copy).then_inc(g_out, 1)
                        act.activation(gs[:, :, 0:2], cache[:, f, :].rearrange("p (b e) -> p b e", e=2),
                                       ACT.Copy).then_inc(g_out, 1)
                        act.wait_ge(g_out, 2 * NG * i + NG * (q + 1))
                        act.activation(tails[:, f, 0:2], gp[:, PROMPT:PROMPT + 2], ACT.Copy).then_inc(tails_done, 1)
                        act.activation(tails[:, f, 2:2 + 2 * NB].rearrange("p (b e) -> p b e", e=2),
                                       gs[:, :, LB:SX], ACT.Copy).then_inc(tails_done, 1)
                    act.wait_ge(conv_done, 6 * i + (n + 1 + CONV))
                    act.activation(gc[:, n % 2, :], gc[:, n % 2, :], ACT.Gelu_apprx_tanh).then_inc(gelu_done, 1)
                    act.wait_ge(u_taken, 6 * i + (n + 1 + UP))
                    act.activation(a_hi[:, q, rb * RBW:(rb + 1) * RBW], gc[:, n % 2, :], ACT.Copy).then_inc(ahi_done, 1)
                    for k in splits_after(n, last):
                        if k < 2:
                            act.wait_ge(up_ready, 12 * i + 1)
                        else:
                            act.wait_ge(up_ready, 12 * i + (5, 6, 11, 12)[k - 2])
                        hi(6 * i + (4 + k), (4 + k) % 6, (4 + k) % 3, 32 * i + 16 * ((4 + k) // 3 + 1))

            pairs(act, body)
            act.wait_ge(piece_split, 6 * NP + RAW)

            def root(r):
                act.wait_ge(inverted, r + 1)
                act.activation(rstd[:, r:r + 1], inv[:, r:r + 1], ACT.Sqrt).then_inc(rooted, 1)

            for r in range(RT):
                if r == RT - 1:
                    root(r - 1)
                act.wait_ge(down_added, 2 * RT * (NP - 1) + 2 * (r + 1) + DOWN)
                if r:
                    act.wait_ge(summed, r)
                act.activation(raw[:, 1, :], x9[:, r, :], ACT.Square, accum_out=ss[:, r:r + 1]).then_inc(summed, 1)
                if 0 < r < RT - 1:
                    root(r - 1)
            root(RT - 1)

        @block.tensor
        def _(pe):
            with pe.Fori(0, NP) as i:
                for q in range(2):
                    for rb in range(RB):
                        n = 3 * q + rb
                        pe.wait_ge(u_taken, 6 * i + (n + 1))
                        for m in range(2):
                            if rb == 0:
                                pe.wait_ge(piece_split, 6 * i + (2 * q + m + 1 + RAW))
                            for k in range(KD):
                                w = [y[:, 2 * q + m, k * P:(k + 1) * P] for y in (w_hi, w_lo)]
                                x = [h[:, k, rb * RBW:(rb + 1) * RBW] for h in hT]
                                mm = mm3(pe, bank[2 * rb + m][:, 0:RBW], w, x, k == 0, k == KD - 1)
                            mm.then_inc(up_ready, 1)
                pe.wait_ge(piece_split, 6 * i + (6 + RAW))
                for r in range(RT):
                    if r % JR == 0:
                        pe.wait_ge(a_split, 6 * i + (RB + r // JR + 1 + GC))
                    for half in range(2):
                        pe.wait_ge(down_added, 2 * RT * i + (2 * r + half + 1))
                        for q in range(2):
                            x = [y[:, q, r * P:(r + 1) * P] for y in (a_hi, a_lo)]
                            w = [y[:, 4 + q, half * 512:(half + 1) * 512] for y in (w_hi, w_lo)]
                            mm = mm3(pe, bank[6 + half], x, w, q == 0, q == 1)
                        mm.then_inc(down_ready, 1)

        @block.vector
        def _(dve):
            dve.wait_ge(small_in, 32)
            dve.wait_ge(zeroed, 1)

            def body(i, last):
                chain = Count(dve, conv_step, 12 * i)
                for n in range(2 * RB):
                    q, rb = divmod(n, RB)
                    tap = [taps[:, 2 * i + q, j:j + 1] for j in range(4)]
                    np_ = min(RBW, PROMPT - rb * RBW)
                    out = gc[:, n % 2, :]
                    parts = [(lambda j: gp[:, rb * RBW + j:rb * RBW + j + np_], out[:, 0:np_])]
                    if np_ < RBW:
                        parts.append((lambda j: gs[:, :, j:j + LB], streams(out[:, np_:RBW])))
                    dve.wait_ge(g_out, 2 * NG * i + (NG * q + (rb + 1 if rb < 2 else NG)))
                    dve.wait_ge(a_split, 6 * i + (n + 1))
                    for src, dst in parts:
                        ins = dve.tensor_scalar(dst, src(2), tap[2], tap[3], ALU.mult, ALU.add)
                    chain.link(ins)
                    for src, dst in parts:
                        ins = dve.scalar_tensor_tensor(out=dst, in0=src(1), scalar=tap[1], in1=dst, op0=ALU.mult,
                                                       op1=ALU.add)
                    chain.link(ins)
                    for src, dst in parts:
                        ins = dve.scalar_tensor_tensor(out=dst, in0=src(0), scalar=tap[0], in1=dst, op0=ALU.mult,
                                                       op1=ALU.add)
                    ins.then_inc(conv_done, 1)
                    dve.wait_ge(gelu_done, 6 * i + (n + 1))
                    dve.wait_ge(up_ready, 12 * i + (2 * n + 2))
                    dve.tensor_tensor(out, bank[2 * rb + 1][:, 0:RBW], out, ALU.mult).then_inc(u_taken, 1)
                assert chain.n == 12
                for u in range(2 * RT):
                    r, half = divmod(u, 2)
                    x = x9[:, r, half * 512:(half + 1) * 512]
                    dve.wait_ge(down_ready, 2 * RT * i + (u + 1))
                    dve.tensor_tensor(x, bank[6 + half], x, ALU.add).then_inc(down_added, 1)
                    if last and r >= 1 and half == (0 if r == RT - 1 else 1):
                        invert(r - 1)
                        if r >= 2:
                            finish(r - 2)

            def invert(r):
                s = slice(r, r + 1)
                dve.wait_ge(summed, r + 1)
                dve.tensor_scalar(ss[:, s], ss[:, s], 1.0 / D, EPS, ALU.mult, ALU.add).then_inc(shifted, 1)
                dve.wait_ge(shifted, r + 1)
                dve.reciprocal(inv[:, s], ss[:, s]).then_inc(inverted, 1)

            def finish(r):
                if r == 0:
                    dve.wait_ge(gain_in, 16)
                dve.wait_ge(rooted, r + 1)
                dve.scalar_tensor_tensor(out=x9[:, r, :], in0=x9[:, r, :], scalar=rstd[:, r:r + 1],
                                         in1=raw[:, 0, :], op0=ALU.mult, op1=ALU.mult).then_inc(y_ready, 1)

            with dve.Fori(0, NP - 1) as i:
                body(i, False)
            body(NP - 1, True)
            finish(RT - 2)
            invert(RT - 1)
            finish(RT - 1)


def kernel(**inputs):
    import numpy as np
    import concourse.bacc as _bacc
    from concourse.bass_utils import run_bass_kernel_spmd as _run

    g = {n: np.asarray(v) for n, v in inputs.items()}
    f32 = np.float32
    w_in, w_out = g["w_in"][0], g["w_out"][0]
    QK, V, W = H * DK, H * DV, H * DH
    ofs = np.cumsum([0, QK, QK, V, V, RANK, W, W, W, W, H, H])
    gq, gk, gv, gr, gl, mq, mk, mv, mo, mi, mf = [w_in[:, ofs[i]:ofs[i + 1]] for i in range(11)]

    def piece(w):
        n = w.shape[1]
        per = PIECE // n
        return w.reshape(KD // per, per, P, n).transpose(0, 2, 1, 3).reshape(KD // per, P, PIECE)

    gate = np.zeros((D, P), f32)
    gate[:, 0:H], gate[:, 32:32 + H], gate[:, 64:64 + RANK] = mf, mi, gl
    trans = np.concatenate([gq, gk, mq, mk], axis=1)
    pieces = [piece(gate)]
    pieces += [piece(trans[:, t * P:(t + 1) * P]) for t in range(NT)]
    pieces += [piece(w) for w in (gv, mv, gr, mo)]
    pieces += [w_out.reshape(KD, P, D)]
    wg, wu, wd = g["w_g"][0], g["w_u"][0], g["w_d"][0].reshape(NF, P, D)
    up = [(piece(wg[:, f * P:(f + 1) * P]), piece(wu[:, f * P:(f + 1) * P])) for f in range(NF)]
    pieces += [*up[0], *up[1]]
    for i in range(0, NF, 2):
        pieces += [wd[i:i + 2]]
        if i + 2 < NF:
            pieces += [*up[i + 2], *up[i + 3]]
    ins = {"w": np.concatenate(pieces)}
    assert ins["w"].shape == (N_PIECES, P, PIECE)
    ins["x"] = np.concatenate([g["x_prompt"][0], g["x_sample"].reshape(-1, D)]).reshape(RT, P, D)
    cols = np.zeros((P, N_COL), f32)
    cols[:, K_N1:K_N1 + KD] = g["norm1"][0].reshape(KD, P).T
    cols[:, K_N2:K_N2 + KD] = g["norm2"][0].reshape(KD, P).T
    cols[:, K_MIX:K_MIX + H] = g["gla_norm"][0][:, None]
    cols[:, K_MIX + H:K_MIX + KD] = g["m_norm"][0][:, None]
    cols[:, K_BA:K_BA + 2] = g["b_gla_a"][0].reshape(2, P).T
    cols[0:H, K_BG], cols[32:32 + H, K_BG] = g["b_m_f"][0], g["b_m_i"][0]
    cols[0:H, K_M0:K_M0 + NB] = g["state_mlstm_m"][0].T
    ins["cols"] = cols
    ins["w_decay"] = g["w_gla_a"][0]
    keep = np.ones((H, ROWS), f32)
    keep[:, 0:PROMPT:P] = 0
    keep[:, PROMPT::LB] = 0
    ins["keep"] = keep
    ins["ident"] = np.eye(P, dtype=f32)
    s, t = np.arange(P)[:, None], np.arange(P)[None, :]
    const = np.zeros((P, N_CONST), f32)
    for lv in range(LEVELS):
        w = P >> (lv + 1)
        second = np.arange(P).reshape(-1, 2, w)[:, 1].reshape(1, -1)
        const[:, C_LV + lv * P // 2:C_LV + (lv + 1) * P // 2] = (s // (2 * w) == second // (2 * w)) & (s % (2 * w) < w)
    const[:, C_DIAG:C_DIAG + P] = s == t
    const[:, C_CAUS:C_CAUS + P] = np.where(s <= t, 0.0, NEG)
    const[:, C_CAUSB:C_CAUSB + P] = np.where((s <= t) & (s // LB == t // LB), 0.0, NEG)
    const[:, C_KEEP:C_KEEP + 2 * P] = np.arange(2 * P) % P != 0
    const[:, C_KEEPB:C_KEEPB + 2 * P] = np.arange(2 * P) % LB != 0
    const[:, C_PARITY:C_PARITY + 2] = s // LB % 2 == np.arange(2)[None, :]
    const[:, C_ONE:C_ONE + P] = 1.0
    ins["const"] = const
    ins["cache"] = g["cache_ffn_conv"][0].reshape(NB * 2, NF, P).transpose(2, 1, 0)
    taps = np.concatenate([g["conv_w"][0], g["conv_b"]])
    ins["taps"] = taps.reshape(4, NF, P).transpose(2, 1, 0)
    ins["norm_f"] = g["norm_f"].reshape(1, D)
    ins["s_gla"] = g["state_gla"][0].reshape(NB, 2, 2, DK, DV).transpose(2, 3, 0, 1, 4).reshape(P, NB, 2, DV)
    ins["s_mc"] = np.concatenate([g["state_mlstm_C"][0].transpose(2, 0, 1, 3),
                                  g["state_mlstm_n"][0].transpose(2, 0, 1)[..., None]], axis=3)
    outs = {"y": (RT, P, D), "p_gla": (P, 2, DV), "p_mc": (P, H, VX), "mm": (H, EXT), "conv": (P, NF, 2 + 2 * NB),
            "q_gla": (P, NB, 2, DV), "q_mc": (P, NB, H, VX)}
    scratch = {"pT": (NT + 2, P, ROWS), "pN": (NN, RT, P, 512), "rows": (H, 5, ROWS)}
    nc = _bacc.Bacc("TRN2", target_bir_lowering=False, num_devices=1)
    ins = {n: np.ascontiguousarray(v) for n, v in ins.items()}
    a = {n: nc.dram_tensor(f"in_{n}", v.shape, F32, kind="ExternalInput").ap() for n, v in ins.items()}
    a.update({n: nc.dram_tensor(f"scratch_{n}", s, F32, kind="Internal").ap() for n, s in scratch.items()})
    o = {n: nc.dram_tensor(f"out_{n}", s, F32, kind="ExternalOutput").ap() for n, s in outs.items()}
    build(nc, a, o)
    r = _run(nc, [{f"in_{n}": v for n, v in ins.items()}], core_ids=[0]).results[0]
    y = r["out_y"].reshape(ROWS, D)
    mm = r["out_mm"]
    conv = r["out_conv"].transpose(2, 1, 0).reshape(2 + 2 * NB, F)

    def gla(s):
        return s.reshape(2, DK, -1, 2, DV).transpose(2, 3, 0, 1, 4).reshape(1, -1, H, DK, DV)

    def mc(s):
        s = s.reshape(P, -1, H, VX)
        return s[..., 0:DH].transpose(1, 2, 0, 3)[None], s[..., DH].transpose(1, 2, 0)[None]

    p_c, p_n = mc(r["out_p_mc"])
    q_c, q_n = mc(r["out_q_mc"])
    q_m = mm[:, 1 + PROMPT:].reshape(H, NB, LB + 1)[:, :, LB].T
    res = (y[0:PROMPT][None], y[PROMPT:].reshape(NB, LB, D),
           gla(r["out_p_gla"]), p_c, p_n, mm[:, PROMPT].reshape(1, 1, H), conv[0:2].reshape(1, 1, 2, F),
           gla(r["out_q_gla"]), q_c, q_n, q_m.reshape(1, NB, H), conv[2:].reshape(1, NB, 2, F))
    return tuple(np.ascontiguousarray(v) for v in res)
```
